# Optimizing a Trainium2 kernel written in Bass

```python
import math
import jax, jax.numpy as jnp
from jax import lax
import numpy as np

D_MODEL = 1024
BATCH = 1
SEQ = 256
DEPTH = 2

CHUNK = 64
N_MIXERS = 2
N_SSD_LAYERS = (DEPTH + 1) // 2
N_ATTN_LAYERS = DEPTH // 2
EPS = 1e-6

SSD_EXPAND = 2
SSD_D_INNER = SSD_EXPAND * D_MODEL
SSD_HEAD_DIM = 64
SSD_HEADS = SSD_D_INNER // SSD_HEAD_DIM
SSD_GROUPS = 4
SSD_HEADS_PER_GROUP = SSD_HEADS // SSD_GROUPS
SSD_STATE = 128
SSD_CONV = 4
SSD_CONV_CH = SSD_D_INNER + 2 * SSD_GROUPS * SSD_STATE
SSD_IN = SSD_D_INNER + SSD_CONV_CH + SSD_HEADS

ATTN_HEADS = 8
ATTN_HEAD_DIM = D_MODEL // ATTN_HEADS // 2
ATTN_V_DIM = 2 * ATTN_HEAD_DIM
ATTN_IN = 3 * D_MODEL
ROPE_THETA = 500000.0
ROPE_DIM = ATTN_HEAD_DIM // 4
Q_BLOCK = 128

D_FF = 2816
FFN_CONV = 3


def rmsnorm(x, g):
    xf = x.astype(jnp.float32)
    y = xf * lax.rsqrt(jnp.mean(xf * xf, axis=-1, keepdims=True) + EPS)
    return (y * g).astype(x.dtype)

def causal_dwconv(x, w, b):
    k_width = w.shape[0]
    s = x.shape[1]
    xp = jnp.pad(x, ((0, 0), (k_width - 1, 0), (0, 0)))
    y = b
    for k in range(k_width):
        y = y + w[k] * xp[:, k:k + s]
    return y

def rope_tables(positions):
    inv_freq = ROPE_THETA ** (-jnp.arange(0, ROPE_DIM, 2, dtype=jnp.float32) / ROPE_DIM)
    ang = positions.astype(jnp.float32)[..., None] * inv_freq
    return jnp.cos(ang), jnp.sin(ang)

def apply_partial_rope(t, cos, sin):
    half = ROPE_DIM // 2
    c = cos[:, :, None, None, :]
    s = sin[:, :, None, None, :]
    tf = t.astype(jnp.float32)
    x1, x2, rest = tf[..., :half], tf[..., half:ROPE_DIM], tf[..., ROPE_DIM:]
    out = jnp.concatenate([x1 * c - x2 * s, x2 * c + x1 * s, rest], axis=-1)
    return out.astype(t.dtype)

def ssd_mixer(xn, in_w, conv_w, conv_b, dt_bias, a_log, d_skip, norm_g, out_w):
    b, s, _ = xn.shape
    nc = s // CHUNK
    G, R, P, N = SSD_GROUPS, SSD_HEADS_PER_GROUP, SSD_HEAD_DIM, SSD_STATE
    proj = xn @ in_w
    z = proj[..., :SSD_D_INNER]
    xbc = proj[..., SSD_D_INNER:SSD_D_INNER + SSD_CONV_CH]
    dt = proj[..., SSD_D_INNER + SSD_CONV_CH:]
    xbc = jax.nn.silu(causal_dwconv(xbc, conv_w, conv_b))
    xs = xbc[..., :SSD_D_INNER].reshape(b, nc, CHUNK, G, R, P)
    Bm = xbc[..., SSD_D_INNER:SSD_D_INNER + G * N].reshape(b, nc, CHUNK, G, N)
    Cm = xbc[..., SSD_D_INNER + G * N:].reshape(b, nc, CHUNK, G, N)
    dt = jax.nn.softplus(dt + dt_bias).reshape(b, nc, CHUNK, G, R)
    a = -jnp.exp(a_log).reshape(G, R)
    dA = (dt * a).transpose(0, 3, 4, 1, 2)
    x_dt = xs * dt[..., None]
    a_cs = jnp.cumsum(dA, axis=-1)
    seg = a_cs[..., :, None] - a_cs[..., None, :]
    tril = jnp.tril(jnp.ones((CHUNK, CHUNK), dtype=bool))
    lmat = jnp.where(tril, jnp.exp(jnp.where(tril, seg, -jnp.inf)), 0.0)
    cb = jnp.einsum("bclgn,bcsgn->bgcls", Cm, Bm)
    y_diag = jnp.einsum("bgrcls,bcsgrp->bclgrp", cb[:, :, None] * lmat, x_dt)
    decay = jnp.exp(a_cs[..., -1:] - a_cs)
    states = jnp.einsum("bclgn,bgrcl,bclgrp->cbgrpn", Bm, decay, x_dt)
    chunk_decay = jnp.exp(a_cs[..., -1]).transpose(3, 0, 1, 2)

    def step(h, inp):
        st, dec = inp
        return dec[..., None, None] * h + st, h

    _, h_in = lax.scan(step, jnp.zeros_like(states[0]), (states, chunk_decay))
    y_off = jnp.einsum("bclgn,cbgrpn,bgrcl->bclgrp", Cm, h_in, jnp.exp(a_cs))
    y = y_diag + y_off + xs * d_skip.reshape(G, R)[:, :, None]
    y = y.reshape(b, s, SSD_D_INNER)
    yg = (y * jax.nn.silu(z)).reshape(b, s, G, SSD_D_INNER // G)
    yg = rmsnorm(yg, 1.0).reshape(b, s, SSD_D_INNER) * norm_g
    return yg.astype(xn.dtype) @ out_w

def diff_attention(xn, cos, sin, in_w, q_norm_g, k_norm_g, lq1, lk1, lq2, lk2,
                   subln_g, out_w, lambda_init):
    b, s, _ = xn.shape
    H, HD = ATTN_HEADS, ATTN_HEAD_DIM
    proj = xn @ in_w
    q = proj[..., :D_MODEL].reshape(b, s, H, 2, HD)
    k = proj[..., D_MODEL:2 * D_MODEL].reshape(b, s, H, 2, HD)
    v = proj[..., 2 * D_MODEL:].reshape(b, s, H, ATTN_V_DIM)
    q = apply_partial_rope(rmsnorm(q, q_norm_g), cos, sin)
    k = apply_partial_rope(rmsnorm(k, k_norm_g), cos, sin)
    lam = (jnp.exp(jnp.sum(lq1.astype(jnp.float32) * lk1.astype(jnp.float32)))
           - jnp.exp(jnp.sum(lq2.astype(jnp.float32) * lk2.astype(jnp.float32)))
           + lambda_init)
    scale = 1.0 / math.sqrt(HD)
    outs = []
    for blk in range(s // Q_BLOCK):
        q0, q1 = blk * Q_BLOCK, (blk + 1) * Q_BLOCK
        qb = q[:, q0:q1]
        kc = k[:, :q1]
        vc = v[:, :q1]
        sc = jnp.einsum("bqhcd,bkhcd->bhcqk", qb, kc).astype(jnp.float32) * scale
        q_chunk = (q0 + jnp.arange(Q_BLOCK)) // CHUNK
        k_chunk = jnp.arange(q1) // CHUNK
        allowed = k_chunk[None, :] <= q_chunk[:, None]
        sc = jnp.where(allowed, sc, -jnp.inf)
        p = jax.nn.softmax(sc, axis=-1)
        attn = p[:, :, 0] - lam * p[:, :, 1]
        outs.append(jnp.einsum("bhqk,bkhe->bqhe", attn.astype(v.dtype), vc))
    o = jnp.concatenate(outs, axis=1)
    o = rmsnorm(o, subln_g) * (1.0 - lambda_init)
    return o.reshape(b, s, H * ATTN_V_DIM).astype(xn.dtype) @ out_w

def conv_ffn(xn, up_w, conv_w, conv_b, down_w):
    h = causal_dwconv(xn @ up_w, conv_w, conv_b)
    g, u = h[..., :D_FF], h[..., D_FF:]
    return (jax.nn.silu(g) * u) @ down_w

def first_inputs(seed: int = 0) -> dict:
    key = jax.random.key(seed)
    ks = jax.random.split(key, 32)
    f32 = jnp.float32

    def nrm(k, shape, std):
        return jax.random.normal(k, shape, f32) * std

    def gain(k, shape):
        return 1.0 + 0.05 * jax.random.normal(k, shape, f32)

    out_scale = 1.0 / math.sqrt(2 * DEPTH)
    x = jax.random.normal(ks[0], (BATCH, SEQ, D_MODEL), f32)
    start = jax.random.randint(ks[1], (BATCH,), 0, 64) * CHUNK
    positions = (start[:, None] + jnp.arange(SEQ)[None, :]).astype(jnp.int32)
    dt0 = jnp.exp(jax.random.uniform(ks[6], (N_SSD_LAYERS, SSD_HEADS), f32,
                                     math.log(0.001), math.log(0.1)))
    return {
        "x": x,
        "positions": positions,
        "norm_mix_g": gain(ks[2], (DEPTH, D_MODEL)),
        "norm_ffn_g": gain(ks[3], (DEPTH, D_MODEL)),
        "ssd_in_w": nrm(ks[4], (N_SSD_LAYERS, D_MODEL, SSD_IN), D_MODEL ** -0.5),
        "ssd_conv_w": nrm(ks[5], (N_SSD_LAYERS, SSD_CONV, SSD_CONV_CH), SSD_CONV ** -0.5),
        "ssd_conv_b": nrm(ks[7], (N_SSD_LAYERS, SSD_CONV_CH), 0.02),
        "ssd_dt_bias": dt0 + jnp.log(-jnp.expm1(-dt0)),
        "ssd_a_log": jnp.log(jax.random.uniform(ks[8], (N_SSD_LAYERS, SSD_HEADS), f32, 1.0, 16.0)),
        "ssd_d": gain(ks[9], (N_SSD_LAYERS, SSD_HEADS)),
        "ssd_norm_g": gain(ks[10], (N_SSD_LAYERS, SSD_D_INNER)),
        "ssd_out_w": nrm(ks[11], (N_SSD_LAYERS, SSD_D_INNER, D_MODEL), SSD_D_INNER ** -0.5 * out_scale),
        "attn_in_w": nrm(ks[12], (N_ATTN_LAYERS, D_MODEL, ATTN_IN), D_MODEL ** -0.5),
        "attn_q_norm_g": gain(ks[13], (N_ATTN_LAYERS, ATTN_HEAD_DIM)),
        "attn_k_norm_g": gain(ks[14], (N_ATTN_LAYERS, ATTN_HEAD_DIM)),
        "attn_lq1": nrm(ks[15], (N_ATTN_LAYERS, ATTN_HEAD_DIM), 0.1),
        "attn_lk1": nrm(ks[16], (N_ATTN_LAYERS, ATTN_HEAD_DIM), 0.1),
        "attn_lq2": nrm(ks[17], (N_ATTN_LAYERS, ATTN_HEAD_DIM), 0.1),
        "attn_lk2": nrm(ks[18], (N_ATTN_LAYERS, ATTN_HEAD_DIM), 0.1),
        "attn_subln_g": gain(ks[19], (N_ATTN_LAYERS, ATTN_V_DIM)),
        "attn_out_w": nrm(ks[20], (N_ATTN_LAYERS, D_MODEL, D_MODEL), D_MODEL ** -0.5 * out_scale),
        "ffn_up_w": nrm(ks[21], (DEPTH, D_MODEL, 2 * D_FF), D_MODEL ** -0.5),
        "ffn_conv_w": nrm(ks[22], (DEPTH, FFN_CONV, 2 * D_FF), FFN_CONV ** -0.5),
        "ffn_conv_b": nrm(ks[23], (DEPTH, 2 * D_FF), 0.02),
        "ffn_down_w": nrm(ks[24], (DEPTH, D_FF, D_MODEL), D_FF ** -0.5 * out_scale),
    }

def first_block(x, positions, norm_mix_g, norm_ffn_g,
              ssd_in_w, ssd_conv_w, ssd_conv_b, ssd_dt_bias, ssd_a_log, ssd_d,
              ssd_norm_g, ssd_out_w,
              attn_in_w, attn_q_norm_g, attn_k_norm_g, attn_lq1, attn_lk1,
              attn_lq2, attn_lk2, attn_subln_g, attn_out_w,
              ffn_up_w, ffn_conv_w, ffn_conv_b, ffn_down_w):
    cos, sin = rope_tables(positions)
    for i in range(DEPTH):
        j = i // N_MIXERS
        h = rmsnorm(x, norm_mix_g[i])
        if i % N_MIXERS == 0:
            x = x + ssd_mixer(h, ssd_in_w[j], ssd_conv_w[j], ssd_conv_b[j],
                              ssd_dt_bias[j], ssd_a_log[j], ssd_d[j],
                              ssd_norm_g[j], ssd_out_w[j])
        else:
            lambda_init = 0.8 - 0.6 * math.exp(-0.3 * i)
            x = x + diff_attention(h, cos, sin, attn_in_w[j], attn_q_norm_g[j],
                                   attn_k_norm_g[j], attn_lq1[j], attn_lk1[j],
                                   attn_lq2[j], attn_lk2[j], attn_subln_g[j],
                                   attn_out_w[j], lambda_init)
        h = rmsnorm(x, norm_ffn_g[i])
        x = x + conv_ffn(h, ffn_up_w[i], ffn_conv_w[i], ffn_conv_b[i], ffn_down_w[i])
    return x


N_A = DEPTH // 2
N_B = DEPTH - N_A
MEM_LEN = 256
MEM_HEADS = 4
MEM_HEAD_DIM = D_MODEL // 8
MEM_WIDTH = MEM_HEADS * MEM_HEAD_DIM
CONV_DIM = D_MODEL
CONV_WIDTH = 3
FOX_HEADS = 8
FOX_HEAD_DIM = D_MODEL // FOX_HEADS
FOX_WIDTH = FOX_HEADS * FOX_HEAD_DIM
D_FF_2 = ((8 * D_MODEL // 3 + 255) // 256) * 256
RMS_EPS = 1e-6
NEG_INF = float(np.finfo(np.float32).min)


def rmsnorm_2(x, g):
    xf = x.astype(jnp.float32)
    y = xf * lax.rsqrt(jnp.mean(xf * xf, axis=-1, keepdims=True) + RMS_EPS)
    return (y * g.astype(jnp.float32)).astype(x.dtype)

def swiglu(h, w_gate_up, w_down):
    gu = h @ w_gate_up
    gate, up = gu[..., :D_FF_2], gu[..., D_FF_2:]
    return (jax.nn.silu(gate) * up) @ w_down

def causal_depthwise_conv(u, w):
    c = u.shape[-1]
    return lax.conv_general_dilated(
        u, w[:, None, :].astype(u.dtype), window_strides=(1,),
        padding=[(CONV_WIDTH - 1, 0)],
        dimension_numbers=('NWC', 'WIO', 'NWC'),
        feature_group_count=c)

def memory_attention(q, mk, mv):
    b, s, h, dh = q.shape
    logits = jnp.einsum('bshd,bmhd->bhsm', q, mk,
                        preferred_element_type=jnp.float32) * (dh ** -0.5)
    p = jax.nn.softmax(logits, axis=-1).astype(mv.dtype)
    return jnp.einsum('bhsm,bmhd->bshd', p, mv).reshape(b, s, h * dh)

def forgetting_attention(q, k, v, logf_cum):
    b, s, h, dh = q.shape
    nb = s // Q_BLOCK
    qb = q.reshape(b, nb, Q_BLOCK, h, dh).transpose(1, 0, 2, 3, 4)
    cb = logf_cum.reshape(b, h, nb, Q_BLOCK).transpose(2, 0, 1, 3)
    k_pos = jnp.arange(s)
    scale = dh ** -0.5

    def block(args):
        q_blk, c_blk, i = args
        q_pos = i * Q_BLOCK + jnp.arange(Q_BLOCK)
        logits = jnp.einsum('bqhd,bkhd->bhqk', q_blk, k,
                            preferred_element_type=jnp.float32) * scale
        logits = logits + c_blk[..., :, None] - logf_cum[:, :, None, :]
        causal = k_pos[None, :] <= q_pos[:, None]
        logits = jnp.where(causal, logits, NEG_INF)
        p = jax.nn.softmax(logits, axis=-1).astype(v.dtype)
        return jnp.einsum('bhqk,bkhd->bqhd', p, v)

    out = lax.map(block, (qb, cb, jnp.arange(nb)))
    return out.transpose(1, 0, 2, 3, 4).reshape(b, s, h * dh)

def second_inputs(seed: int = 0) -> dict:
    key = jax.random.key(seed)
    ks = jax.random.split(key, 20)
    f32 = jnp.float32

    def w(k, shape, fan_in):
        return jax.random.normal(k, shape, f32) * (fan_in ** -0.5)

    def gain(k, shape):
        return 1.0 + 0.02 * jax.random.normal(k, shape, f32)

    a_in_cols = 3 * CONV_DIM + MEM_WIDTH
    b_in_cols = FOX_WIDTH + MEM_WIDTH
    return {
        'x': jax.random.normal(ks[0], (BATCH, SEQ, D_MODEL), f32),
        'mem': jax.random.normal(ks[1], (BATCH, MEM_LEN, D_MODEL), f32),
        'ffn_norm': gain(ks[2], (DEPTH, 2, D_MODEL)),
        'ffn_w_gate_up': w(ks[3], (DEPTH, 2, D_MODEL, 2 * D_FF_2), D_MODEL),
        'ffn_w_down': w(ks[4], (DEPTH, 2, D_FF_2, D_MODEL), D_FF_2),
        'mix_norm': gain(ks[5], (DEPTH, D_MODEL)),
        'mem_norm': gain(ks[6], (D_MODEL,)),
        'mem_w_kv': w(ks[7], (DEPTH, D_MODEL, 2 * MEM_WIDTH), D_MODEL),
        'a_w_in': w(ks[8], (N_A, D_MODEL, a_in_cols), D_MODEL),
        'a_conv_w': w(ks[9], (N_A, CONV_WIDTH, CONV_DIM), CONV_WIDTH),
        'a_w_out': w(ks[10], (N_A, CONV_DIM + MEM_WIDTH, D_MODEL), CONV_DIM + MEM_WIDTH),
        'kv_norm': gain(ks[11], (D_MODEL,)),
        'w_kvf': w(ks[12], (D_MODEL, 2 * FOX_WIDTH + FOX_HEADS), D_MODEL),
        'b_f': jax.random.uniform(ks[13], (FOX_HEADS,), f32, minval=1.0, maxval=6.0),
        'b_w_q': w(ks[14], (N_B, D_MODEL, b_in_cols), D_MODEL),
        'b_w_out': w(ks[15], (N_B, FOX_WIDTH + MEM_WIDTH, D_MODEL), FOX_WIDTH + MEM_WIDTH),
        'final_norm': gain(ks[16], (D_MODEL,)),
    }

def second_block(x, mem, ffn_norm, ffn_w_gate_up, ffn_w_down, mix_norm, mem_norm,
              mem_w_kv, a_w_in, a_conv_w, a_w_out, kv_norm, w_kvf, b_f,
              b_w_q, b_w_out, final_norm):
    b, s, _ = x.shape
    m = mem.shape[1]
    mem_n = rmsnorm_2(mem, mem_norm)
    k_sh = v_sh = c_sh = None

    for l in range(DEPTH):
        if l == N_A:
            hkv = rmsnorm_2(x, kv_norm)
            kvf = hkv @ w_kvf
            k_sh = kvf[..., :FOX_WIDTH].reshape(b, s, FOX_HEADS, FOX_HEAD_DIM)
            v_sh = kvf[..., FOX_WIDTH:2 * FOX_WIDTH].reshape(b, s, FOX_HEADS, FOX_HEAD_DIM)
            f_logit = (kvf[..., 2 * FOX_WIDTH:] + b_f).astype(jnp.float32)
            c_sh = jnp.cumsum(jax.nn.log_sigmoid(f_logit), axis=1).transpose(0, 2, 1)

        x = x + 0.5 * swiglu(rmsnorm_2(x, ffn_norm[l, 0]), ffn_w_gate_up[l, 0], ffn_w_down[l, 0])

        h = rmsnorm_2(x, mix_norm[l])
        mkv = mem_n @ mem_w_kv[l]
        mk = mkv[..., :MEM_WIDTH].reshape(b, m, MEM_HEADS, MEM_HEAD_DIM)
        mv = mkv[..., MEM_WIDTH:].reshape(b, m, MEM_HEADS, MEM_HEAD_DIM)
        if l < N_A:
            i = l
            proj = h @ a_w_in[i]
            gate_b = proj[..., :CONV_DIM]
            gate_c = proj[..., CONV_DIM:2 * CONV_DIM]
            u = proj[..., 2 * CONV_DIM:3 * CONV_DIM]
            qm = proj[..., 3 * CONV_DIM:].reshape(b, s, MEM_HEADS, MEM_HEAD_DIM)
            y_tok = gate_b * causal_depthwise_conv(gate_c * u, a_conv_w[i])
            y_mem = memory_attention(qm, mk, mv)
            x = x + jnp.concatenate([y_tok, y_mem], axis=-1) @ a_w_out[i]
        else:
            j = l - N_A
            proj = h @ b_w_q[j]
            q = proj[..., :FOX_WIDTH].reshape(b, s, FOX_HEADS, FOX_HEAD_DIM)
            qm = proj[..., FOX_WIDTH:].reshape(b, s, MEM_HEADS, MEM_HEAD_DIM)
            y_tok = forgetting_attention(q, k_sh, v_sh, c_sh)
            y_mem = memory_attention(qm, mk, mv)
            x = x + jnp.concatenate([y_tok, y_mem], axis=-1) @ b_w_out[j]

        x = x + 0.5 * swiglu(rmsnorm_2(x, ffn_norm[l, 1]), ffn_w_gate_up[l, 1], ffn_w_down[l, 1])

    return rmsnorm_2(x, final_norm)


def setup_inputs(seed=0):
    out = dict(first_inputs(seed))
    for name, value in second_inputs(seed + 1).items():
        if name != "x":
            out[name + "_2"] = value
    return out


def reference(
    x, positions, norm_mix_g, norm_ffn_g, ssd_in_w, ssd_conv_w, ssd_conv_b, ssd_dt_bias,
    ssd_a_log, ssd_d, ssd_norm_g, ssd_out_w, attn_in_w, attn_q_norm_g, attn_k_norm_g, attn_lq1,
    attn_lk1, attn_lq2, attn_lk2, attn_subln_g, attn_out_w, ffn_up_w, ffn_conv_w, ffn_conv_b,
    ffn_down_w, mem_2, ffn_norm_2, ffn_w_gate_up_2, ffn_w_down_2, mix_norm_2, mem_norm_2,
    mem_w_kv_2, a_w_in_2, a_conv_w_2, a_w_out_2, kv_norm_2, w_kvf_2, b_f_2, b_w_q_2, b_w_out_2,
    final_norm_2,
):
    x = first_block(
        x, positions, norm_mix_g, norm_ffn_g, ssd_in_w, ssd_conv_w, ssd_conv_b, ssd_dt_bias,
        ssd_a_log, ssd_d, ssd_norm_g, ssd_out_w, attn_in_w, attn_q_norm_g, attn_k_norm_g,
        attn_lq1, attn_lk1, attn_lq2, attn_lk2, attn_subln_g, attn_out_w, ffn_up_w, ffn_conv_w,
        ffn_conv_b, ffn_down_w,
    )
    return second_block(
        x, mem_2, ffn_norm_2, ffn_w_gate_up_2, ffn_w_down_2, mix_norm_2, mem_norm_2, mem_w_kv_2,
        a_w_in_2, a_conv_w_2, a_w_out_2, kv_norm_2, w_kvf_2, b_f_2, b_w_q_2, b_w_out_2,
        final_norm_2,
    )


_drawn_inputs = setup_inputs


def setup_inputs(seed=0):
    import zlib

    import numpy as np

    out = dict(_drawn_inputs(seed))
    spreads = {}
    factors = {'ssd_conv_b': 2.775,
     'attn_q_norm_g': 2.885,
     'attn_k_norm_g': 2.957,
     'attn_lk1': 3.189,
     'attn_lk2': 5.004,
     'attn_subln_g': 3.048,
     'ffn_conv_b': 3.653,
     'ffn_norm_2': 4.304,
     'mix_norm_2': 2.909,
     'mem_norm_2': 8.0,
     'kv_norm_2': 8.0,
     'final_norm_2': 2.731}
    for name, (base, spread) in spreads.items():
        noise = np.random.default_rng([zlib.crc32(name.encode()), seed]).standard_normal(out[name].shape)
        drawn = base * np.exp(spread * noise) if base else spread * noise
        out[name] = __import__('jax').numpy.asarray(drawn.astype(out[name].dtype))
    for name, factor in factors.items():
        out[name] = (out[name] * factor).astype(out[name].dtype)
    return out
```

```python
import math
from contextlib import ExitStack, contextmanager

import numpy as np

import concourse.bass as bass
from concourse import mybir

F32 = mybir.dt.float32
F32R = mybir.dt.float32r
I32 = mybir.dt.int32
ACT = mybir.ActivationFunctionType
ALU = mybir.AluOpType
AX_X = mybir.AxisListType.X

P = 128
T = 256
TH = T // P
D = 1024
DK = D // P
EPS = 1e-6
RING = 3

SSD_INNER, SSD_GROUPS, SSD_STATE, SSD_HEADS, SSD_HD, SSD_TAPS = 2048, 4, 128, 32, 64, 4
SSD_XBC = SSD_INNER + 2 * SSD_GROUPS * SSD_STATE
FF = 2816
FT = FF // P
FU = FT // 2
ATT_HEADS, ATT_HD = 8, 64
ROPE_HALF, THETA = 8, 500000.0
LAMBDA_INIT = 0.8 - 0.6 * math.exp(-0.3)
MEM_HEADS, FOX_HEADS = 4, 8
MASKED = -3.0e38
TWO_PI_HI = 6.28125
TWO_PI_LO = 2 * math.pi - 6.28125
ROUND = 1.5 * 2.0 ** 23


class Tally:

    def __init__(self, sem, start, step):
        self.sem, self.n, self.step, self.loop, self.per = sem, start, step, None, 0

    def value(self, ahead=0):
        v = (self.n + ahead) * self.step
        return v if self.loop is None else v + self.loop * (self.per * self.step)

    def plus(self):
        self.n += 1
        return self.step

    def next(self, n=1):
        self.n += n
        return self.value()

    def due(self, n=1):
        self.n += n
        return self.loop is not None or self.n > 0


class Counts:

    def __init__(self, eng, sem):
        self.eng, self.sem, self.all = eng, sem, {}

    def __call__(self, name, start=0, step=1):
        t = self.all.get((name, start))
        if t is None:
            t = self.all[(name, start)] = Tally(self.sem(name), start, step)
        return t

    @contextmanager
    def repeat(self, trips, counts):
        starts = {t: t.n for t in self.all.values()}
        with self.eng.Fori(0, trips) as i:
            for t, per in counts.items():
                t.loop, t.per = i, per
            yield i
        for t, n in starts.items():
            per = counts.get(t, 0)
            assert t.n - n == per, (str(t.sem), t.n - n, per)
            t.n = n + per * trips
            t.loop = None


VECTOR_ROWS = [
    ("norm_mix_g", 2 * DK), ("norm_ffn_g", 2 * DK), ("ffn_norm_2", 4 * DK), ("mix_norm_2", 2 * DK),
    ("mem_norm_2", DK), ("kv_norm_2", DK), ("final_norm_2", DK), ("ssd_norm_g", SSD_INNER // P),
    ("ssd_conv_w", SSD_TAPS * SSD_XBC // P), ("ssd_conv_b", SSD_XBC // P),
    ("ffn_conv_w", 2 * 3 * 2 * FT), ("ffn_conv_b", 2 * 2 * FT), ("a_conv_w_2", 3 * DK),
    ("attn_subln_g", 1), ("attn_q_norm_g", 1), ("attn_k_norm_g", 1),
]
VECTOR_ROWS.append(("pad", -sum(n for _, n in VECTOR_ROWS) % P))
COL = {}
_n = 0
for _name, _rows in VECTOR_ROWS:
    COL[_name] = _n
    _n += _rows
VECTORS = _n
VBLOCKS = -(-VECTORS // P)

STREAM = [
    ("up", "mem_w_kv_2", (0,), 4), ("up", "mem_w_kv_2", (1,), 4),
    ("up", "ssd_in_w", (0,), 20), ("down", "ssd_out_w", (0,), 8),
    ("ffn", ("ffn_up_w", "ffn_down_w"), (0,), 3 * FU),
    ("up", "attn_in_w", (0,), 12), ("down", "attn_out_w", (0,), 4),
    ("ffn", ("ffn_up_w", "ffn_down_w"), (1,), 3 * FU),
    ("ffn", ("ffn_w_gate_up_2", "ffn_w_down_2"), (0, 0), 3 * FU),
    ("up", "a_w_in_2", (0,), 14), ("down", "a_w_out_2", (0,), 6),
    ("ffn", ("ffn_w_gate_up_2", "ffn_w_down_2"), (0, 1), 3 * FU),
    ("up", "w_kvf_2", (), 8),
    ("ffn", ("ffn_w_gate_up_2", "ffn_w_down_2"), (1, 0), 3 * FU),
    ("up", "b_w_q_2", (0,), 6), ("down", "b_w_out_2", (0,), 6),
    ("ffn", ("ffn_w_gate_up_2", "ffn_w_down_2"), (1, 1), 3 * FU),
]
UNITS = sum(s[3] for s in STREAM)



POOL_MADE = 9 + 2 + ROPE_HALF + 3 + 1 + 4
EXTRAS = 9


def staged_loads():
    n, row = 1, 0
    for name, k in VECTOR_ROWS:
        n += 2 if name in ("attn_q_norm_g", "attn_k_norm_g") else (row + k - 1) // P - row // P + 1
        row += k
    return n


STAGED = staged_loads()


def build_program(nc, A, out):
    with ExitStack() as ctx:
        def sb(name, shape, dt=F32):
            return ctx.enter_context(nc.sbuf_tensor(name, shape, dt))

        sems = {}

        def sem(name):
            if name not in sems:
                sems[name] = ctx.enter_context(nc.semaphore(name))
            return sems[name]

        raw = sb("raw_weights", [P, RING, 2048])
        w_hi = sb("weights_hi", [P, RING, 2048], F32R)
        w_lo = sb("weights_lo", [P, RING, 2048], F32R)
        act_hi = sb("down_in_hi", [P, RING, 2, T], F32R)
        act_lo = sb("down_in_lo", [P, RING, 2, T], F32R)
        x = sb("residual", [P, DK, T])
        h_hi = sb("normed_hi", [P, DK, T], F32R)
        h_lo = sb("normed_lo", [P, DK, T], F32R)
        proj = sb("proj", [P, 40, T])
        mem_k = sb("mem_k", [P, 2, MEM_HEADS, T])
        mem_v = sb("mem_v", [P, 2, TH, MEM_HEADS * P])
        vec = sb("vectors", [P, VBLOCKS * P])
        rstd = sb("rstd", [P, T])
        small_raw = sb("small_w_raw", [P, DK, 32])
        small_hi = sb("small_w_hi", [P, DK, 32], F32R)
        small_lo = sb("small_w_lo", [P, DK, 32], F32R)
        ident = sb("ident", [P, P])
        ones = sb("ones", [P, P])
        upper = sb("upper", [P, P])
        half_ones = sb("half_ones", [P, P])
        swap = sb("rope_swap", [P, P])
        chunk_mask = sb("chunk_mask", [P, T])
        causal_mask = sb("causal_mask", [P, T])
        cos = sb("cos", [P, T])
        sin = sb("sin", [P, T])
        cols = sb("columns", [P, 64])
        eps_col, lam_col, subln_col, freq_col = (cols[:, i:i + 1] for i in range(4))
        log_f = cols[:, 16:32].rearrange("p (a h) -> p a h", a=TH)
        cum_f = cols[:, 32:48].rearrange("p (a h) -> p a h", a=TH)
        gate_bias = cols[:, 48:56]
        heads = sb("head_rows", [P, 4, 32])
        S = sb("scratch", [P, 7168])

        def scr(at, *shape):
            n = int(np.prod(shape))
            assert at + n <= 7168
            v = S[:, at:at + n]
            if len(shape) == 1:
                return v
            names = "abc"[:len(shape)]
            return v.rearrange("p (" + " ".join(names) + ") -> p " + " ".join(names),
                               **{names[i]: shape[i] for i in range(1, len(shape))})

        ps = ctx.enter_context(nc.psum_tensor("ps", [P, 8, 512], F32))
        STAT = 7

        squares = scr(0, DK, T)
        partial = scr(2048, T)
        f_in = scr(2304, 2, 2, T)
        f_out = scr(3328, 2, 2, T)
        hidden = scr(4352, 2, T)
        conv_in = [scr(2304 + 512 * s, 2, T) for s in range(RING)]
        conv_out = [scr(3840 + 512 * s, 2, T) for s in range(RING)]
        freq_row = scr(7040, P)[0:1, :]
        x_dt = [[scr(1024 * g + 512 * a, 8, 64) for a in range(TH)] for g in range(2)]
        state = [scr(2048 + 512 * g, 512) for g in range(2)]
        cb = scr(3072, 4, TH, P)
        b_tok = scr(4096, 4, P)
        x_dec = [scr(4608 + 512 * g, 8, 64) for g in range(2)]
        seg = [scr(5632 + 256 * i, T) for i in range(3)]
        row_e = [scr(6400 + 128 * i, P) for i in range(3)]
        dt_tok, dA, a_cs = scr(6784, 64), scr(6848, 64), scr(6912, 64)
        dt_dec, dec = scr(6976, 32), scr(7008, 32)
        sp = [scr(5632 + 64 * i, TH, 32) for i in range(8)]
        v_tok = scr(0, TH, 1024)
        s_buf = [scr(2048 + 512 * i, 2, T) for i in range(2)]
        p_buf = [scr(3072 + 512 * i, 2, T) for i in range(2)]
        probs = [scr(4096 + 256 * i, T) for i in range(2)]
        probs_t = [scr(4608 + 256 * i, T) for i in range(2)]
        tiny = [scr(5120 + 16 * i, 8, 2) for i in range(2)]
        key_row = [scr(5248, P), scr(5376, T)]
        qk_sq = [scr(1024 * i, 2, T) for i in range(2)]
        qk_rn = [scr(512 + 1024 * i, 2, T) for i in range(2)]
        qk_a, qk_b = scr(2048, 2, T), scr(2560, 2, T)
        wide_a, wide_b = scr(0, 8, T), scr(2048, 8, T)
        out_tok = scr(2304, TH, D)

        OUT = out.rearrange("b (a p) n -> p (b a) n", p=P)

        def rows(ap, n):
            return ap.unsqueeze(1).broadcast_to([P, n, ap.shape[-1]])

        def each(ap, n):
            return ap.unsqueeze(2).broadcast_to([P, ap.shape[-1], n])

        def flat(ap):
            return ap.rearrange("p k t -> p (k t)")

        def bank(b, n=2):
            return ps[:, b, :].rearrange("p (k t) -> p k t", k=n)

        def arr(name, idx):
            a = A[name]
            for i in idx:
                a = a[i]
            return a

        def vcol(name, i):
            return vec[:, bass.ds(COL[name] + i, 1)]

        def attention(kind):
            return {"diff": (ATT_HEADS, 0, 24, ATT_HD ** -0.5), "fox": (FOX_HEADS, 16, 28, P ** -0.5),
                    "mem0": (MEM_HEADS, 24, 36, P ** -0.5), "mem1": (MEM_HEADS, 24, 36, P ** -0.5)}[kind]

        def keys_of(kind, a):
            return T if kind.startswith("mem") else P * (a + 1)

        block = ctx.enter_context(nc.Block())

        @block.sync
        def _(sp_eng):
            sp = sp_eng
            c = Counts(sp, sem)
            final_ready = c("final_ready")
            lo_split = c("lo_split", -RING)
            stored = c("stored", step=16)
            landed = [c(f"landed{s}", step=16) for s in range(RING)]
            u = 0

            def load(dst, src, slot):
                if lo_split.due():
                    sp.wait_ge(lo_split.sem, lo_split.value())
                sp.dma_start(dst, src).then_inc(landed[slot].sem, landed[slot].plus())

            def up(w, col, slot):
                load(raw[:, slot, :].rearrange("p (k n) -> p k n", k=DK),
                     w.rearrange("(k p) n -> p k n", p=P)[:, :, bass.ds(col, 256)], slot)

            def down(w, j, slot):
                load(raw[:, slot, :].rearrange("p (j k n) -> p j k n", j=1, k=2),
                     w.rearrange("(j k p) n -> p j k n", k=2, p=P)[:, bass.ds(j, 1), :, :], slot)

            for kind, name, idx, n in STREAM:
                counts = {lo_split: RING, **{t: 1 for t in landed}}
                if kind == "ffn":
                    wu, wd = arr(name[0], idx), arr(name[1], idx)
                    up(wu, 0, u % RING)
                    up(wu, FF, (u + 1) % RING)
                    with c.repeat(FU - 1, counts) as i:
                        up(wu, i * 256 + 256, (u + 2) % RING)
                        up(wu, i * 256 + (256 + FF), u % RING)
                        down(wd, i, (u + 1) % RING)
                    down(wd, FU - 1, (u + 2) % RING)
                    u += 3 * FU
                    continue
                w = arr(name, idx)
                trips = n // RING if u >= RING else 0
                if trips:
                    with c.repeat(trips, counts) as i:
                        for j in range(RING):
                            if kind == "up":
                                up(w, i * (256 * RING) + 256 * j, (u + j) % RING)
                            else:
                                down(w, i * RING + j, (u + j) % RING)
                for j in range(trips * RING, n):
                    if kind == "up":
                        up(w, 256 * j, (u + j) % RING)
                    else:
                        down(w, j, (u + j) % RING)
                u += n
            assert u == UNITS
            for a in range(TH):
                sp.wait_ge(final_ready.sem, final_ready.next(2))
                sp.dma_start(OUT[:, a, :], out_tok[:, a, :]).then_inc(stored.sem, stored.plus())
            sp.wait_ge(stored.sem, stored.value())

        @block.gpsimd
        def _(pool):
            g = nc.gpsimd
            made = Counts(pool, sem)("pool_made")

            def fill(view, value):
                pool.wait_ge(made.sem, made.value())
                g.memset(view, value).then_inc(made.sem, made.plus())

            for m, v in ((ident, 0.0), (ones, 1.0), (upper, 1.0), (half_ones, 0.0), (swap, 0.0),
                         (chunk_mask, 0.0), (causal_mask, 0.0), (cols, EPS)):
                fill(m[:], v)
            fill(freq_row, 0.0)
            for a in range(2):
                fill(half_ones[64 * a:64 * a + 64, 64 * a:64 * a + 64], 1.0)
            row = freq_row.rearrange("p (a b c j) -> p a b c j", a=2, b=4, c=2)[:, :, 0, :, :]
            for j in range(ROPE_HALF):
                fill(row[:, :, :, j], float(np.float32(THETA) ** np.float32(-2.0 * j / (2 * ROPE_HALF))))

            def select(view, pattern, base, mult, value, op=ALU.not_equal):
                pool.wait_ge(made.sem, made.value())
                g.affine_select(out=view, in_=view, compare_op=op, fill=value, base=base, pattern=pattern,
                                channel_multiplier=mult).then_inc(made.sem, made.plus())

            select(ident[:], [[-1, P]], 0, 1, 1.0)
            select(upper[:], [[1, P]], 0, -1, 0.0, ALU.is_ge)
            select(causal_mask[:, P:T], [[-1, P]], 0, 1, MASKED, ALU.is_ge)
            fill(chunk_mask[0:64, P + 64:T], MASKED)
            for b in (0, 64):
                select(swap[:, b:b + 8], [[-1, 8]], -(b + 8), 1, -1.0)
                select(swap[:, b + 8:b + 16], [[-1, 8]], -b, 1, 1.0)
            assert made.n == POOL_MADE

        @block.tensor
        def _(pe):
            mm = nc.tensor.matmul
            c = Counts(pe, sem)
            bank_free = c("bank_free")
            bank_summed = c("bank_summed")
            cb_done = c("cb_done")
            cum_f_done = c("cum_f_done")
            cumsum_done = c("cumsum_done")
            dA_ready = c("dA_ready")
            evacuated = c("evacuated", -2)
            final_normed = c("final_normed")
            freq_done = c("freq_done")
            group_sum = c("group_sum")
            h_ready = c("h_ready")
            hid_ready = c("hid_ready")
            in_ready = c("in_ready")
            lo_split = c("lo_split")
            log_f_ready = c("log_f_ready")
            mask_ready = c("mask_ready")
            o_squares = c("o_squares")
            o_summed = c("o_summed")
            out_done = c("out_done")
            out_read = c("out_read", -2)
            pool_made = c("pool_made")
            probs_copied = c("probs_copied")
            probs_ready = c("probs_ready")
            probs_turned = c("probs_turned")
            qk_normed = c("qk_normed")
            qk_rotated = c("qk_rotated", -2)
            qk_squares = c("qk_squares")
            qk_summed = c("qk_summed")
            qk_swapped = c("qk_swapped")
            row_exp = c("row_exp", -2)
            rows_done = c("rows_done")
            scored = c("scored")
            setup_read = c("setup_read")
            small_done = c("small_done")
            small_ready = c("small_ready")
            staged = c("staged", step=16)
            stat_done = c("stat_done")
            state_done = c("state_done")
            state_ready = c("state_ready")
            su_done = c("su_done")
            sums_ready = c("sums_ready")
            turned = c("turned")
            x_dt_ready = c("x_dt_ready")
            x_staged = c("x_staged", step=16)
            y_done = c("y_done")
            y_read = c("y_read", -2)
            y_squares = c("y_squares")
            slot = [0]

            def up_unit(first=False):
                s = slot[0]
                pe.wait_ge(lo_split.sem, lo_split.next())
                if evacuated.due():
                    pe.wait_ge(evacuated.sem, evacuated.value())
                wh = w_hi[:, s, :].rearrange("p (k n) -> p k n", k=DK)
                wl = w_lo[:, s, :].rearrange("p (k n) -> p k n", k=DK)
                for k in range(DK):
                    if first:
                        pe.wait_ge(h_ready.sem, h_ready.next())
                    for a in range(2):
                        o = ps[:, 4 + s, a * T:(a + 1) * T]
                        hi, lo = wh[:, k, a * P:(a + 1) * P], wl[:, k, a * P:(a + 1) * P]
                        mm(o, hi, h_hi[:, k, :], start=(k == 0 and a == 0), stop=False, skip_group_check=True)
                        mm(o, hi, h_lo[:, k, :], start=False, stop=False, skip_group_check=True)
                        last = mm(o, lo, h_hi[:, k, :], start=False, stop=(k == DK - 1), skip_group_check=True)
                last.then_inc(su_done.sem, su_done.plus())
                slot[0] = (s + 1) % RING

            def down_unit(first=False, last=False):
                s = slot[0]
                pe.wait_ge(lo_split.sem, lo_split.next())
                pe.wait_ge(hid_ready.sem, hid_ready.next())
                wh = w_hi[:, s, :].rearrange("p (k n) -> p k n", k=2)
                wl = w_lo[:, s, :].rearrange("p (k n) -> p k n", k=2)
                for m in range(DK):
                    o = ps[:, m // 2, (m % 2) * T:(m % 2 + 1) * T]
                    for k in range(2):
                        hi, lo = wh[:, k, m * P:(m + 1) * P], wl[:, k, m * P:(m + 1) * P]
                        mm(o, hi, act_hi[:, s, k, :], start=(first and k == 0 and m % 2 == 0), stop=False,
                           skip_group_check=True)
                        mm(o, hi, act_lo[:, s, k, :], start=False, stop=False, skip_group_check=True)
                        ins = mm(o, lo, act_hi[:, s, k, :], start=False, stop=(k == 1), skip_group_check=True)
                    if last and m % 2:
                        ins.then_inc(bank_summed.sem, bank_summed.plus())
                if not last:
                    ins.then_inc(su_done.sem, su_done.plus())
                slot[0] = (s + 1) % RING

            def norm_sum():
                pe.wait_ge(sums_ready.sem, sums_ready.next())
                mm(ps[:, STAT, 0:T], ones[:], partial, start=True, stop=True).then_inc(stat_done.sem, stat_done.plus())

            def ups(n, peeled=1):
                up_unit(first=True)
                norm_sum()
                for _ in range(peeled - 1):
                    up_unit()
                n -= peeled - 1
                with c.repeat((n - 1) // RING, {lo_split: RING, evacuated: RING, su_done: RING}):
                    for _ in range(RING):
                        up_unit()
                for _ in range((n - 1) % RING):
                    up_unit()

            def downs(n):
                down_unit(first=True)
                trips = (n - 2) // RING if n >= 2 + 2 * RING else 0
                if trips:
                    with c.repeat(trips, {lo_split: RING, hid_ready: RING, su_done: RING}):
                        for _ in range(RING):
                            down_unit()
                for _ in range(n - 2 - RING * trips):
                    down_unit()
                down_unit(last=True)

            def ffn(stats=True):
                up_unit(first=True)
                if stats:
                    norm_sum()
                up_unit()
                up_unit()
                up_unit()
                down_unit(first=True)
                with c.repeat(FU - 2, {lo_split: 3, evacuated: 2, su_done: 3, hid_ready: 1}):
                    up_unit()
                    up_unit()
                    down_unit()
                down_unit(last=True)

            def turn_tiles(b, blocks):
                for j, t in enumerate(blocks):
                    last = nc.tensor.transpose(ps[:, b, j * P:(j + 1) * P], t, ident[:])
                last.then_inc(turned.sem, turned.plus())

            def turn_input(tok):
                for b in range(4):
                    turn_tiles(b, [tok[:, a, (2 * b + j) * P:(2 * b + j + 1) * P]
                                   for j in range(2) for a in range(TH)])

            def tok_view(first):
                return flat(proj[:, first:first + 8, :]).rearrange("p (a n) -> p a n", a=TH)

            def small_product(n):
                pe.wait_ge(small_ready.sem, small_ready.next())
                for a in range(TH):
                    o = ps[:, STAT, T + 32 * a:T + 32 * a + n]
                    tok = slice(a * P, (a + 1) * P)
                    for k in range(DK):
                        mm(o, h_hi[:, k, tok], small_hi[:, k, 0:n], start=(k == 0), stop=False)
                        mm(o, h_lo[:, k, tok], small_hi[:, k, 0:n], start=False, stop=False)
                        mm(o, h_hi[:, k, tok], small_lo[:, k, 0:n], start=False, stop=(k == DK - 1))
                for a in range(TH):
                    last = mm(ps[:, STAT, T + 64 + a:T + 65 + a], rstd[0:1, a * P:(a + 1) * P],
                              ones[0:1, 0:1], start=True, stop=True)
                last.then_inc(small_done.sem, small_done.plus())

            def ssd_core():
                pe.wait_ge(dA_ready.sem, dA_ready.next())
                mm(ps[:, STAT, 0:64], upper[:], dA, start=True, stop=True)
                mm(ps[:, STAT, 64:96], ones[:], dA[:, 0:32], start=True, stop=True).then_inc(cumsum_done.sem, cumsum_done.plus())
                pe.wait_ge(in_ready.sem, in_ready.next(20))
                turn_tiles(6, [proj[:, 32 + g, 0:P] for g in range(SSD_GROUPS)])
                for a in range(TH):
                    for g in range(SSD_GROUPS):
                        tok = slice(a * P, (a + 1) * P)
                        last = mm(ps[:, 4 + a, g * P:(g + 1) * P], proj[:, 32 + g, tok], proj[:, 36 + g, tok],
                                  start=True, stop=True)
                last.then_inc(cb_done.sem, cb_done.plus())
                pe.wait_ge(bank_free.sem, bank_free.next())

                def group(g):
                    for a in range(TH):
                        turn_tiles(a, [proj[:, 16 + 4 * g + j, a * P:(a + 1) * P] for j in range(4)])
                    pe.wait_ge(x_dt_ready.sem, x_dt_ready.next())
                    mm(ps[:, 6, :], b_tok[:, g, :], flat(x_dec[g % 2]), start=True, stop=True).then_inc(state_done.sem, state_done.plus())

                def head_rows(h):
                    if row_exp.due():
                        pe.wait_ge(row_exp.sem, row_exp.value())
                    for a in range(TH):
                        last = mm(ps[:, 2 + h % 2, a * P:(a + 1) * P],
                                  dA[:, 32 * a + h:32 * a + h + 1].to_broadcast([P, P]), upper[:],
                                  start=True, stop=True)
                    last.then_inc(rows_done.sem, rows_done.plus())

                def head_out(h):
                    g, p0 = h // 8, 64 * (h % 2)
                    pe.wait_ge(mask_ready.sem, mask_ready.next())
                    if h % 8 == 0:
                        pe.wait_ge(state_ready.sem, state_ready.next())
                    if h % 2 == 0:
                        if y_read.due():
                            pe.wait_ge(y_read.sem, y_read.value())
                    o = ps[p0:p0 + 64, 4 + h // 2 % 2, :]
                    m = seg[h % 3]
                    mm(o[:, 0:P], x_dt[g % 2][0][:, h % 8, :], m[:, 0:P], start=True, stop=True)
                    mm(o[:, P:T], x_dt[g % 2][1][:, h % 8, :], m[:, P:T], start=True, stop=False)
                    mm(o[:, P:T], state[g % 2][:, 64 * (h % 8):64 * (h % 8) + 64],
                                        row_e[h % 3], start=False, stop=True).then_inc(y_done.sem, y_done.plus())

                group(0)
                head_rows(0)
                for h in range(SSD_HEADS):
                    if h + 1 < SSD_HEADS:
                        head_rows(h + 1)
                    if h % 8 == 5 and h // 8 + 1 < SSD_GROUPS:
                        group(h // 8 + 1)
                    head_out(h)
                for g in range(SSD_GROUPS):
                    pe.wait_ge(y_squares.sem, y_squares.next())
                    for j in range(4):
                        last = mm(ps[:, g // 2, (g % 2) * T:(g % 2 + 1) * T], ones[:],
                                  scr(1024 * (g % 2), 4, T)[:, j, :], start=(j == 0), stop=(j == 3))
                    last.then_inc(group_sum.sem, group_sum.plus())

            def softmax_attention(kind):
                n_heads, q0, _, _ = attention(kind)

                def scores(n):
                    h, a, b = n // 2, n % 2, 2 * (n % 2)
                    nk = keys_of(kind, a)
                    q = proj[:, q0 + h, a * P:(a + 1) * P]
                    if kind == "diff":
                        for half in range(2):
                            f = slice(64 * half, 64 * half + 64)
                            last = mm(ps[:, b + half, 0:nk], q[f, :], proj[f, 8 + h, 0:nk], start=True, stop=True)
                    elif kind == "fox":
                        if a == 0:
                            f0 = log_f[:, 0, h:h + 1].to_broadcast([P, P])
                            mm(ps[:, 1, 0:P], f0, upper[:], start=True, stop=True)
                            mm(ps[:, 1, P:T], f0, ones[:], start=True, stop=False)
                            mm(ps[:, 1, P:T], log_f[:, 1, h:h + 1].to_broadcast([P, P]), upper[:],
                               start=False, stop=True)
                        last = mm(ps[:, b, 0:nk], q, proj[:, h, 0:nk], start=True, stop=True)
                    else:
                        last = mm(ps[:, b, 0:nk], q, mem_k[:, int(kind[3]), h, :], start=True, stop=True)
                    last.then_inc(scored.sem, scored.plus())

                def turn(n):
                    nk = keys_of(kind, n % 2)
                    pe.wait_ge(probs_ready.sem, probs_ready.next())
                    for kb in range(nk // P):
                        last = nc.tensor.transpose(ps[:, 4 + n % 2, kb * P:(kb + 1) * P],
                                                   probs[n % 2][:, kb * P:(kb + 1) * P], ident[:])
                    last.then_inc(probs_turned.sem, probs_turned.plus())

                def values(n):
                    h, a = n // 2, n % 2
                    nk = keys_of(kind, a)
                    if a == 0:
                        if out_read.due():
                            pe.wait_ge(out_read.sem, out_read.value())
                    pe.wait_ge(probs_copied.sem, probs_copied.next())
                    for kb in range(nk // P):
                        v = (mem_v[:, int(kind[3]), kb, h * P:(h + 1) * P] if kind.startswith("mem")
                             else v_tok[:, kb, h * P:(h + 1) * P])
                        last = mm(ps[:, 6 + h % 2, a * P:(a + 1) * P], v, probs_t[n % 2][:, kb * P:(kb + 1) * P],
                                  start=(kb == 0), stop=(kb == nk // P - 1))
                    if a == 1:
                        last.then_inc(out_done.sem, out_done.plus())

                n_units = 2 * n_heads
                scores(0)
                for n in range(n_units):
                    if n + 1 < n_units:
                        scores(n + 1)
                    turn(n)
                    if n >= 1:
                        values(n - 1)
                values(n_units - 1)

            def turn_values(v0):
                for a in range(TH):
                    for b in range(2):
                        turn_tiles(4 + 2 * a + b, [proj[:, v0 + 4 * b + h, a * P:(a + 1) * P] for h in range(4)])
                pe.wait_ge(bank_free.sem, bank_free.next(4))

            pe.wait_ge(pool_made.sem, pool_made.next(POOL_MADE))
            pe.wait_ge(staged.sem, staged.next(STAGED))
            turn_input(tok_view(8))
            vrows = flat(proj[:, 24:27, :])
            turn_tiles(4, [vrows[:, b * P:(b + 1) * P] for b in range(4)])
            turn_tiles(5, [vrows[:, b * P:(b + 1) * P] for b in range(4, VBLOCKS)])
            mm(ps[:, 6, 0:1], freq_row, ones[0:1, 0:1], start=True, stop=True).then_inc(freq_done.sem, freq_done.plus())
            pe.wait_ge(setup_read.sem, setup_read.next(3))

            ups(8, peeled=2)
            pe.wait_ge(evacuated.sem, evacuated.value(2))
            for l in range(2):
                for a in range(TH):
                    turn_tiles(2 * l + a, [proj[:, 16 + 4 * l + h, a * P:(a + 1) * P] for h in range(MEM_HEADS)])
            pe.wait_ge(bank_free.sem, bank_free.next(4))
            pe.wait_ge(x_staged.sem, x_staged.next())
            turn_input(tok_view(0))

            ups(20)
            small_product(SSD_HEADS)
            ssd_core()
            downs(8)
            ffn()

            ups(12)
            pe.wait_ge(evacuated.sem, evacuated.value(2))

            def qk_sum(j):
                pe.wait_ge(qk_squares.sem, qk_squares.next())
                mm(ps[:, j % 2, :], half_ones[:], flat(qk_sq[j % 2]), start=True, stop=True).then_inc(qk_summed.sem, qk_summed.plus())

            qk_sum(0)
            for j in range(8):
                if j < 7:
                    qk_sum(j + 1)
                pe.wait_ge(qk_normed.sem, qk_normed.next())
                if qk_rotated.due():
                    pe.wait_ge(qk_rotated.sem, qk_rotated.value())
                mm(ps[:, 2 + j % 2, :], swap[:], flat(proj[:, 2 * j:2 * j + 2, :]),
                                        start=True, stop=True).then_inc(qk_swapped.sem, qk_swapped.plus())
            if qk_rotated.due(2):
                pe.wait_ge(qk_rotated.sem, qk_rotated.value())
            turn_values(16)
            softmax_attention("diff")
            pe.wait_ge(o_squares.sem, o_squares.next())
            for j in range(4):
                last = mm(ps[:, j, :], ones[:], flat(wide_a[:, 2 * j:2 * j + 2, :]), start=True, stop=True)
            last.then_inc(o_summed.sem, o_summed.plus())
            downs(4)
            ffn()
            ffn()

            ups(14)
            pe.wait_ge(evacuated.sem, evacuated.value(2))
            softmax_attention("mem0")
            downs(6)
            ffn()

            ups(8)
            small_product(FOX_HEADS)
            pe.wait_ge(log_f_ready.sem, log_f_ready.next())
            mm(ps[:, STAT, 0:8], upper[:], log_f[:, 0, :], start=True, stop=True)
            mm(ps[:, STAT, 8:16], ones[:], log_f[:, 0, :], start=True, stop=False)
            mm(ps[:, STAT, 8:16], upper[:], log_f[:, 1, :], start=False, stop=True).then_inc(cum_f_done.sem, cum_f_done.plus())
            ffn(stats=False)

            ups(6)
            pe.wait_ge(evacuated.sem, evacuated.value(2))
            turn_values(8)
            softmax_attention("fox")
            softmax_attention("mem1")
            downs(6)
            ffn()

            norm_sum()
            pe.wait_ge(final_normed.sem, final_normed.next())
            for a in range(TH):
                for b in range(2):
                    turn_tiles(2 * a + b, [squares[:, 4 * b + j, a * P:(a + 1) * P] for j in range(4)])

        @block.scalar
        def _(act):
            f = nc.scalar.activation
            c = Counts(act, sem)
            act_hi_made = c("act_hi_made")
            biased = c("biased")
            conv_base = c("conv_base")
            conv_done = c("conv_done")
            decay_done = c("decay_done")
            decay_in = c("decay_in")
            decay_rate = c("decay_rate")
            decay_ready = c("decay_ready")
            evacuated = c("evacuated")
            exps_done = c("exps_done")
            extras = c("extras_staged", step=16)
            gate_act = c("gate_act")
            gate_ready = c("gate_ready")
            gated = c("gated")
            gated_input = c("gated_input")
            group_rstd = c("group_rstd")
            group_sum = c("group_sum")
            h_hi_made = c("h_hi_made")
            half_sin = c("half_sin")
            hi_split = c("hi_split")
            hidden_ready = c("hidden_ready")
            in_ready = c("in_ready")
            kv_done = c("kv_done")
            lam_exp = c("lam_exp")
            lam_in = c("lam_in")
            o_rstd = c("o_rstd")
            o_squares = c("o_squares")
            o_summed = c("o_summed")
            out_done = c("out_done")
            out_read = c("out_read")
            pool_made = c("pool_made")
            probs_copied = c("probs_copied")
            probs_turned = c("probs_turned")
            qk_old = c("qk_normed", -2)
            qk_rstd = c("qk_rstd")
            qk_squares = c("qk_squares")
            qk_summed = c("qk_summed")
            row_exp = c("row_exp")
            rstd_ready = c("rstd_ready")
            scored = c("scored")
            seg_ready = c("seg_ready")
            shifted = c("shifted")
            small_free = c("small_free")
            small_hi_made = c("small_hi_made")
            small_landed = c("small_landed", step=16)
            source_ready = c("source_ready")
            sp_exp = c("sp_exp")
            sp_in = c("sp_in")
            sp_ln = c("sp_ln")
            sp_one = c("sp_one")
            squares_made = c("squares_made")
            staged = c("staged", step=16)
            stat_done = c("stat_done")
            state_done = c("state_done")
            state_ready = c("state_ready")
            step = c("act_step")
            su_done = c("su_done")
            trig_in = c("trig_in")
            x_ready = c("x_ready")
            x_staged = c("x_staged", step=16)
            y_squares = c("y_squares")
            landed = [c(f"landed{s}", step=16) for s in range(RING)]
            slot, unit = [0], [0]

            def split(s):
                act.wait_ge(landed[s].sem, landed[s].next())
                f(w_hi[:, s, :], raw[:, s, :], ACT.Copy).then_inc(hi_split.sem, hi_split.plus())

            def split_next(trips=1):
                if unit[0] + RING < UNITS:
                    split(slot[0])
                unit[0] += trips
                slot[0] = (slot[0] + 1) % RING

            def per_trip(**extra):
                return {hi_split: RING, su_done: RING, **{t: 1 for t in landed},
                        **{c(k): v for k, v in extra.items()}}

            def units(n, work, **extra):
                trips = n // RING
                if trips:
                    with c.repeat(trips, per_trip(**{k: RING * v for k, v in extra.items()})) as i:
                        for j in range(RING):
                            act.wait_ge(su_done.sem, su_done.next())
                            work(i * RING + j, slot[0])
                            split_next(trips)
                for j in range(trips * RING, n):
                    act.wait_ge(su_done.sem, su_done.next())
                    work(j, slot[0])
                    split_next()

            def columns():
                act.wait_ge(sem("setup_read"), 3)

            def skip(j, s):
                act.wait_ge(evacuated.sem, evacuated.next())

            def inverse_root(dst, src, scale):
                f(dst, src, ACT.Ln, bias=eps_col, scale=scale).then_inc(step.sem, step.plus())
                act.wait_ge(step.sem, step.value())
                return f(dst, dst, ACT.Exp, scale=-0.5)

            def norm(gain, g0, again=False, h=True, stats=True, split=True):
                for b in range(4):
                    if not again:
                        act.wait_ge(x_ready.sem, x_ready.next())
                    for k in (2 * b, 2 * b + 1):
                        if h:
                            f(h_hi[:, k, :], x[:, k, :], ACT.Copy, scale=vcol(gain, g0 + k)).then_inc(h_hi_made.sem, h_hi_made.plus())
                if stats:
                    f(squares, x[:], ACT.Square).then_inc(squares_made.sem, squares_made.plus())
                if split:
                    split_next()
                if stats:
                    act.wait_ge(stat_done.sem, stat_done.next())
                    inverse_root(rstd[:], ps[:, STAT, 0:T], 1.0 / D).then_inc(rstd_ready.sem, rstd_ready.plus())

            def feed(src, j, s):
                f(act_hi[:, s, :, :], src[:, 2 * j:2 * j + 2, :], ACT.Copy).then_inc(act_hi_made.sem, act_hi_made.plus())

            def downs(n, src):
                s = slot[0]
                for j in range(min(RING, n)):
                    feed(src, j, (s + j) % RING)
                for j in range(n - 1):
                    act.wait_ge(su_done.sem, su_done.next())
                    if j + RING < n:
                        feed(src, j + RING, (s + j) % RING)
                    split_next()

            def ffn(conv=None):
                def tap_and_bias(w, tile):
                    columns()
                    for a in range(2):
                        last = f(f_out[:, w, a, :], f_in[:, w, a, :], ACT.Identity,
                                 scale=vcol("ffn_conv_w", conv * 6 * FT + 4 * FT + a + tile),
                                 bias=vcol("ffn_conv_b", conv * 2 * FT + a + tile))
                    last.then_inc(conv_base.sem, conv_base.plus())

                def gate(j):
                    act.wait_ge(su_done.sem, su_done.next())
                    act.wait_ge(evacuated.sem, evacuated.next())
                    if conv is None:
                        f(f_out[:, 0, :, :], f_in[:, 0, :, :], ACT.Silu).then_inc(gate_act.sem, gate_act.plus())
                    else:
                        tap_and_bias(0, j * 2)
                    split_next()

                def up(j):
                    act.wait_ge(su_done.sem, su_done.next())
                    act.wait_ge(evacuated.sem, evacuated.next())
                    if conv is not None:
                        tap_and_bias(1, j * 2 + FT)
                        act.wait_ge(gate_ready.sem, gate_ready.next())
                        f(f_out[:, 0, :, :], f_out[:, 0, :, :], ACT.Silu).then_inc(gate_act.sem, gate_act.plus())
                    split_next()

                down_slot, last_slot = (slot[0] + 4) % RING, (slot[0] + 2) % RING

                def give(s):
                    act.wait_ge(hidden_ready.sem, hidden_ready.next())
                    f(act_hi[:, s, :, :], hidden, ACT.Copy).then_inc(act_hi_made.sem, act_hi_made.plus())

                gate(0)
                up(0)
                give(down_slot)
                extra = dict(evacuated=2, gate_act=1, hidden_ready=1, act_hi_made=1)
                if conv is not None:
                    extra.update(conv_base=2, gate_ready=1)

                def trip(j, s):
                    gate(j + 1)
                    up(j + 1)
                    act.wait_ge(su_done.sem, su_done.next())
                    give(s)
                    split_next()

                u0 = unit[0]
                with c.repeat(FU - 2, per_trip(**extra)) as i:
                    trip(i, down_slot)
                unit[0] = u0 + 3 * (FU - 2)
                trip(FU - 2, last_slot)

            def softmax_attention(kind):
                n_heads, _, out0, scale = attention(kind)

                def query_bias(n):
                    h, a = n // 2, n % 2
                    nk = keys_of(kind, a)
                    act.wait_ge(scored.sem, scored.next())
                    f(s_buf[n % 2][:, 0, 0:nk], ps[:, 2 * (n % 2), 0:nk], ACT.Identity,
                                       scale=scale, bias=cum_f[:, a, h:h + 1]).then_inc(biased.sem, biased.plus())

                def exps(n):
                    nk = keys_of(kind, n % 2)
                    t = tiny[n % 2]
                    act.wait_ge(shifted.sem, shifted.next())
                    if kind == "diff":
                        for j in range(2):
                            last = f(p_buf[n % 2][:, j, 0:nk], s_buf[n % 2][:, j, 0:nk], ACT.Exp,
                                     bias=t[:, 1, j:j + 1], accum_out=t[:, 2, j:j + 1])
                    elif kind == "fox":
                        last = f(p_buf[n % 2][:, 0, 0:nk], s_buf[n % 2][:, 0, 0:nk], ACT.Exp,
                                 bias=t[:, 1, 0:1], accum_out=t[:, 2, 0:1])
                    else:
                        last = f(p_buf[n % 2][:, 0, 0:nk], ps[:, 2 * (n % 2), 0:nk], ACT.Exp, scale=scale,
                                 bias=t[:, 1, 0:1], accum_out=t[:, 2, 0:1])
                    last.then_inc(exps_done.sem, exps_done.plus())

                def copy_turned(n):
                    nk = keys_of(kind, n % 2)
                    act.wait_ge(probs_turned.sem, probs_turned.next())
                    f(probs_t[n % 2][:, 0:nk], ps[:, 4 + n % 2, 0:nk], ACT.Copy).then_inc(probs_copied.sem, probs_copied.plus())

                def copy_out(h):
                    act.wait_ge(out_done.sem, out_done.next())
                    f(proj[:, out0 + h, :], ps[:, 6 + h % 2, 0:T], ACT.Copy).then_inc(out_read.sem, out_read.plus())

                n_units = 2 * n_heads
                if kind == "fox":
                    query_bias(0)
                else:
                    scored.n += n_units
                for n in range(n_units):
                    if kind == "fox" and n + 1 < n_units:
                        query_bias(n + 1)
                    exps(n)
                    if n >= 1:
                        copy_turned(n - 1)
                    if n % 2 == 1 and n >= 3:
                        copy_out((n - 3) // 2)
                copy_turned(n_units - 1)
                copy_out(n_heads - 1)
                act.wait_ge(out_read.sem, out_read.value())

            def softplus():
                act.wait_ge(sp_in.sem, sp_in.next())
                f(sp[1], sp[0], ACT.Abs).then_inc(step.sem, step.plus())
                act.wait_ge(step.sem, step.value())
                f(sp[2], sp[1], ACT.Exp, scale=-1.0).then_inc(sp_exp.sem, sp_exp.plus())
                act.wait_ge(sp_one.sem, sp_one.next())
                f(sp[4], sp[3], ACT.Ln).then_inc(sp_ln.sem, sp_ln.plus())

            def small_weights():
                act.wait_ge(small_landed.sem, small_landed.next())
                f(small_hi[:], small_raw[:], ACT.Copy).then_inc(small_hi_made.sem, small_hi_made.plus())

            vrows = flat(proj[:, 24:27, :])
            act.dma_start(flat(proj[:, 8:16, :]).rearrange("p (a n) -> p a n", a=TH),
                                      A["mem_2"][0].rearrange("(a p) n -> p a n", p=P)).then_inc(staged.sem, staged.plus())
            row = 0
            for name, n in VECTOR_ROWS:
                if name in ("attn_q_norm_g", "attn_k_norm_g"):
                    for half in range(2):
                        act.dma_start(
                            vrows[row % P:row % P + 1, row // P * P + 64 * half:row // P * P + 64 * half + 64],
                            A[name]).then_inc(staged.sem, staged.plus())
                    row += 1
                    continue
                src = A["ffn_conv_b" if name == "pad" else name]
                while len(src.shape) > 1:
                    dims = " ".join(f"d{i}" for i in range(len(src.shape)))
                    src = src.rearrange(f"{dims} -> ({dims})")
                src = src.rearrange("(r q) -> r q", q=P)
                at = 0
                while at < n:
                    k = min(n - at, P - row % P)
                    act.dma_start(vrows[row % P:row % P + k, row // P * P:row // P * P + P],
                                              src[at:at + k, :]).then_inc(staged.sem, staged.plus())
                    at += k
                    row += k
            assert staged.n == STAGED
            for i, name in enumerate(("ssd_dt_bias", "ssd_a_log", "ssd_d")):
                act.dma_start(heads[:, i, :], A[name].broadcast_to([P, SSD_HEADS])).then_inc(extras.sem, extras.plus())
            act.dma_start(scr(6400, T).bitcast(I32), A["positions"].broadcast_to([P, T])).then_inc(extras.sem, extras.plus())
            for i, name in enumerate(("attn_lq1", "attn_lk1", "attn_lq2", "attn_lk2")):
                act.dma_start(scr(6656, 4, 64)[:, i, :], A[name].broadcast_to([P, ATT_HD])).then_inc(extras.sem, extras.plus())
            act.wait_ge(pool_made.sem, pool_made.next(POOL_MADE))
            act.dma_start(gate_bias, A["b_f_2"].unsqueeze(0).broadcast_to([P, FOX_HEADS])).then_inc(extras.sem, extras.plus())
            assert extras.n == EXTRAS
            act.dma_start(
                flat(proj[:, 0:8, :]).rearrange("p (a n) -> p a n", a=TH),
                A["x"][0].rearrange("(a p) n -> p a n", p=P)).then_inc(x_staged.sem, x_staged.plus())
            act.dma_start(small_raw[:], A["ssd_in_w"][0].rearrange("(k p) n -> p k n", p=P)
                          [:, :, SSD_INNER + SSD_XBC:]).then_inc(sem("small_landed"), 16)
            for s in range(RING):
                split(s)

            norm("mem_norm_2", 0, split=False)
            units(8, skip, evacuated=1)

            def silu_z(j, s):
                act.wait_ge(evacuated.sem, evacuated.next())
                columns()
                z = proj[:, bass.ds(j * 2, 2), :]
                f(z, z, ACT.Silu).then_inc(in_ready.sem, in_ready.plus())

            def conv_xbc(j, s):
                act.wait_ge(evacuated.sem, evacuated.next())
                columns()
                for a in range(2):
                    last = f(conv_out[s][:, a, :], conv_in[s][:, a, :], ACT.Identity,
                             scale=vcol("ssd_conv_w", j * 2 + (3 * SSD_XBC // P + a)),
                             bias=vcol("ssd_conv_b", j * 2 + a))
                last.then_inc(conv_base.sem, conv_base.plus())
                act.wait_ge(conv_done.sem, conv_done.next())
                f(proj[:, bass.ds(j * 2 + 16, 2), :], conv_out[s], ACT.Silu).then_inc(in_ready.sem, in_ready.plus())

            norm("norm_mix_g", 0, split=False)
            act.wait_ge(trig_in.sem, trig_in.next())
            f(sin[:], scr(5632, T), ACT.Sin).then_inc(step.sem, step.plus())
            f(cos[:], scr(5632, T), ACT.Sin, scale=0.5).then_inc(half_sin.sem, half_sin.plus())
            act.wait_ge(lam_in.sem, lam_in.next(2))
            f(cols[:, 4:6], cols[:, 6:8], ACT.Exp).then_inc(lam_exp.sem, lam_exp.plus())
            units(8, silu_z, evacuated=1, in_ready=1)
            units(12, conv_xbc, evacuated=1, in_ready=1, conv_base=1, conv_done=1)
            small_weights()
            softplus()
            f(heads[:, 1, :], heads[:, 1, :], ACT.Exp).then_inc(decay_rate.sem, decay_rate.plus())
            act.wait_ge(decay_in.sem, decay_in.next())
            f(dec, dec, ACT.Exp).then_inc(decay_done.sem, decay_done.plus())

            def state_copy(g):
                act.wait_ge(state_done.sem, state_done.next())
                f(state[g % 2], ps[:, 6, :], ACT.Copy).then_inc(state_ready.sem, state_ready.plus())

            state_copy(0)
            for h in range(SSD_HEADS):
                act.wait_ge(seg_ready.sem, seg_ready.next())
                f(seg[h % 3], seg[h % 3], ACT.Exp).then_inc(decay_ready.sem, decay_ready.plus())
                f(row_e[h % 3], ps[:, 2 + h % 2, P:T], ACT.Exp).then_inc(row_exp.sem, row_exp.plus())
                if h % 8 == 6 and h // 8 + 1 < SSD_GROUPS:
                    state_copy(h // 8 + 1)
            act.wait_ge(gated.sem, gated.next())
            for g in range(SSD_GROUPS):
                if g >= 2:
                    act.wait_ge(group_sum.sem, group_sum.next())
                f(scr(1024 * (g % 2), 4, T), proj[:, 16 + 4 * g:20 + 4 * g, :], ACT.Square).then_inc(y_squares.sem, y_squares.plus())
            act.wait_ge(group_sum.sem, group_sum.next(2))
            inverse_root(scr(2048, 1024), ps[:, 0:2, :].rearrange("p b t -> p (b t)"),
                                              1.0 / (SSD_INNER // SSD_GROUPS)).then_inc(group_rstd.sem, group_rstd.plus())
            act.wait_ge(source_ready.sem, source_ready.next())
            downs(8, proj[:, 16:32, :])
            norm("norm_ffn_g", 0)
            ffn(conv=0)

            norm("norm_mix_g", DK)
            units(12, skip, evacuated=1)

            def qk_square(j):
                f(qk_sq[j % 2], proj[:, 2 * j:2 * j + 2, :], ACT.Square).then_inc(qk_squares.sem, qk_squares.plus())

            qk_square(0)
            for j in range(8):
                if j < 7:
                    qk_square(j + 1)
                act.wait_ge(qk_summed.sem, qk_summed.next())
                if qk_old.due():
                    act.wait_ge(qk_old.sem, qk_old.value())
                inverse_root(flat(qk_rn[j % 2]), ps[:, j % 2, :], 1.0 / ATT_HD).then_inc(qk_rstd.sem, qk_rstd.plus())
            softmax_attention("diff")
            f(wide_a, proj[:, 24:32, :], ACT.Square).then_inc(o_squares.sem, o_squares.plus())
            act.wait_ge(o_summed.sem, o_summed.next())
            inverse_root(flat(wide_b), ps[:, 0:4, :].rearrange("p b t -> p (b t)"), 1.0 / P).then_inc(o_rstd.sem, o_rstd.plus())
            act.wait_ge(source_ready.sem, source_ready.next())
            downs(4, proj[:, 24:32, :])
            norm("norm_ffn_g", DK)
            ffn(conv=1)
            norm("ffn_norm_2", 0)
            ffn()

            norm("mix_norm_2", 0)
            units(14, skip, evacuated=1)
            act.wait_ge(gated_input.sem, gated_input.next())
            for k in range(DK):
                last = f(proj[:, 28 + k, :], proj[:, 8 + k, :], ACT.Copy, scale=vcol("a_conv_w_2", 2 * DK + k))
            last.then_inc(conv_base.sem, conv_base.plus())
            softmax_attention("mem0")
            act.wait_ge(source_ready.sem, source_ready.next())
            downs(6, proj[:, 28:40, :])
            norm("ffn_norm_2", DK)
            ffn()

            act.wait_ge(small_free.sem, small_free.next())
            small_n = w_small_f = A["w_kvf_2"].rearrange("(k p) n -> p k n", p=P)[:, :, 2 * D:]
            act.dma_start(small_raw[:, :, 0:FOX_HEADS], w_small_f).then_inc(sem("small_landed"), 16)
            norm("kv_norm_2", 0)
            units(8, skip, evacuated=1)
            act.wait_ge(small_landed.sem, small_landed.next())
            f(small_hi[:, :, 0:FOX_HEADS], small_raw[:, :, 0:FOX_HEADS], ACT.Copy).then_inc(small_hi_made.sem, small_hi_made.plus())
            softplus()
            act.wait_ge(kv_done.sem, kv_done.next())
            norm("ffn_norm_2", 2 * DK, again=True, stats=False, split=False)
            ffn()

            norm("mix_norm_2", DK)
            units(6, skip, evacuated=1)
            softmax_attention("fox")
            softmax_attention("mem1")
            downs(6, proj[:, 28:40, :])
            norm("ffn_norm_2", 3 * DK)
            ffn()
            norm(None, 0, h=False)

        @block.vector
        def _(dve):
            v = nc.vector
            tt, stt, ts = v.tensor_tensor, v.scalar_tensor_tensor, v.tensor_scalar
            c = Counts(dve, sem)
            bank_summed = c("bank_summed")
            act_hi_made = c("act_hi_made")
            bank_free = c("bank_free")
            biased = c("biased")
            cb_done = c("cb_done")
            conv_base = c("conv_base")
            conv_done = c("conv_done")
            cum_f_done = c("cum_f_done")
            cumsum_done = c("cumsum_done")
            dA_ready = c("dA_ready")
            decay_done = c("decay_done")
            decay_in = c("decay_in")
            decay_rate = c("decay_rate")
            decay_ready = c("decay_ready")
            evacuated = c("evacuated")
            exps_done = c("exps_done")
            extras = c("extras_staged", step=16)
            final_normed = c("final_normed")
            final_ready = c("final_ready")
            freq_done = c("freq_done")
            gate_act = c("gate_act")
            gate_ready = c("gate_ready")
            gated = c("gated")
            gated_input = c("gated_input")
            group_rstd = c("group_rstd")
            h_hi_made = c("h_hi_made")
            h_ready = c("h_ready")
            half_sin = c("half_sin")
            hi_split = c("hi_split")
            hid_ready = c("hid_ready")
            hidden_ready = c("hidden_ready")
            in_ready = c("in_ready")
            kv_done = c("kv_done")
            lam_exp = c("lam_exp")
            lam_in = c("lam_in")
            lo_split = c("lo_split")
            log_f_ready = c("log_f_ready")
            mask_ready = c("mask_ready")
            o_rstd = c("o_rstd")
            out_read = c("out_read")
            pool_made = c("pool_made")
            probs_old = c("probs_turned", -2)
            probs_ready = c("probs_ready")
            qk_normed = c("qk_normed")
            qk_rotated = c("qk_rotated")
            qk_rstd = c("qk_rstd")
            qk_swapped = c("qk_swapped")
            row_exp = c("row_exp")
            rows_done = c("rows_done")
            rstd_ready = c("rstd_ready")
            scored = c("scored")
            seg_ready = c("seg_ready")
            setup_read = c("setup_read")
            shifted = c("shifted")
            small_done = c("small_done")
            small_free = c("small_free")
            small_hi_made = c("small_hi_made")
            small_ready = c("small_ready")
            source_ready = c("source_ready")
            sp_exp = c("sp_exp")
            sp_in = c("sp_in")
            sp_ln = c("sp_ln")
            sp_one = c("sp_one")
            squares_made = c("squares_made")
            step = c("vec_step")
            su_done = c("su_done")
            sums_ready = c("sums_ready")
            trig_in = c("trig_in")
            turned = c("turned")
            x_dt_ready = c("x_dt_ready")
            x_ready = c("x_ready")
            y_done = c("y_done")
            y_old = c("y_done", -3)
            y_read = c("y_read")
            slot, unit = [0], [0]

            def f32(ap):
                return ap.bitcast(F32)

            def split(s):
                dve.wait_ge(hi_split.sem, hi_split.next())
                tt(w_lo[:, s, :], raw[:, s, :], f32(w_hi[:, s, :]), ALU.subtract).then_inc(lo_split.sem, lo_split.plus())

            def split_next(trips=1):
                if unit[0] + RING < UNITS:
                    split(slot[0])
                unit[0] += trips
                slot[0] = (slot[0] + 1) % RING

            def per_trip(**extra):
                return {hi_split: RING, lo_split: RING, su_done: RING, **{c(k): n for k, n in extra.items()}}

            def units(n, work, **extra):
                trips = n // RING
                if trips:
                    with c.repeat(trips, per_trip(**{k: RING * m for k, m in extra.items()})) as i:
                        for j in range(RING):
                            dve.wait_ge(su_done.sem, su_done.next())
                            work(i * RING + j, slot[0])
                            split_next(trips)
                for j in range(trips * RING, n):
                    dve.wait_ge(su_done.sem, su_done.next())
                    work(j, slot[0])
                    split_next()

            def evacuate(dst, s):
                tt(dst, bank(4 + s), rows(rstd[:], 2), ALU.mult).then_inc(evacuated.sem, evacuated.plus())

            def to_proj(first):
                def work(j, s):
                    evacuate(proj[:, bass.ds(j * 2 + first, 2), :], s)
                return work

            def residual(scale=1.0):
                def take(b):
                    dve.wait_ge(bank_summed.sem, bank_summed.next())
                    t = x[:, 2 * b:2 * b + 2, :]
                    stt(t, bank(b), scale, t, ALU.mult, ALU.add).then_inc(x_ready.sem, x_ready.plus())
                return take

            def norm(gain, g0, take=None, stats=True, split=True):
                for b in range(5):
                    if take and b < 4:
                        take(b)
                    for k in (2 * b - 2, 2 * b - 1):
                        if gain and k >= 0:
                            dve.wait_ge(h_hi_made.sem, h_hi_made.next())
                            stt(h_lo[:, k, :], x[:, k, :], vcol(gain, g0 + k), f32(h_hi[:, k, :]),
                                ALU.mult, ALU.subtract).then_inc(h_ready.sem, h_ready.plus())
                if stats:
                    dve.wait_ge(squares_made.sem, squares_made.next())
                    v.tensor_reduce(partial, squares.rearrange("p k t -> p t k"), AX_X,
                                    ALU.add).then_inc(sums_ready.sem, sums_ready.plus())
                if split:
                    split_next()
                if stats:
                    dve.wait_ge(rstd_ready.sem, rstd_ready.next())

            def feed(src, j, s):
                dve.wait_ge(act_hi_made.sem, act_hi_made.next())
                tt(act_lo[:, s, :, :], src[:, 2 * j:2 * j + 2, :], f32(act_hi[:, s, :, :]), ALU.subtract).then_inc(hid_ready.sem, hid_ready.plus())

            def downs(n, src):
                s = slot[0]
                for j in range(min(RING, n)):
                    feed(src, j, (s + j) % RING)
                for j in range(n - 1):
                    dve.wait_ge(su_done.sem, su_done.next())
                    if j + RING < n:
                        feed(src, j + RING, (s + j) % RING)
                    split_next()

            def ffn(conv=None):
                down_slot, last_slot = (slot[0] + 4) % RING, (slot[0] + 2) % RING

                def taps(w, tile):
                    dve.wait_ge(conv_base.sem, conv_base.next())
                    for d in (1, 2):
                        for a in range(2):
                            o = f_out[:, w, a, d:T]
                            ins = stt(o, f_in[:, w, a, 0:T - d],
                                      vcol("ffn_conv_w", conv * 6 * FT + (2 - d) * 2 * FT + a + tile), o,
                                      ALU.mult, ALU.add)
                            if d == 1:
                                ins.then_inc(step.sem, step.plus())
                        if d == 1:
                            dve.wait_ge(step.sem, step.value())
                    return ins

                def gate(j):
                    dve.wait_ge(su_done.sem, su_done.next())
                    evacuate(f_in[:, 0, :, :], slot[0])
                    if conv is not None:
                        taps(0, j * 2).then_inc(gate_ready.sem, gate_ready.plus())
                    split_next()

                def up(j):
                    dve.wait_ge(su_done.sem, su_done.next())
                    evacuate(f_in[:, 1, :, :], slot[0])
                    if conv is None:
                        dve.wait_ge(evacuated.sem, evacuated.value())
                    else:
                        taps(1, j * 2 + FT).then_inc(step.sem, step.plus())
                        dve.wait_ge(step.sem, step.value())
                    dve.wait_ge(gate_act.sem, gate_act.next())
                    u = f_in if conv is None else f_out
                    tt(hidden, f_out[:, 0, :, :], u[:, 1, :, :], ALU.mult).then_inc(hidden_ready.sem, hidden_ready.plus())
                    split_next()

                def give(s):
                    dve.wait_ge(act_hi_made.sem, act_hi_made.next())
                    tt(act_lo[:, s, :, :], hidden, f32(act_hi[:, s, :, :]), ALU.subtract).then_inc(hid_ready.sem, hid_ready.plus())

                gate(0)
                up(0)
                give(down_slot)
                extra = dict(evacuated=2, gate_act=1, hidden_ready=1, act_hi_made=1, hid_ready=1)
                if conv is not None:
                    extra.update(conv_base=2, gate_ready=1, vec_step=5)

                def trip(j, s):
                    gate(j + 1)
                    up(j + 1)
                    dve.wait_ge(su_done.sem, su_done.next())
                    give(s)
                    split_next()

                u0 = unit[0]
                with c.repeat(FU - 2, per_trip(**extra)) as i:
                    trip(i, down_slot)
                unit[0] = u0 + 3 * (FU - 2)
                trip(FU - 2, last_slot)

            def copy_values(dst, b0):
                for i, d in enumerate(dst):
                    dve.wait_ge(turned.sem, turned.next())
                    v.tensor_copy(d, ps[:, b0 + i, :]).then_inc(bank_free.sem, bank_free.plus())

            def softplus(negate, bias, n):
                dve.wait_ge(small_done.sem, small_done.next())
                v.tensor_copy(cols[:, 8:10], ps[:, STAT, T + 64:T + 66]).then_inc(step.sem, step.plus())
                dve.wait_ge(step.sem, step.value())
                for a in range(TH):
                    stt(sp[0][:, a, 0:n], ps[:, STAT, T + 32 * a:T + 32 * a + n], cols[:, 8 + a:9 + a],
                                  bias, ALU.mult, ALU.add).then_inc(step.sem, step.plus())
                dve.wait_ge(step.sem, step.value())
                ts(sp[0][:, :, 0:n], sp[0][:, :, 0:n], -1.0 if negate else 1.0, None, ALU.mult).then_inc(sp_in.sem, sp_in.plus())
                dve.wait_ge(sp_exp.sem, sp_exp.next())
                ts(sp[3], sp[2], 1.0, None, ALU.add).then_inc(sp_one.sem, sp_one.plus())
                dve.wait_ge(sp_one.sem, sp_one.value())
                ts(sp[5], sp[3], -1.0, None, ALU.add).then_inc(step.sem, step.plus())
                dve.wait_ge(step.sem, step.value())
                ts(sp[6], sp[5], 0.0, None, ALU.is_equal).then_inc(step.sem, step.plus())
                dve.wait_ge(step.sem, step.value())
                tt(sp[5], sp[5], sp[6], ALU.add).then_inc(step.sem, step.plus())
                dve.wait_ge(step.sem, step.value())
                v.reciprocal(sp[5], sp[5]).then_inc(step.sem, step.plus())
                dve.wait_ge(step.sem, step.value())
                dve.wait_ge(sp_ln.sem, sp_ln.next())
                tt(sp[6], sp[4], sp[6], ALU.add).then_inc(step.sem, step.plus())
                dve.wait_ge(step.sem, step.value())
                tt(sp[6], sp[6], sp[5], ALU.mult).then_inc(step.sem, step.plus())
                dve.wait_ge(step.sem, step.value())
                tt(sp[6], sp[6], sp[2], ALU.mult).then_inc(step.sem, step.plus())
                dve.wait_ge(step.sem, step.value())
                dve.wait_ge(sp_in.sem, sp_in.value())
                ts(sp[7], sp[0], 0.0, None, ALU.max).then_inc(step.sem, step.plus())
                dve.wait_ge(step.sem, step.value())
                tt(sp[7], sp[7], sp[6], ALU.add).then_inc(step.sem, step.plus())
                dve.wait_ge(step.sem, step.value())

            def small_weights(n):
                dve.wait_ge(small_hi_made.sem, small_hi_made.next())
                tt(small_lo[:, :, 0:n], small_raw[:, :, 0:n], f32(small_hi[:, :, 0:n]),
                                         ALU.subtract).then_inc(small_ready.sem, small_ready.plus())

            def softmax_attention(kind):
                n_heads, _, _, scale = attention(kind)

                def shift(n):
                    h, a, i = n // 2, n % 2, n % 2
                    nk = keys_of(kind, a)
                    t, s = tiny[i], s_buf[i]
                    if kind == "diff":
                        dve.wait_ge(scored.sem, scored.next())
                        mask = chunk_mask[:, T - nk:T]
                        stt(s[:, :, 0:nk], ps[:, 2 * i:2 * i + 2, 0:nk], scale, rows(mask, 2),
                                  ALU.mult, ALU.add).then_inc(step.sem, step.plus())
                        dve.wait_ge(step.sem, step.value())
                        v.tensor_reduce(t[:, 0, :], s[:, :, 0:nk], AX_X, ALU.max).then_inc(step.sem, step.plus())
                        dve.wait_ge(step.sem, step.value())
                        ts(t[:, 1, :], t[:, 0, :], -1.0, None, ALU.mult).then_inc(shifted.sem, shifted.plus())
                        return
                    if kind == "fox":
                        if a == 0:
                            dve.wait_ge(scored.sem, scored.next())
                            tt(key_row[0], causal_mask[:, P:T], ps[:, 1, 0:P], ALU.subtract).then_inc(step.sem, step.plus())
                            tt(key_row[1], causal_mask[:], ps[:, 1, 0:T], ALU.subtract).then_inc(step.sem, step.plus())
                            dve.wait_ge(step.sem, step.value())
                        else:
                            scored.n += 1
                        dve.wait_ge(biased.sem, biased.next())
                        tt(s[:, 0, 0:nk], s[:, 0, 0:nk], key_row[a], ALU.add).then_inc(step.sem, step.plus())
                        dve.wait_ge(step.sem, step.value())
                        v.tensor_reduce(t[:, 0, 0:1], s[:, 0, 0:nk], AX_X, ALU.max).then_inc(step.sem, step.plus())
                        dve.wait_ge(step.sem, step.value())
                        ts(t[:, 1, 0:1], t[:, 0, 0:1], -1.0, None, ALU.mult).then_inc(shifted.sem, shifted.plus())
                        return
                    dve.wait_ge(scored.sem, scored.next())
                    v.tensor_reduce(t[:, 0, 0:1], ps[:, 2 * i, 0:nk], AX_X, ALU.max).then_inc(step.sem, step.plus())
                    dve.wait_ge(step.sem, step.value())
                    ts(t[:, 1, 0:1], t[:, 0, 0:1], -scale, None, ALU.mult).then_inc(shifted.sem, shifted.plus())

                def normalise(n):
                    i = n % 2
                    nk = keys_of(kind, i)
                    t, p, o = tiny[i], p_buf[i], probs[i][:, 0:nk]
                    m = 2 if kind == "diff" else 1
                    dve.wait_ge(exps_done.sem, exps_done.next())
                    v.reciprocal(t[:, 3, 0:m], t[:, 2, 0:m]).then_inc(step.sem, step.plus())
                    dve.wait_ge(step.sem, step.value())
                    if probs_old.due():
                        dve.wait_ge(probs_old.sem, probs_old.value())
                    if kind != "diff":
                        ts(o, p[:, 0, 0:nk], t[:, 3, 0:1], None, ALU.mult).then_inc(probs_ready.sem, probs_ready.plus())
                        return
                    tt(t[:, 4, 0:1], t[:, 3, 1:2], lam_col, ALU.mult).then_inc(step.sem, step.plus())
                    ts(o, p[:, 0, 0:nk], t[:, 3, 0:1], None, ALU.mult).then_inc(step.sem, step.plus())
                    dve.wait_ge(step.sem, step.value())
                    stt(o, p[:, 1, 0:nk], t[:, 4, 0:1], o, ALU.mult, ALU.add).then_inc(probs_ready.sem, probs_ready.plus())

                shift(0)
                for n in range(2 * n_heads):
                    if n + 1 < 2 * n_heads:
                        shift(n + 1)
                    normalise(n)

            def take_input(b):
                dve.wait_ge(turned.sem, turned.next())
                v.tensor_copy(x[:, 2 * b:2 * b + 2, :], bank(b)).then_inc(x_ready.sem, x_ready.plus())

            dve.wait_ge(turned.sem, turned.next(4))
            dve.wait_ge(turned.sem, turned.next(1))
            v.tensor_copy(vec[:, 0:512], ps[:, 4, :]).then_inc(setup_read.sem, setup_read.plus())
            dve.wait_ge(turned.sem, turned.next(1))
            v.tensor_copy(vec[:, 512:VBLOCKS * P], ps[:, 5, 0:(VBLOCKS - 4) * P]).then_inc(setup_read.sem, setup_read.plus())
            dve.wait_ge(freq_done.sem, freq_done.next())
            dve.wait_ge(pool_made.sem, pool_made.next(POOL_MADE))
            v.tensor_copy(freq_col, ps[:, 6, 0:1]).then_inc(setup_read.sem, setup_read.plus())
            dve.wait_ge(setup_read.sem, setup_read.value())
            for b in range(4):
                v.tensor_copy(x[:, 2 * b:2 * b + 2, :], bank(b)).then_inc(x_ready.sem, x_ready.plus())
            for s in range(RING):
                split(s)

            norm("mem_norm_2", 0, split=False)
            for j in range(8):
                dve.wait_ge(su_done.sem, su_done.next())
                l, i = j // 4, j % 4
                evacuate(mem_k[:, l, 2 * i:2 * i + 2, :] if i < 2
                         else proj[:, 16 + 4 * l + 2 * i - 4:16 + 4 * l + 2 * i - 2, :], slot[0])
                split_next()
            copy_values([mem_v[:, l, a, :] for l in range(2) for a in range(TH)], 0)
            norm("norm_mix_g", 0, take_input, split=False)
            dve.wait_ge(extras.sem, extras.next(EXTRAS))
            ang, turns = scr(5632, T), scr(5888, T)
            v.tensor_copy(ang, scr(6400, T).bitcast(I32)).then_inc(step.sem, step.plus())
            dve.wait_ge(step.sem, step.value())
            ts(ang, ang, freq_col, None, ALU.mult).then_inc(step.sem, step.plus())
            dve.wait_ge(step.sem, step.value())
            ts(turns, ang, 1.0 / (2 * math.pi), ROUND, ALU.mult, ALU.add).then_inc(step.sem, step.plus())
            dve.wait_ge(step.sem, step.value())
            ts(turns, turns, -ROUND, None, ALU.add).then_inc(step.sem, step.plus())
            dve.wait_ge(step.sem, step.value())
            stt(ang, turns, -TWO_PI_HI, ang, ALU.mult, ALU.add).then_inc(step.sem, step.plus())
            dve.wait_ge(step.sem, step.value())
            stt(ang, turns, -TWO_PI_LO, ang, ALU.mult, ALU.add).then_inc(step.sem, step.plus())
            dve.wait_ge(step.sem, step.value())
            ts(ang, ang, 3.1415925, -3.1415925, ALU.min, ALU.max).then_inc(trig_in.sem, trig_in.plus())
            lam = scr(6656, 4, 64)
            for i in range(2):
                tt(lam[:, 2 * i, :], lam[:, 2 * i, :], lam[:, 2 * i + 1, :], ALU.mult).then_inc(step.sem, step.plus())
                dve.wait_ge(step.sem, step.value())
                v.tensor_reduce(cols[:, 6 + i:7 + i], lam[:, 2 * i, :], AX_X, ALU.add).then_inc(lam_in.sem, lam_in.plus())
            dve.wait_ge(half_sin.sem, half_sin.next())
            tt(cos[:], cos[:], cos[:], ALU.mult).then_inc(step.sem, step.plus())
            dve.wait_ge(step.sem, step.value())
            ts(cos[:], cos[:], -2.0, 1.0, ALU.mult, ALU.add).then_inc(step.sem, step.plus())
            dve.wait_ge(lam_exp.sem, lam_exp.next())
            tt(lam_col, cols[:, 5:6], cols[:, 4:5], ALU.subtract).then_inc(step.sem, step.plus())
            dve.wait_ge(step.sem, step.value())
            ts(lam_col, lam_col, -LAMBDA_INIT, None, ALU.add).then_inc(step.sem, step.plus())
            ts(subln_col, vcol("attn_subln_g", 0), 1.0 - LAMBDA_INIT, None, ALU.mult).then_inc(step.sem, step.plus())
            d_skip = heads[:, 2, :].rearrange("p (t q) -> p t q", q=2)
            for q in range(2):
                rng = slice(64 * q, 64 * q + 64)
                v.tensor_copy(heads[rng, 3, 0:16], d_skip[rng, :, q]).then_inc(step.sem, step.plus())

            def conv_xbc(j, s):
                evacuate(conv_in[s], s)
                dve.wait_ge(conv_base.sem, conv_base.next())
                for d in (1, 2, 3):
                    for a in range(2):
                        o = conv_out[s][:, a, d:T]
                        ins = stt(o, conv_in[s][:, a, 0:T - d],
                                  vcol("ssd_conv_w", j * 2 + ((3 - d) * SSD_XBC // P + a)), o, ALU.mult, ALU.add)
                        if d < 3:
                            ins.then_inc(step.sem, step.plus())
                    if d < 3:
                        dve.wait_ge(step.sem, step.value())
                ins.then_inc(conv_done.sem, conv_done.plus())

            units(8, to_proj(0), evacuated=1)
            units(12, conv_xbc, evacuated=1, conv_base=1, conv_done=1, vec_step=4)
            small_weights(SSD_HEADS)
            softplus(False, heads[:, 0, :], SSD_HEADS)
            v.tensor_copy(dt_tok.rearrange("p (a n) -> p a n", a=TH), sp[7]).then_inc(small_free.sem, small_free.plus())
            dve.wait_ge(small_free.sem, small_free.value())
            dve.wait_ge(decay_rate.sem, decay_rate.next())
            stt(dA.rearrange("p (a n) -> p a n", a=TH), sp[7], -1.0, rows(heads[:, 1, :], TH),
                                   ALU.mult, ALU.mult).then_inc(dA_ready.sem, dA_ready.plus())
            dve.wait_ge(cumsum_done.sem, cumsum_done.next())
            v.tensor_copy(a_cs, ps[:, STAT, 0:64]).then_inc(step.sem, step.plus())
            dve.wait_ge(step.sem, step.value())
            tt(dec, ps[:, STAT, 64:96], a_cs[:, 0:32], ALU.subtract).then_inc(decay_in.sem, decay_in.plus())
            dve.wait_ge(turned.sem, turned.next())
            v.tensor_copy(flat(b_tok), ps[:, 6, :]).then_inc(bank_free.sem, bank_free.plus())
            dve.wait_ge(decay_done.sem, decay_done.next())
            tt(dt_dec, dt_tok[:, 0:32], dec, ALU.mult).then_inc(step.sem, step.plus())
            dve.wait_ge(step.sem, step.value())
            dve.wait_ge(cb_done.sem, cb_done.next())
            for a in range(TH):
                tt(cb[:, :, a, :], bank(4 + a, 4), rows(upper[:], 4), ALU.mult).then_inc(step.sem, step.plus())
            dve.wait_ge(in_ready.sem, in_ready.next(20))
            dve.wait_ge(step.sem, step.value())

            def x_times_dt(g):
                hs = slice(8 * g, 8 * g + 8)
                dve.wait_ge(turned.sem, turned.next())
                b0 = ps[:, 0, :].rearrange("p (h d) -> p h d", h=8)
                b1 = ps[:, 1, :].rearrange("p (h d) -> p h d", h=8)
                tt(x_dt[g % 2][0], b0, each(dt_tok[:, hs], 64), ALU.mult).then_inc(step.sem, step.plus())
                tt(x_dec[g % 2], b0, each(dt_dec[:, hs], 64), ALU.mult).then_inc(step.sem, step.plus())
                dve.wait_ge(turned.sem, turned.next())
                tt(x_dt[g % 2][1], b1, each(dt_tok[:, 32 + 8 * g:40 + 8 * g], 64), ALU.mult).then_inc(x_dt_ready.sem, x_dt_ready.plus())


            def segments(h):
                dve.wait_ge(rows_done.sem, rows_done.next())
                if y_old.due():
                    dve.wait_ge(y_old.sem, y_old.value())
                for a in range(TH):
                    ins = ts(seg[h % 3][:, a * P:(a + 1) * P], ps[:, 2 + h % 2, a * P:(a + 1) * P],
                             a_cs[:, 32 * a + h:32 * a + h + 1], 0.0, ALU.subtract, ALU.min)
                    if a:
                        ins.then_inc(seg_ready.sem, seg_ready.plus())

            def mask(h):
                g = h // 8
                dve.wait_ge(decay_ready.sem, decay_ready.next())
                m = seg[h % 3].rearrange("p (a t) -> p a t", a=TH)
                tt(m, m, cb[:, g, :, :], ALU.mult).then_inc(step.sem, step.plus())
                dve.wait_ge(row_exp.sem, row_exp.next())
                tt(row_e[h % 3], row_e[h % 3], proj[:, 36 + g, P:T], ALU.mult).then_inc(mask_ready.sem, mask_ready.plus())

            def pair(p):
                dve.wait_ge(y_done.sem, y_done.next(2))
                t = proj[:, 16 + p, :]
                stt(t, t, heads[:, 3, p:p + 1], ps[:, 4 + p % 2, 0:T], ALU.mult, ALU.add).then_inc(y_read.sem, y_read.plus())
                dve.wait_ge(y_read.sem, y_read.value())
                ins = tt(t, t, proj[:, p, :], ALU.mult)
                if p == SSD_HEADS // 2 - 1:
                    ins.then_inc(gated.sem, gated.plus())
                else:
                    ins.then_inc(step.sem, step.plus())

            x_times_dt(0)
            segments(0)
            for h in range(SSD_HEADS):
                if h + 1 < SSD_HEADS:
                    segments(h + 1)
                if h % 8 == 5 and h // 8 + 1 < SSD_GROUPS:
                    x_times_dt(h // 8 + 1)
                mask(h)
                if h % 2 and h >= 3:
                    pair((h - 3) // 2)
            pair(15)
            dve.wait_ge(group_rstd.sem, group_rstd.next())
            for t in range(16):
                ins = stt(proj[:, 16 + t, :], proj[:, 16 + t, :], vcol("ssd_norm_g", t),
                          scr(2048, 4, T)[:, t // 4, :], ALU.mult, ALU.mult)
            ins.then_inc(source_ready.sem, source_ready.plus())
            downs(8, proj[:, 16:32, :])
            norm("norm_ffn_g", 0, residual())
            ffn(conv=0)

            norm("norm_mix_g", DK, residual())
            units(12, to_proj(0), evacuated=1)
            dve.wait_ge(evacuated.sem, evacuated.value())
            for j in range(8):
                t = proj[:, 2 * j:2 * j + 2, :]
                dve.wait_ge(qk_rstd.sem, qk_rstd.next())
                stt(t, t, vcol("attn_q_norm_g" if j < 4 else "attn_k_norm_g", 0),
                                        qk_rn[j % 2], ALU.mult, ALU.mult).then_inc(qk_normed.sem, qk_normed.plus())
                dve.wait_ge(qk_normed.sem, qk_normed.value())
                tt(qk_a, t, rows(cos[:], 2), ALU.mult).then_inc(step.sem, step.plus())
                dve.wait_ge(qk_swapped.sem, qk_swapped.next())
                tt(qk_b, bank(2 + j % 2), rows(sin[:], 2), ALU.mult).then_inc(step.sem, step.plus())
                dve.wait_ge(step.sem, step.value())
                tt(t, qk_a, qk_b, ALU.add).then_inc(qk_rotated.sem, qk_rotated.plus())
            copy_values([v_tok[:, a, 512 * b:512 * b + 512] for a in range(TH) for b in range(2)], 4)
            softmax_attention("diff")
            dve.wait_ge(o_rstd.sem, o_rstd.next())
            o = proj[:, 24:32, :]
            stt(o, o, subln_col, wide_b, ALU.mult, ALU.mult).then_inc(source_ready.sem, source_ready.plus())
            downs(4, proj[:, 24:32, :])
            norm("norm_ffn_g", DK, residual())
            ffn(conv=1)
            norm("ffn_norm_2", 0, residual())
            ffn()

            norm("mix_norm_2", 0, residual(0.5))
            units(14, to_proj(0), evacuated=1)
            dve.wait_ge(evacuated.sem, evacuated.value())
            cu = proj[:, 8:16, :]
            tt(cu, cu, proj[:, 16:24, :], ALU.mult).then_inc(gated_input.sem, gated_input.plus())
            dve.wait_ge(conv_base.sem, conv_base.next())
            for d in (1, 2):
                for k in range(DK):
                    o = proj[:, 28 + k, d:T]
                    stt(o, proj[:, 8 + k, 0:T - d], vcol("a_conv_w_2", (2 - d) * DK + k), o,
                                  ALU.mult, ALU.add).then_inc(step.sem, step.plus())
                dve.wait_ge(step.sem, step.value())
            o = proj[:, 28:36, :]
            tt(o, o, proj[:, 0:8, :], ALU.mult).then_inc(source_ready.sem, source_ready.plus())
            softmax_attention("mem0")
            out_read.n = 12
            dve.wait_ge(out_read.sem, out_read.value())
            downs(6, proj[:, 28:40, :])
            norm("ffn_norm_2", DK, residual())
            ffn()

            norm("kv_norm_2", 0, residual(0.5))
            units(8, to_proj(0), evacuated=1)
            small_weights(FOX_HEADS)
            softplus(True, gate_bias, FOX_HEADS)
            ts(log_f, sp[7][:, :, 0:FOX_HEADS], -1.0, None, ALU.mult).then_inc(log_f_ready.sem, log_f_ready.plus())
            dve.wait_ge(cum_f_done.sem, cum_f_done.next())
            v.tensor_copy(cum_f, ps[:, STAT, 0:16].rearrange("p (a h) -> p a h", a=TH)).then_inc(kv_done.sem, kv_done.plus())
            norm("ffn_norm_2", 2 * DK, stats=False, split=False)
            ffn()

            norm("mix_norm_2", DK, residual(0.5))
            units(6, to_proj(16), evacuated=1)
            copy_values([v_tok[:, a, 512 * b:512 * b + 512] for a in range(TH) for b in range(2)], 4)
            softmax_attention("fox")
            softmax_attention("mem1")
            out_read.n = 24
            dve.wait_ge(out_read.sem, out_read.value())
            downs(6, proj[:, 28:40, :])
            norm("ffn_norm_2", 3 * DK, residual())
            ffn()

            norm(None, 0, residual(0.5))
            for k in range(DK):
                ins = stt(squares[:, k, :], x[:, k, :], vcol("final_norm_2", k), rstd[:], ALU.mult, ALU.mult)
            ins.then_inc(final_normed.sem, final_normed.plus())
            for a in range(TH):
                for b in range(2):
                    dve.wait_ge(turned.sem, turned.next())
                    v.tensor_copy(out_tok[:, a, 512 * b:512 * b + 512], ps[:, 2 * a + b, :]).then_inc(final_ready.sem, final_ready.plus())


def kernel(**inputs):
    import concourse.bacc as _bacc
    from concourse import mybir as _mybir
    from concourse.bass_utils import run_bass_kernel_spmd as _run

    nc = _bacc.Bacc("TRN2", target_bir_lowering=False, num_devices=1)
    arrays, args = {}, {}
    for name, value in inputs.items():
        a = np.ascontiguousarray(value)
        arrays[f"in_{name}_dram"] = a
        args[name] = nc.dram_tensor(f"in_{name}_dram", a.shape, _mybir.dt.from_np(a.dtype),
                                    kind="ExternalInput").ap()
    out = nc.dram_tensor("out_0_dram", (1, T, D), F32, kind="ExternalOutput").ap()
    build_program(nc, args, out)
    r = _run(nc, [arrays], core_ids=[0])
    return r.results[0]["out_0_dram"]
```

```python
import math
from contextlib import ExitStack, contextmanager

import numpy as np

import concourse.bass as bass
from concourse import mybir

F32 = mybir.dt.float32
F32R = mybir.dt.float32r
I32 = mybir.dt.int32
ACT = mybir.ActivationFunctionType
ALU = mybir.AluOpType
AX_X = mybir.AxisListType.X

P = 128
T = 256
TH = T // P
D = 1024
DK = D // P
EPS = 1e-6
RING = 3

Z_WOVEN = 6
KV_ROPE, KV_WOVEN = 2, 2
A_WOVEN = 4
B_WOVEN = 3
MIXED_ORDER = (4, 5, 0, 1, 2, 3)

SSD_INNER, SSD_GROUPS, SSD_STATE, SSD_HEADS, SSD_HD, SSD_TAPS = 2048, 4, 128, 32, 64, 4
SSD_PAIRS = SSD_HEADS // 2
SSD_XBC = SSD_INNER + 2 * SSD_GROUPS * SSD_STATE
FF = 2816
FT = FF // P
FU = FT // 2
ATT_HEADS, ATT_HD = 8, 64
ROPE_HALF, THETA = 8, 500000.0
LAMBDA_INIT = 0.8 - 0.6 * math.exp(-0.3)
MEM_HEADS, FOX_HEADS = 4, 8
MASKED = -3.0e38
TWO_PI_HI = 6.28125
TWO_PI_LO = 2 * math.pi - 6.28125
ROUND = 1.5 * 2.0 ** 23


class Tally:

    def __init__(self, sem, start, step):
        self.sem, self.n, self.step, self.loop, self.per = sem, start, step, None, 0

    def value(self, ahead=0):
        v = (self.n + ahead) * self.step
        return v if self.loop is None else v + self.loop * (self.per * self.step)

    def plus(self):
        self.n += 1
        return self.step

    def next(self, n=1):
        self.n += n
        return self.value()

    def due(self, n=1):
        self.n += n
        return self.loop is not None or self.n > 0


class Counts:

    def __init__(self, eng, sem):
        self.eng, self.sem, self.all = eng, sem, {}

    def __call__(self, name, start=0, step=1):
        t = self.all.get((name, start))
        if t is None:
            t = self.all[(name, start)] = Tally(self.sem(name), start, step)
        return t

    @contextmanager
    def repeat(self, trips, counts):
        starts = {t: t.n for t in self.all.values()}
        with self.eng.Fori(0, trips) as i:
            for t, per in counts.items():
                t.loop, t.per = i, per
            yield i
        for t, n in starts.items():
            per = counts.get(t, 0)
            assert t.n - n == per, (str(t.sem), t.n - n, per)
            t.n = n + per * trips
            t.loop = None


VECTOR_ROWS = [
    ("norm_mix_g", 2 * DK), ("norm_ffn_g", 2 * DK), ("ffn_norm_2", 4 * DK), ("mix_norm_2", 2 * DK),
    ("mem_norm_2", DK), ("kv_norm_2", DK), ("final_norm_2", DK), ("ssd_norm_g", SSD_INNER // P),
    ("ssd_conv_w", SSD_TAPS * SSD_XBC // P), ("ssd_conv_b", SSD_XBC // P),
    ("ffn_conv_w", 2 * 3 * 2 * FT), ("ffn_conv_b", 2 * 2 * FT), ("a_conv_w_2", 3 * DK),
    ("attn_subln_g", 1), ("attn_q_norm_g", 1), ("attn_k_norm_g", 1),
]
VECTOR_ROWS.append(("pad", -sum(n for _, n in VECTOR_ROWS) % P))
COL = {}
_n = 0
for _name, _rows in VECTOR_ROWS:
    COL[_name] = _n
    _n += _rows
VECTORS = _n
VBLOCKS = -(-VECTORS // P)

STREAM = [
    ("up", "ssd_in_w", (0,), 8, 12), ("up", "ssd_in_w", (0,), 0, 8),
    ("down", "ssd_out_w", (0,), 0, 8),
    ("ffn", ("ffn_up_w", "ffn_down_w"), (0,), 0, 3 * FU),
    ("up", "attn_in_w", (0,), 0, 12),
    ("up", "mem_w_kv_2", (0,), 0, 4), ("up", "mem_w_kv_2", (1,), 0, 4),
    ("down", "attn_out_w", (0,), 0, 4),
    ("ffn", ("ffn_up_w", "ffn_down_w"), (1,), 0, 3 * FU),
    ("ffn", ("ffn_w_gate_up_2", "ffn_w_down_2"), (0, 0), 0, 3 * FU),
    ("up", "a_w_in_2", (0,), 12, 2), ("up", "a_w_in_2", (0,), 4, 8),
    ("down", "a_w_out_2", (0,), 4, 2),
    ("up", "a_w_in_2", (0,), 0, 4), ("down", "a_w_out_2", (0,), 0, 4),
    ("ffn", ("ffn_w_gate_up_2", "ffn_w_down_2"), (0, 1), 0, 3 * FU),
    ("up", "w_kvf_2", (), 0, 8),
    ("ffn", ("ffn_w_gate_up_2", "ffn_w_down_2"), (1, 0), 0, 3 * FU),
    ("up", "b_w_q_2", (0,), 4, 2), ("up", "b_w_q_2", (0,), 0, 4),
    ("down", "b_w_out_2", (0,), 4, 2), ("down", "b_w_out_2", (0,), 0, 4),
    ("ffn", ("ffn_w_gate_up_2", "ffn_w_down_2"), (1, 1), 0, 3 * FU),
]
UNITS = sum(s[4] for s in STREAM)



POOL_MADE = 9 + 2 + ROPE_HALF + 3 + 1 + 4
EXTRAS = 9


def vector_loads():
    loads, row = [], 0
    for name, n in VECTOR_ROWS:
        at = 0
        while at < n:
            k = min(n - at, P - row % P)
            loads.append((name, at, k, row))
            at += k
            row += k
    return loads


LOADS = vector_loads()
HALVES = ("attn_q_norm_g", "attn_k_norm_g")
LOADED_FIRST = sum(row < P for _, _, _, row in LOADS)
LOADED_LATER = len(LOADS) - LOADED_FIRST + len(HALVES)


def build_program(nc, A, out):
    with ExitStack() as ctx:
        def sb(name, shape, dt=F32):
            return ctx.enter_context(nc.sbuf_tensor(name, shape, dt))

        sems = {}

        def sem(name):
            if name not in sems:
                sems[name] = ctx.enter_context(nc.semaphore(name))
            return sems[name]

        raw = sb("raw_weights", [P, RING, 2048])
        w_hi = sb("weights_hi", [P, RING, 2048], F32R)
        w_lo = sb("weights_lo", [P, RING, 2048], F32R)
        act_hi = sb("down_in_hi", [P, RING, 2, T], F32R)
        act_lo = sb("down_in_lo", [P, RING, 2, T], F32R)
        x = sb("residual", [P, DK, T])
        h_hi = sb("normed_hi", [P, DK, T], F32R)
        h_lo = sb("normed_lo", [P, DK, T], F32R)
        proj = sb("proj", [P, 40, T])
        mem_k = sb("mem_k", [P, 2, MEM_HEADS, T])
        mem_v = sb("mem_v", [P, 2, TH, MEM_HEADS * P])
        vec = sb("vectors", [P, VBLOCKS * P])
        rstd = sb("rstd", [P, T])
        small_raw = sb("small_w_raw", [P, DK, 32])
        small_hi = sb("small_w_hi", [P, DK, 32], F32R)
        small_lo = sb("small_w_lo", [P, DK, 32], F32R)
        ident = sb("ident", [P, P])
        ones = sb("ones", [P, P])
        upper = sb("upper", [P, P])
        half_ones = sb("half_ones", [P, P])
        swap = sb("rope_swap", [P, P])
        chunk_mask = sb("chunk_mask", [P, T])
        causal_mask = sb("causal_mask", [P, T])
        cos = sb("cos", [P, T])
        sin = sb("sin", [P, T])
        cols = sb("columns", [P, 64])
        eps_col, lam_col, subln_col, freq_col = (cols[:, i:i + 1] for i in range(4))
        log_f = cols[:, 16:32].rearrange("p (a h) -> p a h", a=TH)
        cum_f = cols[:, 32:48].rearrange("p (a h) -> p a h", a=TH)
        gate_bias = cols[:, 48:56]
        heads = sb("head_rows", [P, 4, 32])
        S = sb("scratch", [P, 7168])

        def scr(at, *shape):
            n = int(np.prod(shape))
            assert at + n <= 7168
            v = S[:, at:at + n]
            if len(shape) == 1:
                return v
            names = "abc"[:len(shape)]
            return v.rearrange("p (" + " ".join(names) + ") -> p " + " ".join(names),
                               **{names[i]: shape[i] for i in range(1, len(shape))})

        ps = ctx.enter_context(nc.psum_tensor("ps", [P, 8, 512], F32))
        STAT = 7

        mem_squares, mem_partial = proj[:, 24:32, :], proj[:, 32, :]

        squares = scr(0, DK, T)
        partial = scr(2048, T)
        f_in = scr(2304, 2, 2, T)
        f_out = scr(3328, 2, 2, T)
        hidden = scr(4352, 2, T)
        conv_in = [scr(2304 + 512 * s, 2, T) for s in range(RING)]
        conv_out = [scr(3840 + 512 * s, 2, T) for s in range(RING)]
        freq_row = scr(7040, P)[0:1, :]
        mem_flat = mem_v[:].rearrange("p l a n -> p (l a n)")
        mem_raw = mem_k[:].rearrange("p l h t -> p (l h) t")
        x_dt = [[scr(1024 * g + 512 * a, 8, 64) for a in range(TH)] for g in range(2)]
        state = [scr(2048 + 512 * g, 512) for g in range(2)]
        cb = scr(3072, 4, TH, P)
        b_tok = scr(4096, 4, P)
        x_dec = [scr(4608 + 512 * g, 8, 64) for g in range(2)]
        seg = [mem_flat[:, 512 * i:512 * i + 512].rearrange("p (q n) -> p q n", q=2) for i in range(3)]
        row_e = [scr(5632 + 256 * i, 2, P) for i in range(3)]
        group_rs = scr(0, SSD_GROUPS, T)
        dt_tok, dA, a_cs = scr(6784, 64), scr(6848, 64), scr(6912, 64)
        dt_dec, dec = scr(6976, 32), scr(7008, 32)
        small_sum = scr(6144, T)
        sp = [scr(5632 + 64 * i, TH, 32) for i in range(8)]
        v_tok = scr(0, TH, 1024)
        s_buf = [scr(2048 + 512 * i, 2, T) for i in range(2)]
        p_buf = [scr(3072 + 512 * i, 2, T) for i in range(2)]
        probs = [scr(4096 + 256 * i, T) for i in range(2)]
        probs_t = [scr(4608 + 256 * i, T) for i in range(2)]
        tiny = [scr(5120 + 16 * i, 8, 2) for i in range(2)]
        key_row = [scr(5248, P), scr(5376, T)]
        qk_sq = [scr(0, 8, T), scr(4096, 8, T)]
        qk_rn = [scr(2048, 8, T), scr(4096, 8, T)]
        qk_a, qk_b = scr(6144, 2, T), scr(6656, 2, T)
        wide_a, wide_b = scr(0, 8, T), scr(2048, 8, T)
        out_tok = scr(2304, TH, D)
        gained = proj[:, 0:DK, :]

        OUT = out.rearrange("b (a p) n -> p (b a) n", p=P)

        def rows(ap, n):
            return ap.unsqueeze(1).broadcast_to([P, n, ap.shape[-1]])

        def each(ap, n):
            return ap.unsqueeze(2).broadcast_to([P, ap.shape[-1], n])

        def flat(ap):
            return ap.rearrange("p k t -> p (k t)")

        def bank(b, n=2):
            return ps[:, b, :].rearrange("p (k t) -> p k t", k=n)

        def arr(name, idx):
            a = A[name]
            for i in idx:
                a = a[i]
            return a

        def vcol(name, i):
            return vec[:, bass.ds(COL[name] + i, 1)]

        def attention(kind):
            return {"diff": (ATT_HEADS, 0, 24, ATT_HD ** -0.5), "fox": (FOX_HEADS, 16, 28, P ** -0.5),
                    "mem0": (MEM_HEADS, 24, 36, P ** -0.5), "mem1": (MEM_HEADS, 24, 36, P ** -0.5)}[kind]

        def keys_of(kind, a):
            return T if kind.startswith("mem") else P * (a + 1)

        group_squares = [proj[:, 4 * g:4 * g + 4, :] for g in range(SSD_GROUPS)]

        block = ctx.enter_context(nc.Block())

        @block.sync
        def _(sp_eng):
            sp = sp_eng
            c = Counts(sp, sem)
            final_ready = c("final_ready")
            lo_split = c("lo_split", -RING)
            stored = c("stored", step=16)
            x_staged = c("x_staged", step=16)
            first_staged = c("first_staged", step=16)
            staged = c("staged", step=16)
            mem_staged = c("mem_staged", step=16)
            extras = c("extras_staged", step=16)
            pool_made = c("pool_made")
            landed = [c(f"landed{s}", step=16) for s in range(RING)]
            u = 0

            def load(dst, src, slot):
                if lo_split.due():
                    sp.wait_ge(lo_split.sem, lo_split.value())
                sp.dma_start(dst, src).then_inc(landed[slot].sem, landed[slot].plus())

            def up(w, col, slot):
                load(raw[:, slot, :].rearrange("p (k n) -> p k n", k=DK),
                     w.rearrange("(k p) n -> p k n", p=P)[:, :, bass.ds(col, 256)], slot)

            def down(w, j, slot):
                load(raw[:, slot, :].rearrange("p (j k n) -> p j k n", j=1, k=2),
                     w.rearrange("(j k p) n -> p j k n", k=2, p=P)[:, bass.ds(j, 1), :, :], slot)


            vrows = flat(proj[:, 24:27, :])
            sp.dma_start(flat(proj[:, 0:8, :]).rearrange("p (a n) -> p a n", a=TH),
                          A["x"][0].rearrange("(a p) n -> p a n", p=P)).then_inc(x_staged.sem, x_staged.plus())

            def load_vector(name, at, k, row):
                landing = first_staged if row < P else staged
                dst = vrows[row % P:row % P + k, row // P * P:row // P * P + P]
                if name in HALVES:
                    for half in range(2):
                        sp.dma_start(dst[:, 64 * half:64 * half + 64],
                                      A[name]).then_inc(landing.sem, landing.plus())
                    return
                src = A["ffn_conv_b" if name == "pad" else name]
                while len(src.shape) > 1:
                    dims = " ".join(f"d{i}" for i in range(len(src.shape)))
                    src = src.rearrange(f"{dims} -> ({dims})")
                src = src.rearrange("(r q) -> r q", q=P)
                sp.dma_start(dst, src[at:at + k, :]).then_inc(landing.sem, landing.plus())

            for vector in LOADS[:LOADED_FIRST]:
                load_vector(*vector)

            def load_rest():
                for vector in LOADS[LOADED_FIRST:]:
                    load_vector(*vector)
                assert (first_staged.n, staged.n) == (LOADED_FIRST, LOADED_LATER)
                sp.dma_start(mem_flat.rearrange("p (a n) -> p a n", a=TH),
                              A["mem_2"][0].rearrange("(a p) n -> p a n", p=P)).then_inc(mem_staged.sem, mem_staged.plus())
                for i, name in enumerate(("ssd_dt_bias", "ssd_a_log", "ssd_d")):
                    sp.dma_start(heads[:, i, :], A[name].broadcast_to([P, SSD_HEADS])).then_inc(extras.sem, extras.plus())
                sp.dma_start(scr(6400, T).bitcast(I32), A["positions"].broadcast_to([P, T])).then_inc(extras.sem, extras.plus())
                for i, name in enumerate(("attn_lq1", "attn_lk1", "attn_lq2", "attn_lk2")):
                    sp.dma_start(scr(6656, 4, 64)[:, i, :], A[name].broadcast_to([P, ATT_HD])).then_inc(extras.sem, extras.plus())
                sp.wait_ge(pool_made.sem, pool_made.next(POOL_MADE))
                sp.dma_start(gate_bias, A["b_f_2"].unsqueeze(0).broadcast_to([P, FOX_HEADS])).then_inc(extras.sem, extras.plus())
                assert extras.n == EXTRAS
                sp.dma_start(small_raw[:], A["ssd_in_w"][0].rearrange("(k p) n -> p k n", p=P)
                              [:, :, SSD_INNER + SSD_XBC:]).then_inc(sem("small_landed"), 16)

            for kind, name, idx, first, n in STREAM:
                counts = {lo_split: RING, **{t: 1 for t in landed}}
                if kind == "ffn":
                    wu, wd = arr(name[0], idx), arr(name[1], idx)
                    up(wu, 0, u % RING)
                    up(wu, FF, (u + 1) % RING)
                    with c.repeat(FU - 1, counts) as i:
                        up(wu, i * 256 + 256, (u + 2) % RING)
                        up(wu, i * 256 + (256 + FF), u % RING)
                        down(wd, i, (u + 1) % RING)
                    down(wd, FU - 1, (u + 2) % RING)
                    u += 3 * FU
                    continue
                w = arr(name, idx)

                def load_unit(j, slot):
                    if kind == "up":
                        up(w, j * 256, slot)
                    else:
                        down(w, j, slot)

                peeled = max(RING - u, 0)
                trips = (n - peeled) // RING
                trips = trips if trips > 1 else 0
                for j in range(peeled):
                    load_unit(first + j, (u + j) % RING)
                if peeled:
                    load_rest()
                if trips:
                    with c.repeat(trips, counts) as i:
                        for j in range(RING):
                            load_unit(i * RING + (first + peeled + j), (u + peeled + j) % RING)
                for j in range(peeled + trips * RING, n):
                    load_unit(first + j, (u + j) % RING)
                u += n
            assert u == UNITS
            for a in range(TH):
                sp.wait_ge(final_ready.sem, final_ready.next(2))
                sp.dma_start(OUT[:, a, :], out_tok[:, a, :]).then_inc(stored.sem, stored.plus())
            sp.wait_ge(stored.sem, stored.value())

        @block.gpsimd
        def _(pool):
            g = nc.gpsimd
            made = Counts(pool, sem)("pool_made")

            def fill(view, value):
                pool.wait_ge(made.sem, made.value())
                g.memset(view, value).then_inc(made.sem, made.plus())

            for m, v in ((ident, 0.0), (ones, 1.0), (upper, 1.0), (half_ones, 0.0), (swap, 0.0),
                         (chunk_mask, 0.0), (causal_mask, 0.0), (cols, EPS)):
                fill(m[:], v)
            fill(freq_row, 0.0)
            for a in range(2):
                fill(half_ones[64 * a:64 * a + 64, 64 * a:64 * a + 64], 1.0)
            row = freq_row.rearrange("p (a b c j) -> p a b c j", a=2, b=4, c=2)[:, :, 0, :, :]
            for j in range(ROPE_HALF):
                fill(row[:, :, :, j], float(np.float32(THETA) ** np.float32(-2.0 * j / (2 * ROPE_HALF))))

            def select(view, pattern, base, mult, value, op=ALU.not_equal):
                pool.wait_ge(made.sem, made.value())
                g.affine_select(out=view, in_=view, compare_op=op, fill=value, base=base, pattern=pattern,
                                channel_multiplier=mult).then_inc(made.sem, made.plus())

            select(ident[:], [[-1, P]], 0, 1, 1.0)
            select(upper[:], [[1, P]], 0, -1, 0.0, ALU.is_ge)
            select(causal_mask[:, P:T], [[-1, P]], 0, 1, MASKED, ALU.is_ge)
            fill(chunk_mask[0:64, P + 64:T], MASKED)
            for b in (0, 64):
                select(swap[:, b:b + 8], [[-1, 8]], -(b + 8), 1, -1.0)
                select(swap[:, b + 8:b + 16], [[-1, 8]], -b, 1, 1.0)
            assert made.n == POOL_MADE

        @block.tensor
        def _(pe):
            mm = nc.tensor.matmul
            c = Counts(pe, sem)
            bank_free = c("bank_free")
            bank_summed = c("bank_summed")
            cb_read = c("cb_read")
            first_staged = c("first_staged", step=16)
            mem_staged = c("mem_staged", step=16)
            cb_done = c("cb_done")
            cum_f_done = c("cum_f_done")
            cum_f_read = c("cum_f_read")
            cumsum_done = c("cumsum_done")
            dA_ready = c("dA_ready")
            first_scored = c("first_scored")
            evacuated = c("evacuated", -2)
            freq_done = c("freq_done")
            group_sum = c("group_sum")
            h_ready = c("h_ready")
            hid_ready = c("hid_ready")
            in_ready = c("in_ready")
            lo_split = c("lo_split")
            log_f_ready = c("log_f_ready")
            mask_ready = c("mask_ready")
            o_squares = c("o_squares")
            o_summed = c("o_summed")
            out_done = c("out_done")
            out_read = c("out_read", -1)
            pool_made = c("pool_made")
            probs_copied = c("probs_copied")
            probs_ready = c("probs_ready")
            probs_turned = c("probs_turned")
            qk_normed = c("qk_normed")
            qk_logs = c("qk_logs")
            qk_rotated = c("qk_rotated", -4)
            qk_squares = c("qk_squares")
            qk_summed = c("qk_summed")
            qk_swapped = c("qk_swapped")
            rows_done = c("rows_done")
            scored = c("scored")
            setup_read = c("setup_read")
            small_done = c("small_done")
            small_normed = c("small_normed")
            small_turned = c("small_turned")
            final_x = c("final_x")
            small_ready = c("small_ready")
            staged = c("staged", step=16)
            stat_done = c("stat_done")
            state_done = c("state_done")
            state_ready = c("state_ready")
            su_done = c("su_done")
            sums_ready = c("sums_ready")
            turned = c("turned")
            x_dt_ready = c("x_dt_ready")
            x_staged = c("x_staged", step=16)
            y_done = c("y_done")
            y_read = c("y_read", -1)
            y_squares = c("y_squares")
            slot = [0]

            def up_unit(first=False, ks=range(DK)):
                s = slot[0]
                if ks[0] == 0:
                    pe.wait_ge(lo_split.sem, lo_split.next())
                    if evacuated.due():
                        pe.wait_ge(evacuated.sem, evacuated.value())
                wh = w_hi[:, s, :].rearrange("p (k n) -> p k n", k=DK)
                wl = w_lo[:, s, :].rearrange("p (k n) -> p k n", k=DK)
                for k in ks:
                    if first:
                        pe.wait_ge(h_ready.sem, h_ready.next())
                    for a in range(2):
                        o = ps[:, 4 + s, a * T:(a + 1) * T]
                        hi, lo = wh[:, k, a * P:(a + 1) * P], wl[:, k, a * P:(a + 1) * P]
                        mm(o, hi, h_hi[:, k, :], start=(k == 0 and a == 0), stop=False, skip_group_check=True)
                        mm(o, hi, h_lo[:, k, :], start=False, stop=False, skip_group_check=True)
                        last = mm(o, lo, h_hi[:, k, :], start=False, stop=(k == DK - 1), skip_group_check=True)
                if ks[-1] == DK - 1:
                    last.then_inc(su_done.sem, su_done.plus())
                    slot[0] = (s + 1) % RING

            def woven(n):
                def step(t):
                    if t < 2 * n:
                        up_unit(ks=range(t % 2 * DK // 2, (t % 2 + 1) * DK // 2))
                return step

            def down_unit(first=False, last=False):
                s = slot[0]
                pe.wait_ge(lo_split.sem, lo_split.next())
                pe.wait_ge(hid_ready.sem, hid_ready.next())
                wh = w_hi[:, s, :].rearrange("p (k n) -> p k n", k=2)
                wl = w_lo[:, s, :].rearrange("p (k n) -> p k n", k=2)
                for m in range(DK):
                    o = ps[:, m // 2, (m % 2) * T:(m % 2 + 1) * T]
                    for k in range(2):
                        hi, lo = wh[:, k, m * P:(m + 1) * P], wl[:, k, m * P:(m + 1) * P]
                        mm(o, hi, act_hi[:, s, k, :], start=(first and k == 0 and m % 2 == 0), stop=False,
                           skip_group_check=True)
                        mm(o, hi, act_lo[:, s, k, :], start=False, stop=False, skip_group_check=True)
                        ins = mm(o, lo, act_hi[:, s, k, :], start=False, stop=(k == 1), skip_group_check=True)
                    if last and m % 2:
                        ins.then_inc(bank_summed.sem, bank_summed.plus())
                if not last:
                    ins.then_inc(su_done.sem, su_done.plus())
                slot[0] = (s + 1) % RING

            def norm_sum(squares_sum=partial):
                pe.wait_ge(sums_ready.sem, sums_ready.next())
                mm(ps[:, STAT, 0:T], ones[:], squares_sum, start=True,
                   stop=True).then_inc(stat_done.sem, stat_done.plus())

            def more_ups(n):
                trips = n // RING if n >= 2 * RING else 0
                if trips:
                    with c.repeat(trips, {lo_split: RING, evacuated: RING, su_done: RING}):
                        for _ in range(RING):
                            up_unit()
                for _ in range(n - RING * trips):
                    up_unit()

            def ups(n):
                up_unit(first=True)
                norm_sum()
                more_ups(n - 1)

            def downs(n):
                down_unit(first=True)
                trips = (n - 2) // RING if n >= 2 + 2 * RING else 0
                if trips:
                    with c.repeat(trips, {lo_split: RING, hid_ready: RING, su_done: RING}):
                        for _ in range(RING):
                            down_unit()
                for _ in range(n - 2 - RING * trips):
                    down_unit()
                down_unit(last=True)

            def ffn(stats=True):
                up_unit(first=True)
                if stats:
                    norm_sum()
                else:
                    turn_small(FOX_HEADS)
                up_unit()
                up_unit()
                up_unit()
                down_unit(first=True)
                with c.repeat(FU - 2, {lo_split: 3, evacuated: 2, su_done: 3, hid_ready: 1}):
                    up_unit()
                    up_unit()
                    down_unit()
                down_unit(last=True)

            def turn_tiles(b, blocks):
                for j, t in enumerate(blocks):
                    last = nc.tensor.transpose(ps[:, b, j * P:(j + 1) * P], t, ident[:])
                last.then_inc(turned.sem, turned.plus())

            def turn_input(tok):
                for b in range(4):
                    turn_tiles(b, [tok[:, a, (2 * b + j) * P:(2 * b + j + 1) * P]
                                   for j in range(2) for a in range(TH)])

            def tok_view(first):
                return flat(proj[:, first:first + 8, :]).rearrange("p (a n) -> p a n", a=TH)

            def small_product(n):
                pe.wait_ge(small_ready.sem, small_ready.next())
                o = ps[0:n, STAT, 0:T]
                for k in range(DK):
                    mm(o, small_hi[:, k, 0:n], h_hi[:, k, :], start=(k == 0), stop=False)
                    mm(o, small_hi[:, k, 0:n], h_lo[:, k, :], start=False, stop=False)
                    last = mm(o, small_lo[:, k, 0:n], h_hi[:, k, :], start=False, stop=(k == DK - 1))
                last.then_inc(small_done.sem, small_done.plus())

            def turn_small(n):
                pe.wait_ge(small_normed.sem, small_normed.next())
                for a in range(TH):
                    last = nc.tensor.transpose(ps[:, STAT, T + 32 * a:T + 32 * a + n],
                                               small_sum[0:n, a * P:(a + 1) * P], ident[0:n, 0:n])
                last.then_inc(small_turned.sem, small_turned.plus())

            def ssd_core():
                up_unit()
                pe.wait_ge(in_ready.sem, in_ready.next(12))
                turn_tiles(0, [proj[:, 32 + g, 0:P] for g in range(SSD_GROUPS)])
                for a in range(TH):
                    for g in range(SSD_GROUPS):
                        tok = slice(a * P, (a + 1) * P)
                        last = mm(ps[:, 1 + a, g * P:(g + 1) * P], proj[:, 32 + g, tok], proj[:, 36 + g, tok],
                                  start=True, stop=True)
                last.then_inc(cb_done.sem, cb_done.plus())

                def turn_x(g, a, b=0):
                    turn_tiles(b, [proj[:, 16 + 4 * g + j, a * P:(a + 1) * P] for j in range(4)])

                def new_state(g):
                    pe.wait_ge(x_dt_ready.sem, x_dt_ready.next())
                    mm(ps[:, 0, :], b_tok[:, g, :], flat(x_dec[g % 2]), start=True,
                       stop=True).then_inc(state_done.sem, state_done.plus())

                def head_rows(p):
                    for q in range(2):
                        for a in range(TH):
                            col = 32 * a + 2 * p + q
                            last = mm(ps[:, 1 + p % 3, (2 * q + a) * P:(2 * q + a + 1) * P],
                                      dA[:, col:col + 1].to_broadcast([P, P]), upper[:], start=True, stop=True)
                    last.then_inc(rows_done.sem, rows_done.plus())

                def heads_out(p):
                    g = p // 4
                    pe.wait_ge(mask_ready.sem, mask_ready.next())
                    if p % 4 == 0:
                        pe.wait_ge(state_ready.sem, state_ready.next())
                    if y_read.due():
                        pe.wait_ge(y_read.sem, y_read.value())
                    for q in range(2):
                        h, m = (2 * p + q) % 8, seg[p % 3][:, q, :]
                        o = ps[64 * q:64 * q + 64, 7, :]
                        mm(o[:, 0:P], x_dt[g % 2][0][:, h, :], m[:, 0:P], start=True, stop=True)
                        mm(o[:, P:T], x_dt[g % 2][1][:, h, :], m[:, P:T], start=True, stop=False)
                        last = mm(o[:, P:T], state[g % 2][:, 64 * h:64 * h + 64], row_e[p % 3][:, q, :],
                                  start=False, stop=True)
                    last.then_inc(y_done.sem, y_done.plus())

                def square_sum(g, b, half):
                    pe.wait_ge(y_squares.sem, y_squares.next())
                    for j in range(4):
                        last = mm(ps[:, b, half * T:(half + 1) * T], ones[:], group_squares[g][:, j, :],
                                  start=(j == 0), stop=(j == 3))
                    last.then_inc(group_sum.sem, group_sum.plus())

                turn_x(0, 0, 3)
                turn_x(0, 1, 7)
                up_unit()
                pe.wait_ge(bank_free.sem, bank_free.next(2))
                new_state(0)
                pe.wait_ge(cb_read.sem, cb_read.next())
                head_rows(0)
                head_rows(1)
                gates = woven(Z_WOVEN)
                for p in range(SSD_PAIRS):
                    if p + 2 < SSD_PAIRS:
                        head_rows(p + 2)
                    heads_out(p)
                    if p // 4 + 1 < SSD_GROUPS:
                        if p % 4 == 1:
                            turn_x(p // 4 + 1, 0)
                        elif p % 4 == 2:
                            pe.wait_ge(bank_free.sem, bank_free.next())
                            turn_x(p // 4 + 1, 1)
                        elif p % 4 == 3:
                            new_state(p // 4 + 1)
                    gates(p)
                    if p == SSD_PAIRS - 3:
                        pe.wait_ge(evacuated.sem, evacuated.value(2))
                    if p >= SSD_PAIRS - 3:
                        g = p - (SSD_PAIRS - 3)
                        square_sum(g, 4 + g // 2, g % 2)
                square_sum(3, 6, 0)

            def softmax_attention(kind, between=lambda n: None):
                n_heads, q0, _, _ = attention(kind)

                def scores(n):
                    h, a, b = n // 2, n % 2, n % 3
                    nk = keys_of(kind, a)
                    q = proj[:, q0 + h, a * P:(a + 1) * P]
                    if kind == "diff":
                        mm(ps[:, b, 0:nk], q[0:64, :], proj[0:64, 8 + h, 0:nk],
                           start=True, stop=True).then_inc(first_scored.sem, first_scored.plus())
                        return
                    elif kind == "fox":
                        if a == 0:
                            f0 = log_f[:, 0, h:h + 1].to_broadcast([P, P])
                            mm(ps[:, 4 + h % 2, 0:P], f0, upper[:], start=True, stop=True)
                            mm(ps[:, 4 + h % 2, P:T], f0, ones[:], start=True, stop=False)
                            mm(ps[:, 4 + h % 2, P:T], log_f[:, 1, h:h + 1].to_broadcast([P, P]), upper[:],
                               start=False, stop=True)
                        last = mm(ps[:, b, 0:nk], q, proj[:, h, 0:nk], start=True, stop=True)
                    else:
                        last = mm(ps[:, b, 0:nk], q, mem_k[:, int(kind[3]), h, :], start=True, stop=True)
                    last.then_inc(scored.sem, scored.plus())

                def scores_second(n):
                    if kind == "diff":
                        h, a, b = n // 2, n % 2, n % 3
                        nk = keys_of(kind, a)
                        pe.wait_ge(first_scored.sem, first_scored.value())
                        mm(ps[:, b, T:T + nk], proj[64:P, q0 + h, a * P:(a + 1) * P], proj[64:P, 8 + h, 0:nk],
                           start=True, stop=True).then_inc(scored.sem, scored.plus())

                def turn(n):
                    nk = keys_of(kind, n % 2)
                    pe.wait_ge(probs_ready.sem, probs_ready.next())
                    for kb in range(nk // P):
                        last = nc.tensor.transpose(ps[:, 3, kb * P:(kb + 1) * P],
                                                   probs[n % 2][:, kb * P:(kb + 1) * P], ident[:])
                    last.then_inc(probs_turned.sem, probs_turned.plus())

                def values(n):
                    h, a = n // 2, n % 2
                    nk = keys_of(kind, a)
                    if a == 0:
                        if out_read.due():
                            pe.wait_ge(out_read.sem, out_read.value())
                    pe.wait_ge(probs_copied.sem, probs_copied.next())
                    for kb in range(nk // P):
                        v = (mem_v[:, int(kind[3]), kb, h * P:(h + 1) * P] if kind.startswith("mem")
                             else v_tok[:, kb, h * P:(h + 1) * P])
                        last = mm(ps[:, 7, a * P:(a + 1) * P], v, probs_t[n % 2][:, kb * P:(kb + 1) * P],
                                  start=(kb == 0), stop=(kb == nk // P - 1))
                    if a == 1:
                        last.then_inc(out_done.sem, out_done.plus())

                n_units = 2 * n_heads
                for n in range(2):
                    scores(n)
                    scores_second(n)
                for n in range(n_units):
                    if n + 2 < n_units:
                        scores(n + 2)
                    if n >= 1:
                        values(n - 1)
                    if n + 2 < n_units:
                        scores_second(n + 2)
                    turn(n)
                    between(n)
                values(n_units - 1)

            def turn_values(v0):
                for a in range(TH):
                    for b in range(2):
                        turn_tiles(2 * a + b, [proj[:, v0 + 4 * b + h, a * P:(a + 1) * P] for h in range(4)])
                pe.wait_ge(bank_free.sem, bank_free.next(4))

            pe.wait_ge(pool_made.sem, pool_made.next(POOL_MADE))
            pe.wait_ge(x_staged.sem, x_staged.next())
            turn_input(flat(proj[:, 0:8, :]).rearrange("p (a n) -> p a n", a=TH))
            vrows = flat(proj[:, 24:27, :])
            pe.wait_ge(first_staged.sem, first_staged.next(LOADED_FIRST))
            turn_tiles(4, [vrows[:, 0:P]])
            pe.wait_ge(setup_read.sem, setup_read.next())

            up_unit(first=True)
            norm_sum()
            pe.wait_ge(staged.sem, staged.next(LOADED_LATER))
            turn_tiles(5, [vrows[:, b * P:(b + 1) * P] for b in range(1, VBLOCKS)])
            mm(ps[:, 6, 0:1], freq_row, ones[0:1, 0:1], start=True, stop=True).then_inc(freq_done.sem, freq_done.plus())
            pe.wait_ge(mem_staged.sem, mem_staged.next())
            turn_input(mem_flat.rearrange("p (a n) -> p a n", a=TH))
            pe.wait_ge(setup_read.sem, setup_read.next(2))
            more_ups(5)
            small_product(SSD_HEADS)
            turn_small(SSD_HEADS)
            more_ups(3)
            pe.wait_ge(dA_ready.sem, dA_ready.next())
            mm(ps[:, STAT, 0:64], upper[:], dA, start=True, stop=True)
            mm(ps[:, STAT, 64:96], ones[:], dA[:, 0:32], start=True, stop=True).then_inc(cumsum_done.sem, cumsum_done.plus())
            more_ups(3)
            ssd_core()
            downs(8)
            ffn()

            ups(12)
            pe.wait_ge(evacuated.sem, evacuated.value(2))

            def qk_sum(i):
                pe.wait_ge(qk_squares.sem, qk_squares.next())
                for j in range(4):
                    last = mm(ps[:, j, :], half_ones[:], flat(qk_sq[i][:, 2 * j:2 * j + 2, :]), start=True, stop=True)
                last.then_inc(qk_summed.sem, qk_summed.plus())

            up_unit(first=True)
            norm_sum(mem_partial)
            up_unit()
            qk_sum(0)
            up_unit()
            pe.wait_ge(qk_logs.sem, qk_logs.next())
            qk_sum(1)
            up_unit()
            pe.wait_ge(qk_logs.sem, qk_logs.next())
            kv_units = woven(KV_ROPE)
            for j in range(8):
                pe.wait_ge(qk_normed.sem, qk_normed.next())
                if qk_rotated.due():
                    pe.wait_ge(qk_rotated.sem, qk_rotated.value())
                mm(ps[:, j % 4, :], swap[:], flat(proj[:, 2 * j:2 * j + 2, :]),
                   start=True, stop=True).then_inc(qk_swapped.sem, qk_swapped.plus())
                kv_units(j)
            if qk_rotated.due(4):
                pe.wait_ge(qk_rotated.sem, qk_rotated.value())
            turn_values(16)
            softmax_attention("diff", woven(KV_WOVEN))
            pe.wait_ge(evacuated.sem, evacuated.value(2))
            pe.wait_ge(out_read.sem, out_read.value(1))
            for l in range(2):
                for a in range(TH):
                    turn_tiles(4 + 2 * l + a, [proj[:, 32 + 4 * l + h, a * P:(a + 1) * P] for h in range(MEM_HEADS)])
            pe.wait_ge(o_squares.sem, o_squares.next())
            for j in range(4):
                last = mm(ps[:, j, :], ones[:], flat(wide_a[:, 2 * j:2 * j + 2, :]), start=True, stop=True)
            last.then_inc(o_summed.sem, o_summed.plus())
            pe.wait_ge(bank_free.sem, bank_free.next(4))
            downs(4)
            ffn()
            ffn()

            ups(3)
            pe.wait_ge(evacuated.sem, evacuated.value(1))
            softmax_attention("mem0", woven(A_WOVEN))
            more_ups(7 - A_WOVEN)
            down_unit(first=True)
            down_unit()
            more_ups(4)
            for j in range(4):
                down_unit(last=(j == 3))
            ffn()

            ups(8)
            small_product(FOX_HEADS)
            ffn(stats=False)
            pe.wait_ge(log_f_ready.sem, log_f_ready.next())
            mm(ps[:, STAT, 0:8], upper[:], log_f[:, 0, :], start=True, stop=True)
            mm(ps[:, STAT, 8:16], ones[:], log_f[:, 0, :], start=True, stop=False)
            mm(ps[:, STAT, 8:16], upper[:], log_f[:, 1, :], start=False, stop=True).then_inc(cum_f_done.sem, cum_f_done.plus())
            pe.wait_ge(cum_f_read.sem, cum_f_read.next())

            ups(3)
            pe.wait_ge(evacuated.sem, evacuated.value(1))
            softmax_attention("mem1", woven(B_WOVEN))
            pe.wait_ge(evacuated.sem, evacuated.value(2))
            pe.wait_ge(out_read.sem, out_read.value(1))
            turn_values(8)
            softmax_attention("fox")
            downs(6)
            ffn()

            pe.wait_ge(final_x.sem, final_x.next())
            for a in range(TH):
                for b in range(2):
                    turn_tiles(2 * a + b, [gained[:, 4 * b + j, a * P:(a + 1) * P] for j in range(4)])
            pe.wait_ge(sums_ready.sem, sums_ready.next())
            for a in range(TH):
                last = mm(ps[:, STAT, a:a + 1], partial[:, a * P:(a + 1) * P], ones[:, 0:1], start=True, stop=True)
            last.then_inc(stat_done.sem, stat_done.plus())

        @block.scalar
        def _(act):
            f = nc.scalar.activation
            c = Counts(act, sem)
            act_hi_made = c("act_hi_made")
            biased = c("biased")
            conv_base = c("conv_base")
            conv_done = c("conv_done")
            decay_done = c("decay_done")
            decay_in = c("decay_in")
            decay_rate = c("decay_rate")
            decay_ready = c("decay_ready")
            evacuated = c("evacuated")
            exps_done = c("exps_done")
            extras = c("extras_staged", step=16)
            final_x = c("final_x")
            gate_act = c("gate_act")
            gate_ready = c("gate_ready")
            gated = c("gated")
            gated_input = c("gated_input")
            group_rstd = c("group_rstd")
            group_sum = c("group_sum")
            h_hi_made = c("h_hi_made")
            half_sin = c("half_sin")
            hi_split = c("hi_split")
            hidden_ready = c("hidden_ready")
            in_ready = c("in_ready")
            small_done = c("small_done")
            lam_exp = c("lam_exp")
            lam_in = c("lam_in")
            o_rstd = c("o_rstd")
            o_squares = c("o_squares")
            o_summed = c("o_summed")
            out_done = c("out_done")
            out_read = c("out_read")
            pool_made = c("pool_made")
            probs_copied = c("probs_copied")
            probs_turned = c("probs_turned")
            qk_logs = c("qk_logs")
            qk_rstd = c("qk_rstd")
            qk_squares = c("qk_squares")
            qk_summed = c("qk_summed")
            row_exp = c("row_exp")
            rstd_ready = c("rstd_ready")
            scored = c("scored")
            seg_ready = c("seg_ready")
            setup_read = c("setup_read")
            z_ready = c("z_ready")
            mem_staged = c("mem_staged", step=16)
            first_staged = c("first_staged", step=16)
            shifted = c("shifted")
            small_free = c("small_free")
            small_hi_made = c("small_hi_made")
            small_landed = c("small_landed", step=16)
            source_ready = c("source_ready")
            sp_exp = c("sp_exp")
            sp_in = c("sp_in")
            sp_ln = c("sp_ln")
            sp_one = c("sp_one")
            squares_made = c("squares_made")
            staged = c("staged", step=16)
            stat_done = c("stat_done")
            state_done = c("state_done")
            state_ready = c("state_ready")
            step = c("act_step")
            su_done = c("su_done")
            trig_in = c("trig_in")
            x_ready = c("x_ready")
            x_staged = c("x_staged", step=16)
            y_squares = c("y_squares")
            landed = [c(f"landed{s}", step=16) for s in range(RING)]
            slot, unit = [0], [0]

            def split(s):
                act.wait_ge(landed[s].sem, landed[s].next())
                f(w_hi[:, s, :], raw[:, s, :], ACT.Copy).then_inc(hi_split.sem, hi_split.plus())

            def split_next(trips=1):
                if unit[0] + RING < UNITS:
                    split(slot[0])
                unit[0] += trips
                slot[0] = (slot[0] + 1) % RING

            def per_trip(**extra):
                return {hi_split: RING, su_done: RING, **{t: 1 for t in landed},
                        **{c(k): v for k, v in extra.items()}}

            def one_unit(work, j):
                act.wait_ge(su_done.sem, su_done.next())
                work(j, slot[0])
                split_next()

            def units(n, work, j0=0, late=lambda j, s: None, **extra):
                trips = n // RING if n >= 2 * RING else 0
                if trips:
                    with c.repeat(trips, per_trip(**{k: RING * v for k, v in extra.items()})) as i:
                        for j in range(RING):
                            act.wait_ge(su_done.sem, su_done.next())
                            s = slot[0]
                            work(i * RING + (j0 + j), s)
                            split_next(trips)
                            late(i * RING + (j0 + j), s)
                for j in range(j0 + trips * RING, j0 + n):
                    act.wait_ge(su_done.sem, su_done.next())
                    s = slot[0]
                    work(j, s)
                    split_next()
                    late(j, s)

            def woven(n, read=None):
                def step(t):
                    if t % 2 == 0 and 2 <= t < 2 * n + 2:
                        act.wait_ge(su_done.sem, su_done.next())
                        split_next()
                    if t % 2 and 3 <= t < 2 * n + 3:
                        act.wait_ge(evacuated.sem, evacuated.next())
                        if read:
                            read((t - 3) // 2)
                return step

            def columns():
                act.wait_ge(setup_read.sem, 3)

            def skip(j, s):
                act.wait_ge(evacuated.sem, evacuated.next())

            def inverse_root(dst, src, scale):
                f(dst, src, ACT.Ln, bias=eps_col, scale=scale).then_inc(step.sem, step.plus())
                act.wait_ge(step.sem, step.value())
                return f(dst, dst, ACT.Exp, scale=-0.5)

            def norm(gain, g0, again=False, h=True, stats=True, renew=True, src=x, sq=squares):
                for b in range(4):
                    if not again:
                        act.wait_ge(x_ready.sem, x_ready.next())
                    for k in (2 * b, 2 * b + 1):
                        if h:
                            f(h_hi[:, k, :], src[:, k, :], ACT.Copy,
                              scale=vcol(gain, g0 + k)).then_inc(h_hi_made.sem, h_hi_made.plus())
                if stats:
                    f(sq, src[:], ACT.Square).then_inc(squares_made.sem, squares_made.plus())
                if renew is True:
                    split_next()
                elif renew:
                    renew()
                if stats:
                    act.wait_ge(stat_done.sem, stat_done.next())
                    inverse_root(rstd[:], ps[:, STAT, 0:T], 1.0 / D).then_inc(rstd_ready.sem, rstd_ready.plus())

            def feed(src, j, s):
                f(act_hi[:, s, :, :], src[:, 2 * j:2 * j + 2, :], ACT.Copy).then_inc(act_hi_made.sem, act_hi_made.plus())

            def downs(n, src, order=None, ready=lambda j: None):
                s, order = slot[0], order or range(n)

                def give(j):
                    ready(j)
                    feed(src, order[j], (s + j) % RING)

                for j in range(min(RING, n)):
                    give(j)
                for j in range(n - 1):
                    act.wait_ge(su_done.sem, su_done.next())
                    if j + RING < n:
                        give(j + RING)
                    split_next()

            def ffn(conv=None):
                def tap_and_bias(w, tile):
                    columns()
                    for a in range(2):
                        last = f(f_out[:, w, a, :], f_in[:, w, a, :], ACT.Identity,
                                 scale=vcol("ffn_conv_w", conv * 6 * FT + 4 * FT + a + tile),
                                 bias=vcol("ffn_conv_b", conv * 2 * FT + a + tile))
                    last.then_inc(conv_base.sem, conv_base.plus())

                def gate(j):
                    act.wait_ge(su_done.sem, su_done.next())
                    act.wait_ge(evacuated.sem, evacuated.next())
                    if conv is None:
                        f(f_out[:, 0, :, :], f_in[:, 0, :, :], ACT.Silu).then_inc(gate_act.sem, gate_act.plus())
                    else:
                        tap_and_bias(0, j * 2)
                    split_next()

                def up(j):
                    act.wait_ge(su_done.sem, su_done.next())
                    act.wait_ge(evacuated.sem, evacuated.next())
                    if conv is not None:
                        tap_and_bias(1, j * 2 + FT)
                        act.wait_ge(gate_ready.sem, gate_ready.next())
                        f(f_out[:, 0, :, :], f_out[:, 0, :, :], ACT.Silu).then_inc(gate_act.sem, gate_act.plus())
                    split_next()

                down_slot, last_slot = (slot[0] + 4) % RING, (slot[0] + 2) % RING

                def give(s):
                    act.wait_ge(hidden_ready.sem, hidden_ready.next())
                    f(act_hi[:, s, :, :], hidden, ACT.Copy).then_inc(act_hi_made.sem, act_hi_made.plus())

                gate(0)
                up(0)
                give(down_slot)
                extra = dict(evacuated=2, gate_act=1, hidden_ready=1, act_hi_made=1)
                if conv is not None:
                    extra.update(conv_base=2, gate_ready=1)

                def trip(j, s):
                    gate(j + 1)
                    up(j + 1)
                    act.wait_ge(su_done.sem, su_done.next())
                    give(s)
                    split_next()

                u0 = unit[0]
                with c.repeat(FU - 2, per_trip(**extra)) as i:
                    trip(i, down_slot)
                unit[0] = u0 + 3 * (FU - 2)
                trip(FU - 2, last_slot)

            def softmax_attention(kind, between=lambda n: None):
                n_heads, _, out0, scale = attention(kind)

                def query_bias(n):
                    h, a = n // 2, n % 2
                    nk = keys_of(kind, a)
                    act.wait_ge(scored.sem, scored.next())
                    if n >= 2:
                        act.wait_ge(exps_done.sem, exps_done.value())
                    f(s_buf[n % 2][:, 0, 0:nk], ps[:, n % 3, 0:nk], ACT.Identity,
                                       scale=scale, bias=cum_f[:, a, h:h + 1]).then_inc(biased.sem, biased.plus())

                def exps(n):
                    nk = keys_of(kind, n % 2)
                    t = tiny[n % 2]
                    act.wait_ge(shifted.sem, shifted.next())
                    if kind == "diff":
                        for j in range(2):
                            last = f(p_buf[n % 2][:, j, 0:nk], s_buf[n % 2][:, j, 0:nk], ACT.Exp,
                                     bias=t[:, 1, j:j + 1], accum_out=t[:, 2, j:j + 1])
                    elif kind == "fox":
                        last = f(p_buf[n % 2][:, 0, 0:nk], s_buf[n % 2][:, 0, 0:nk], ACT.Exp,
                                 bias=t[:, 1, 0:1], accum_out=t[:, 2, 0:1])
                    else:
                        last = f(p_buf[n % 2][:, 0, 0:nk], ps[:, n % 3, 0:nk], ACT.Exp, scale=scale,
                                 bias=t[:, 1, 0:1], accum_out=t[:, 2, 0:1])
                    last.then_inc(exps_done.sem, exps_done.plus())

                def copy_turned(n):
                    nk = keys_of(kind, n % 2)
                    act.wait_ge(probs_turned.sem, probs_turned.next())
                    f(probs_t[n % 2][:, 0:nk], ps[:, 3, 0:nk], ACT.Copy).then_inc(probs_copied.sem, probs_copied.plus())

                def copy_out(h):
                    act.wait_ge(out_done.sem, out_done.next())
                    f(proj[:, out0 + h, :], ps[:, 7, 0:T], ACT.Copy).then_inc(out_read.sem, out_read.plus())

                n_units = 2 * n_heads
                if kind == "fox":
                    query_bias(0)
                else:
                    scored.n += n_units
                for n in range(n_units):
                    if kind == "fox" and n + 1 < n_units:
                        query_bias(n + 1)
                    exps(n)
                    if n % 2 == 1 and n >= 3:
                        copy_out((n - 3) // 2)
                    if n >= 1:
                        copy_turned(n - 1)
                    between(n)
                copy_turned(n_units - 1)
                copy_out(n_heads - 1)
                for n in range(n_units, n_units + 3):
                    between(n)
                act.wait_ge(out_read.sem, out_read.value())

            def softplus():
                act.wait_ge(sp_in.sem, sp_in.next())
                f(sp[1], sp[0], ACT.Abs).then_inc(step.sem, step.plus())
                act.wait_ge(step.sem, step.value())
                f(sp[2], sp[1], ACT.Exp, scale=-1.0).then_inc(sp_exp.sem, sp_exp.plus())
                act.wait_ge(sp_one.sem, sp_one.next())
                f(sp[4], sp[3], ACT.Ln).then_inc(sp_ln.sem, sp_ln.plus())

            def small_weights():
                act.wait_ge(small_landed.sem, small_landed.next())
                f(small_hi[:], small_raw[:], ACT.Copy).then_inc(small_hi_made.sem, small_hi_made.plus())

            split(0)

            def activate_z(j):
                z = proj[:, 2 * j:2 * j + 2, :]
                f(z, z, ACT.Silu).then_inc(z_ready.sem, z_ready.plus())

            def silu_z(j, s):
                act.wait_ge(evacuated.sem, evacuated.next())
                activate_z(j)

            def conv_xbc(j, s):
                act.wait_ge(evacuated.sem, evacuated.next())
                columns()
                for a in range(2):
                    last = f(conv_out[s][:, a, :], conv_in[s][:, a, :], ACT.Identity,
                             scale=vcol("ssd_conv_w", j * 2 + (3 * SSD_XBC // P + a)),
                             bias=vcol("ssd_conv_b", j * 2 + a))
                last.then_inc(conv_base.sem, conv_base.plus())

            def silu_xbc(j, s):
                act.wait_ge(conv_done.sem, conv_done.next())
                f(proj[:, bass.ds(j * 2 + 16, 2), :], conv_out[s], ACT.Silu).then_inc(in_ready.sem, in_ready.plus())

            act.wait_ge(setup_read.sem, 1)

            def fill_ring():
                split(1)
                split(2)

            norm("norm_mix_g", 0, renew=fill_ring)
            units(3, conv_xbc, 0, late=silu_xbc, evacuated=1, in_ready=1, conv_base=1, conv_done=1)
            act.wait_ge(trig_in.sem, trig_in.next())
            f(sin[:], scr(5632, T), ACT.Sin).then_inc(step.sem, step.plus())
            f(cos[:], scr(5632, T), ACT.Sin, scale=0.5).then_inc(half_sin.sem, half_sin.plus())
            act.wait_ge(lam_in.sem, lam_in.next(2))
            f(cols[:, 4:6], cols[:, 6:8], ACT.Exp).then_inc(lam_exp.sem, lam_exp.plus())
            units(3, conv_xbc, 3, late=silu_xbc, evacuated=1, in_ready=1, conv_base=1, conv_done=1)
            small_weights()
            softplus()
            f(heads[:, 1, :], heads[:, 1, :], ACT.Exp).then_inc(decay_rate.sem, decay_rate.plus())
            units(3, conv_xbc, 6, late=silu_xbc, evacuated=1, in_ready=1, conv_base=1, conv_done=1)
            act.wait_ge(decay_in.sem, decay_in.next())
            f(dec, dec, ACT.Exp).then_inc(decay_done.sem, decay_done.plus())
            units(3, conv_xbc, 9, late=silu_xbc, evacuated=1, in_ready=1, conv_base=1, conv_done=1)

            def state_copy(g):
                act.wait_ge(state_done.sem, state_done.next())
                f(state[g % 2], ps[:, 0, :], ACT.Copy).then_inc(state_ready.sem, state_ready.plus())

            def group_square(g):
                act.wait_ge(gated.sem, gated.next(4))
                f(group_squares[g], proj[:, 16 + 4 * g:20 + 4 * g, :],
                  ACT.Square).then_inc(y_squares.sem, y_squares.plus())

            one_unit(silu_z, 0)
            one_unit(silu_z, 1)
            state_copy(0)
            gates = woven(Z_WOVEN, lambda j: activate_z(j + 2))
            for p in range(SSD_PAIRS):
                act.wait_ge(seg_ready.sem, seg_ready.next())
                f(seg[p % 3], seg[p % 3], ACT.Exp).then_inc(decay_ready.sem, decay_ready.plus())
                rows_t = ps[:, 1 + p % 3, :].rearrange("p (q a t) -> p q a t", q=2, a=TH)[:, :, 1, :]
                f(row_e[p % 3], rows_t, ACT.Exp).then_inc(row_exp.sem, row_exp.plus())
                if p % 4 == 3 and p // 4 + 1 < SSD_GROUPS:
                    state_copy(p // 4 + 1)
                gates(p)
                if p >= SSD_PAIRS - 3:
                    group_square(p - (SSD_PAIRS - 3))
            group_square(3)
            for g0, g1, b in ((0, 2, 4), (2, 3, 5), (3, 4, 6)):
                act.wait_ge(group_sum.sem, group_sum.next(g1 - g0))
                f(flat(group_rs[:, g0:g1, :]), ps[:, b, 0:(g1 - g0) * T], ACT.Ln, bias=eps_col,
                  scale=1.0 / (SSD_INNER // SSD_GROUPS)).then_inc(step.sem, step.plus())
            act.wait_ge(step.sem, step.value())
            f(group_rs, group_rs, ACT.Exp, scale=-0.5).then_inc(group_rstd.sem, group_rstd.plus())

            def group_normed(j):
                if j % 2 == 0:
                    act.wait_ge(source_ready.sem, source_ready.next())

            downs(8, proj[:, 16:32, :], ready=group_normed)
            norm("norm_ffn_g", 0)
            ffn(conv=0)

            norm("norm_mix_g", DK)
            units(12, skip, evacuated=1)
            norm("mem_norm_2", 0, again=True, renew=None, src=mem_raw, sq=mem_squares)
            for i in range(2):
                f(qk_sq[i], proj[:, 8 * i:8 * i + 8, :], ACT.Square).then_inc(qk_squares.sem, qk_squares.plus())
            one_unit(skip, 0)
            one_unit(skip, 0)
            for i in range(2):
                act.wait_ge(qk_summed.sem, qk_summed.next())
                f(flat(qk_rn[i]), ps[:, 0:4, :].rearrange("p b t -> p (b t)"), ACT.Ln, bias=eps_col,
                  scale=1.0 / ATT_HD).then_inc(qk_logs.sem, qk_logs.plus())
                one_unit(skip, 0)
            act.wait_ge(qk_logs.sem, qk_logs.value())
            for i in range(2):
                f(qk_rn[i], qk_rn[i], ACT.Exp, scale=-0.5).then_inc(qk_rstd.sem, qk_rstd.plus())
            kv_units = woven(KV_ROPE)
            for j in range(8):
                kv_units(j)
            softmax_attention("diff", woven(KV_WOVEN))
            f(wide_a, proj[:, 24:32, :], ACT.Square).then_inc(o_squares.sem, o_squares.plus())
            act.wait_ge(o_summed.sem, o_summed.next())
            inverse_root(flat(wide_b), ps[:, 0:4, :].rearrange("p b t -> p (b t)"), 1.0 / P).then_inc(o_rstd.sem, o_rstd.plus())
            act.wait_ge(source_ready.sem, source_ready.next())
            downs(4, proj[:, 24:32, :])
            norm("norm_ffn_g", DK)
            ffn(conv=1)
            norm("ffn_norm_2", 0)
            ffn()

            norm("mix_norm_2", 0)
            units(2, skip, evacuated=1)
            one_unit(skip, 0)
            softmax_attention("mem0", woven(A_WOVEN))
            units(7 - A_WOVEN, skip, evacuated=1)
            for j in range(2):
                feed(proj[:, 36:40, :], j, (slot[0] + j) % RING)
            act.wait_ge(gated_input.sem, gated_input.next())
            for k in range(DK):
                last = f(proj[:, 28 + k, :], proj[:, 8 + k, :], ACT.Copy, scale=vcol("a_conv_w_2", 2 * DK + k))
            last.then_inc(conv_base.sem, conv_base.plus())
            for j in range(2):
                act.wait_ge(su_done.sem, su_done.next())
                split_next()
            units(4, skip, evacuated=1)

            def convolved(j):
                act.wait_ge(source_ready.sem, source_ready.next())

            downs(4, proj[:, 28:36, :], ready=convolved)
            norm("ffn_norm_2", DK)
            ffn()

            act.wait_ge(small_free.sem, small_free.next())
            small_n = w_small_f = A["w_kvf_2"].rearrange("(k p) n -> p k n", p=P)[:, :, 2 * D:]
            act.dma_start(small_raw[:, :, 0:FOX_HEADS], w_small_f).then_inc(sem("small_landed"), 16)
            norm("kv_norm_2", 0)
            units(8, skip, evacuated=1)
            act.wait_ge(small_landed.sem, small_landed.next())
            f(small_hi[:, :, 0:FOX_HEADS], small_raw[:, :, 0:FOX_HEADS], ACT.Copy).then_inc(small_hi_made.sem, small_hi_made.plus())
            act.wait_ge(small_done.sem, small_done.next(2))
            norm("ffn_norm_2", 2 * DK, again=True, stats=False, renew=None)
            softplus()
            ffn()

            norm("mix_norm_2", DK)
            units(2, skip, evacuated=1)
            one_unit(skip, 0)
            softmax_attention("mem1", woven(B_WOVEN))
            softmax_attention("fox")
            downs(6, proj[:, 28:40, :], MIXED_ORDER)
            norm("ffn_norm_2", 3 * DK)
            ffn()
            for b in range(4):
                act.wait_ge(x_ready.sem, x_ready.next())
                for k in (2 * b, 2 * b + 1):
                    f(squares[:, k, :], x[:, k, :], ACT.Square).then_inc(squares_made.sem, squares_made.plus())
            for k in range(DK):
                last = f(gained[:, k, :], x[:, k, :], ACT.Copy, scale=vcol("final_norm_2", k))
            last.then_inc(final_x.sem, final_x.plus())
            act.wait_ge(stat_done.sem, stat_done.next())
            inverse_root(cols[:, 8:10], ps[:, STAT, 0:TH], 1.0 / D).then_inc(rstd_ready.sem, rstd_ready.plus())

        @block.vector
        def _(dve):
            v = nc.vector
            tt, stt, ts = v.tensor_tensor, v.scalar_tensor_tensor, v.tensor_scalar
            c = Counts(dve, sem)
            bank_summed = c("bank_summed")
            cb_read = c("cb_read")
            z_ready = c("z_ready")
            act_hi_made = c("act_hi_made")
            bank_free = c("bank_free")
            biased = c("biased")
            cb_done = c("cb_done")
            conv_base = c("conv_base")
            conv_done = c("conv_done")
            cum_f_done = c("cum_f_done")
            cum_f_read = c("cum_f_read")
            cumsum_done = c("cumsum_done")
            dA_ready = c("dA_ready")
            decay_done = c("decay_done")
            decay_in = c("decay_in")
            decay_rate = c("decay_rate")
            decay_ready = c("decay_ready")
            evacuated = c("evacuated")
            exps_done = c("exps_done")
            extras = c("extras_staged", step=16)
            final_ready = c("final_ready")
            freq_done = c("freq_done")
            gate_act = c("gate_act")
            gate_ready = c("gate_ready")
            gated = c("gated")
            gated_input = c("gated_input")
            group_rstd = c("group_rstd")
            h_hi_made = c("h_hi_made")
            h_ready = c("h_ready")
            half_sin = c("half_sin")
            hi_split = c("hi_split")
            hid_ready = c("hid_ready")
            hidden_ready = c("hidden_ready")
            in_ready = c("in_ready")
            lam_exp = c("lam_exp")
            lam_in = c("lam_in")
            lo_split = c("lo_split")
            log_f_ready = c("log_f_ready")
            mask_ready = c("mask_ready")
            o_rstd = c("o_rstd")
            out_read = c("out_read")
            pool_made = c("pool_made")
            probs_old = c("probs_turned", -2)
            probs_ready = c("probs_ready")
            qk_normed = c("qk_normed")
            qk_rotated = c("qk_rotated")
            qk_rstd = c("qk_rstd")
            qk_swapped = c("qk_swapped")
            row_exp = c("row_exp")
            rows_done = c("rows_done")
            rstd_ready = c("rstd_ready")
            scored = c("scored")
            seg_ready = c("seg_ready")
            setup_read = c("setup_read")
            shifted = c("shifted")
            small_done = c("small_done")
            small_normed = c("small_normed")
            small_turned = c("small_turned")
            small_free = c("small_free")
            small_hi_made = c("small_hi_made")
            small_ready = c("small_ready")
            source_ready = c("source_ready")
            sp_exp = c("sp_exp")
            sp_in = c("sp_in")
            sp_ln = c("sp_ln")
            sp_one = c("sp_one")
            squares_made = c("squares_made")
            step = c("vec_step")
            su_done = c("su_done")
            sums_ready = c("sums_ready")
            trig_in = c("trig_in")
            turned = c("turned")
            x_dt_ready = c("x_dt_ready")
            x_ready = c("x_ready")
            y_done = c("y_done")
            y_old = c("y_done", -3)
            y_read = c("y_read")
            slot, unit = [0], [0]

            def f32(ap):
                return ap.bitcast(F32)

            def split(s):
                dve.wait_ge(hi_split.sem, hi_split.next())
                tt(w_lo[:, s, :], raw[:, s, :], f32(w_hi[:, s, :]), ALU.subtract).then_inc(lo_split.sem, lo_split.plus())

            def split_next(trips=1):
                if unit[0] + RING < UNITS:
                    split(slot[0])
                unit[0] += trips
                slot[0] = (slot[0] + 1) % RING

            def per_trip(**extra):
                return {hi_split: RING, lo_split: RING, su_done: RING, **{c(k): n for k, n in extra.items()}}

            def one_unit(work, j):
                dve.wait_ge(su_done.sem, su_done.next())
                work(j, slot[0])
                split_next()

            def units(n, work, j0=0, **extra):
                trips = n // RING if n >= 2 * RING else 0
                if trips:
                    with c.repeat(trips, per_trip(**{k: RING * m for k, m in extra.items()})) as i:
                        for j in range(RING):
                            dve.wait_ge(su_done.sem, su_done.next())
                            work(i * RING + (j0 + j), slot[0])
                            split_next(trips)
                for j in range(j0 + trips * RING, j0 + n):
                    one_unit(work, j)

            def woven(n, work, j0=0):
                def step(t):
                    if t % 2 == 0 and 2 <= t < 2 * n + 2:
                        dve.wait_ge(su_done.sem, su_done.next())
                        work(j0 + (t - 2) // 2, slot[0])
                    if t % 2 and 3 <= t < 2 * n + 3:
                        split_next()
                return step

            def evacuate(dst, s):
                tt(dst, bank(4 + s), rows(rstd[:], 2), ALU.mult).then_inc(evacuated.sem, evacuated.plus())

            def to_proj(first):
                def work(j, s):
                    evacuate(proj[:, bass.ds(j * 2 + first, 2), :], s)
                return work

            def residual(scale=1.0):
                def take(b):
                    dve.wait_ge(bank_summed.sem, bank_summed.next())
                    t = x[:, 2 * b:2 * b + 2, :]
                    stt(t, bank(b), scale, t, ALU.mult, ALU.add).then_inc(x_ready.sem, x_ready.plus())
                return take

            def norm(gain, g0, take=None, stats=True, renew=True, src=x, sq=squares, total=partial):
                for b in range(5):
                    if take and b < 4:
                        take(b)
                    for k in (2 * b - 2, 2 * b - 1):
                        if gain and k >= 0:
                            dve.wait_ge(h_hi_made.sem, h_hi_made.next())
                            stt(h_lo[:, k, :], src[:, k, :], vcol(gain, g0 + k), f32(h_hi[:, k, :]),
                                ALU.mult, ALU.subtract).then_inc(h_ready.sem, h_ready.plus())
                if stats:
                    dve.wait_ge(squares_made.sem, squares_made.next())
                    v.tensor_reduce(total, sq.rearrange("p k t -> p t k"), AX_X,
                                    ALU.add).then_inc(sums_ready.sem, sums_ready.plus())
                if renew is True:
                    split_next()
                elif renew:
                    renew()
                if stats:
                    dve.wait_ge(rstd_ready.sem, rstd_ready.next())

            def feed(src, j, s):
                dve.wait_ge(act_hi_made.sem, act_hi_made.next())
                tt(act_lo[:, s, :, :], src[:, 2 * j:2 * j + 2, :], f32(act_hi[:, s, :, :]), ALU.subtract).then_inc(hid_ready.sem, hid_ready.plus())

            def downs(n, src, order=None, prepare=lambda j: None):
                s, order = slot[0], order or range(n)

                def give(j):
                    prepare(j)
                    feed(src, order[j], (s + j) % RING)

                for j in range(min(RING, n)):
                    give(j)
                for j in range(n - 1):
                    dve.wait_ge(su_done.sem, su_done.next())
                    if j + RING < n:
                        give(j + RING)
                    split_next()

            def ffn(conv=None):
                down_slot, last_slot = (slot[0] + 4) % RING, (slot[0] + 2) % RING

                def taps(w, tile):
                    dve.wait_ge(conv_base.sem, conv_base.next())
                    for d in (1, 2):
                        for a in range(2):
                            o = f_out[:, w, a, d:T]
                            if d > 1:
                                dve.wait_ge(step.sem, step.value(a - 1))
                            ins = stt(o, f_in[:, w, a, 0:T - d],
                                      vcol("ffn_conv_w", conv * 6 * FT + (2 - d) * 2 * FT + a + tile), o,
                                      ALU.mult, ALU.add)
                            if d == 1:
                                ins.then_inc(step.sem, step.plus())
                    return ins

                def gate(j):
                    dve.wait_ge(su_done.sem, su_done.next())
                    evacuate(f_in[:, 0, :, :], slot[0])
                    if conv is not None:
                        taps(0, j * 2).then_inc(gate_ready.sem, gate_ready.plus())
                    split_next()

                def up(j):
                    dve.wait_ge(su_done.sem, su_done.next())
                    evacuate(f_in[:, 1, :, :], slot[0])
                    if conv is None:
                        dve.wait_ge(evacuated.sem, evacuated.value())
                    else:
                        taps(1, j * 2 + FT).then_inc(step.sem, step.plus())
                        dve.wait_ge(step.sem, step.value())
                    dve.wait_ge(gate_act.sem, gate_act.next())
                    u = f_in if conv is None else f_out
                    tt(hidden, f_out[:, 0, :, :], u[:, 1, :, :], ALU.mult).then_inc(hidden_ready.sem, hidden_ready.plus())
                    split_next()

                def give(s):
                    dve.wait_ge(act_hi_made.sem, act_hi_made.next())
                    tt(act_lo[:, s, :, :], hidden, f32(act_hi[:, s, :, :]), ALU.subtract).then_inc(hid_ready.sem, hid_ready.plus())

                gate(0)
                up(0)
                give(down_slot)
                extra = dict(evacuated=2, gate_act=1, hidden_ready=1, act_hi_made=1, hid_ready=1)
                if conv is not None:
                    extra.update(conv_base=2, gate_ready=1, vec_step=5)

                def trip(j, s):
                    gate(j + 1)
                    up(j + 1)
                    dve.wait_ge(su_done.sem, su_done.next())
                    give(s)
                    split_next()

                u0 = unit[0]
                with c.repeat(FU - 2, per_trip(**extra)) as i:
                    trip(i, down_slot)
                unit[0] = u0 + 3 * (FU - 2)
                trip(FU - 2, last_slot)

            def copy_values(dst, b0):
                for i, d in enumerate(dst):
                    dve.wait_ge(turned.sem, turned.next())
                    v.tensor_copy(d, ps[:, b0 + i, :]).then_inc(bank_free.sem, bank_free.plus())

            def norm_small(n):
                dve.wait_ge(small_done.sem, small_done.next())
                tt(small_sum[0:n, :], ps[0:n, STAT, 0:T], rstd[0:n, :], ALU.mult).then_inc(small_normed.sem, small_normed.plus())

            def softplus(negate, bias, n):
                dve.wait_ge(small_turned.sem, small_turned.next())
                o = ps[:, STAT, T:T + 64].rearrange("p (a n) -> p a n", a=TH)[:, :, 0:n]
                tt(sp[0][:, :, 0:n], o, rows(bias, TH), ALU.add).then_inc(step.sem, step.plus())
                dve.wait_ge(step.sem, step.value())
                ts(sp[0][:, :, 0:n], sp[0][:, :, 0:n], -1.0 if negate else 1.0, None, ALU.mult).then_inc(sp_in.sem, sp_in.plus())
                dve.wait_ge(sp_exp.sem, sp_exp.next())
                ts(sp[3], sp[2], 1.0, None, ALU.add).then_inc(sp_one.sem, sp_one.plus())
                dve.wait_ge(sp_one.sem, sp_one.value())
                ts(sp[5], sp[3], -1.0, None, ALU.add).then_inc(step.sem, step.plus())
                dve.wait_ge(step.sem, step.value())
                ts(sp[6], sp[5], 0.0, None, ALU.is_equal).then_inc(step.sem, step.plus())
                dve.wait_ge(step.sem, step.value())
                tt(sp[5], sp[5], sp[6], ALU.add).then_inc(step.sem, step.plus())
                dve.wait_ge(step.sem, step.value())
                v.reciprocal(sp[5], sp[5]).then_inc(step.sem, step.plus())
                dve.wait_ge(step.sem, step.value())
                dve.wait_ge(sp_ln.sem, sp_ln.next())
                tt(sp[6], sp[4], sp[6], ALU.add).then_inc(step.sem, step.plus())
                dve.wait_ge(step.sem, step.value())
                tt(sp[6], sp[6], sp[5], ALU.mult).then_inc(step.sem, step.plus())
                dve.wait_ge(step.sem, step.value())
                tt(sp[6], sp[6], sp[2], ALU.mult).then_inc(step.sem, step.plus())
                dve.wait_ge(step.sem, step.value())
                dve.wait_ge(sp_in.sem, sp_in.value())
                ts(sp[7], sp[0], 0.0, None, ALU.max).then_inc(step.sem, step.plus())
                dve.wait_ge(step.sem, step.value())
                tt(sp[7], sp[7], sp[6], ALU.add).then_inc(step.sem, step.plus())
                dve.wait_ge(step.sem, step.value())

            def small_weights(n):
                dve.wait_ge(small_hi_made.sem, small_hi_made.next())
                tt(small_lo[:, :, 0:n], small_raw[:, :, 0:n], f32(small_hi[:, :, 0:n]),
                                         ALU.subtract).then_inc(small_ready.sem, small_ready.plus())

            def softmax_attention(kind, between=lambda n: None):
                n_heads, _, _, scale = attention(kind)

                def shift(n):
                    h, a, i = n // 2, n % 2, n % 2
                    nk = keys_of(kind, a)
                    t, s = tiny[i], s_buf[i]
                    if kind == "diff":
                        dve.wait_ge(scored.sem, scored.next())
                        mask = chunk_mask[:, T - nk:T]
                        stt(s[:, :, 0:nk], bank(n % 3)[:, :, 0:nk], scale, rows(mask, 2),
                                  ALU.mult, ALU.add).then_inc(step.sem, step.plus())
                        dve.wait_ge(step.sem, step.value())
                        v.tensor_reduce(t[:, 0, :], s[:, :, 0:nk], AX_X, ALU.max).then_inc(step.sem, step.plus())
                        dve.wait_ge(step.sem, step.value())
                        ts(t[:, 1, :], t[:, 0, :], -1.0, None, ALU.mult).then_inc(shifted.sem, shifted.plus())
                        return
                    if kind == "fox":
                        if a == 0:
                            dve.wait_ge(scored.sem, scored.next())
                            tt(key_row[0], causal_mask[:, P:T], ps[:, 4 + h % 2, 0:P], ALU.subtract).then_inc(step.sem, step.plus())
                            tt(key_row[1], causal_mask[:], ps[:, 4 + h % 2, 0:T], ALU.subtract).then_inc(step.sem, step.plus())
                            dve.wait_ge(step.sem, step.value())
                        else:
                            scored.n += 1
                        dve.wait_ge(biased.sem, biased.next())
                        tt(s[:, 0, 0:nk], s[:, 0, 0:nk], key_row[a], ALU.add).then_inc(step.sem, step.plus())
                        dve.wait_ge(step.sem, step.value())
                        v.tensor_reduce(t[:, 0, 0:1], s[:, 0, 0:nk], AX_X, ALU.max).then_inc(step.sem, step.plus())
                        dve.wait_ge(step.sem, step.value())
                        ts(t[:, 1, 0:1], t[:, 0, 0:1], -1.0, None, ALU.mult).then_inc(shifted.sem, shifted.plus())
                        return
                    dve.wait_ge(scored.sem, scored.next())
                    v.tensor_reduce(t[:, 0, 0:1], ps[:, n % 3, 0:nk], AX_X, ALU.max).then_inc(step.sem, step.plus())
                    dve.wait_ge(step.sem, step.value())
                    ts(t[:, 1, 0:1], t[:, 0, 0:1], -scale, None, ALU.mult).then_inc(shifted.sem, shifted.plus())

                def normalise(n):
                    i = n % 2
                    nk = keys_of(kind, i)
                    t, p, o = tiny[i], p_buf[i], probs[i][:, 0:nk]
                    m = 2 if kind == "diff" else 1
                    dve.wait_ge(exps_done.sem, exps_done.next())
                    v.reciprocal(t[:, 3, 0:m], t[:, 2, 0:m]).then_inc(step.sem, step.plus())
                    dve.wait_ge(step.sem, step.value())
                    if probs_old.due():
                        dve.wait_ge(probs_old.sem, probs_old.value())
                    if kind != "diff":
                        ts(o, p[:, 0, 0:nk], t[:, 3, 0:1], None, ALU.mult).then_inc(probs_ready.sem, probs_ready.plus())
                        return
                    tt(t[:, 4, 0:1], t[:, 3, 1:2], lam_col, ALU.mult).then_inc(step.sem, step.plus())
                    ts(o, p[:, 0, 0:nk], t[:, 3, 0:1], None, ALU.mult).then_inc(step.sem, step.plus())
                    dve.wait_ge(step.sem, step.value())
                    stt(o, p[:, 1, 0:nk], t[:, 4, 0:1], o, ALU.mult, ALU.add).then_inc(probs_ready.sem, probs_ready.plus())

                shift(0)
                for n in range(2 * n_heads):
                    if n + 1 < 2 * n_heads:
                        shift(n + 1)
                    normalise(n)
                    between(n)
                for n in range(2 * n_heads, 2 * n_heads + 3):
                    between(n)

            def take_input(b):
                v.tensor_copy(x[:, 2 * b:2 * b + 2, :], bank(b)).then_inc(x_ready.sem, x_ready.plus())

            split(0)
            dve.wait_ge(turned.sem, turned.next(5))
            v.tensor_copy(vec[:, 0:P], ps[:, 4, 0:P]).then_inc(setup_read.sem, setup_read.plus())
            dve.wait_ge(setup_read.sem, setup_read.value())

            def fill_ring():
                split(1)
                split(2)

            norm("norm_mix_g", 0, take_input, renew=fill_ring)
            dve.wait_ge(turned.sem, turned.next())
            v.tensor_copy(vec[:, P:VBLOCKS * P], ps[:, 5, 0:(VBLOCKS - 1) * P]).then_inc(setup_read.sem, setup_read.plus())
            dve.wait_ge(freq_done.sem, freq_done.next())
            dve.wait_ge(pool_made.sem, pool_made.next(POOL_MADE))
            v.tensor_copy(freq_col, ps[:, 6, 0:1]).then_inc(setup_read.sem, setup_read.plus())
            dve.wait_ge(setup_read.sem, setup_read.value())
            for b in range(4):
                dve.wait_ge(turned.sem, turned.next())
                v.tensor_copy(mem_raw[:, 2 * b:2 * b + 2, :], bank(b)).then_inc(step.sem, step.plus())

            def conv_xbc(j, s):
                evacuate(conv_in[s], s)
                dve.wait_ge(conv_base.sem, conv_base.next())
                for d in (1, 2, 3):
                    for a in range(2):
                        o = conv_out[s][:, a, d:T]
                        if d > 1:
                            dve.wait_ge(step.sem, step.value(-1))
                        ins = stt(o, conv_in[s][:, a, 0:T - d],
                                  vcol("ssd_conv_w", j * 2 + ((3 - d) * SSD_XBC // P + a)), o, ALU.mult, ALU.add)
                        if d < 3 or a == 0:
                            ins.then_inc(step.sem, step.plus())
                ins.then_inc(conv_done.sem, conv_done.plus())

            units(3, conv_xbc, 0, evacuated=1, conv_base=1, conv_done=1, vec_step=5)
            dve.wait_ge(extras.sem, extras.next(EXTRAS))
            ang, turns = scr(5632, T), scr(5888, T)
            v.tensor_copy(ang, scr(6400, T).bitcast(I32)).then_inc(step.sem, step.plus())
            dve.wait_ge(step.sem, step.value())
            ts(ang, ang, freq_col, None, ALU.mult).then_inc(step.sem, step.plus())
            dve.wait_ge(step.sem, step.value())
            ts(turns, ang, 1.0 / (2 * math.pi), ROUND, ALU.mult, ALU.add).then_inc(step.sem, step.plus())
            dve.wait_ge(step.sem, step.value())
            ts(turns, turns, -ROUND, None, ALU.add).then_inc(step.sem, step.plus())
            dve.wait_ge(step.sem, step.value())
            stt(ang, turns, -TWO_PI_HI, ang, ALU.mult, ALU.add).then_inc(step.sem, step.plus())
            dve.wait_ge(step.sem, step.value())
            stt(ang, turns, -TWO_PI_LO, ang, ALU.mult, ALU.add).then_inc(step.sem, step.plus())
            dve.wait_ge(step.sem, step.value())
            ts(ang, ang, 3.1415925, -3.1415925, ALU.min, ALU.max).then_inc(trig_in.sem, trig_in.plus())
            lam = scr(6656, 4, 64)
            for i in range(2):
                tt(lam[:, 2 * i, :], lam[:, 2 * i, :], lam[:, 2 * i + 1, :], ALU.mult).then_inc(step.sem, step.plus())
                dve.wait_ge(step.sem, step.value())
                v.tensor_reduce(cols[:, 6 + i:7 + i], lam[:, 2 * i, :], AX_X, ALU.add).then_inc(lam_in.sem, lam_in.plus())
            dve.wait_ge(half_sin.sem, half_sin.next())
            tt(cos[:], cos[:], cos[:], ALU.mult).then_inc(step.sem, step.plus())
            dve.wait_ge(step.sem, step.value())
            ts(cos[:], cos[:], -2.0, 1.0, ALU.mult, ALU.add).then_inc(step.sem, step.plus())
            dve.wait_ge(lam_exp.sem, lam_exp.next())
            tt(lam_col, cols[:, 5:6], cols[:, 4:5], ALU.subtract).then_inc(step.sem, step.plus())
            dve.wait_ge(step.sem, step.value())
            ts(lam_col, lam_col, -LAMBDA_INIT, None, ALU.add).then_inc(step.sem, step.plus())
            ts(subln_col, vcol("attn_subln_g", 0), 1.0 - LAMBDA_INIT, None, ALU.mult).then_inc(step.sem, step.plus())
            d_skip = heads[:, 2, :].rearrange("p (t q) -> p t q", q=2)
            for q in range(2):
                rng = slice(64 * q, 64 * q + 64)
                v.tensor_copy(heads[rng, 3, 0:16], d_skip[rng, :, q]).then_inc(step.sem, step.plus())

            units(3, conv_xbc, 3, evacuated=1, conv_base=1, conv_done=1, vec_step=5)
            small_weights(SSD_HEADS)
            norm_small(SSD_HEADS)
            softplus(False, heads[:, 0, :], SSD_HEADS)
            v.tensor_copy(dt_tok.rearrange("p (a n) -> p a n", a=TH), sp[7]).then_inc(small_free.sem, small_free.plus())
            dve.wait_ge(small_free.sem, small_free.value())
            dve.wait_ge(decay_rate.sem, decay_rate.next())
            stt(dA.rearrange("p (a n) -> p a n", a=TH), sp[7], -1.0, rows(heads[:, 1, :], TH),
                                   ALU.mult, ALU.mult).then_inc(dA_ready.sem, dA_ready.plus())
            units(3, conv_xbc, 6, evacuated=1, conv_base=1, conv_done=1, vec_step=5)
            dve.wait_ge(cumsum_done.sem, cumsum_done.next())
            v.tensor_copy(a_cs, ps[:, STAT, 0:64]).then_inc(step.sem, step.plus())
            dve.wait_ge(step.sem, step.value())
            tt(dec, ps[:, STAT, 64:96], a_cs[:, 0:32], ALU.subtract).then_inc(decay_in.sem, decay_in.plus())
            dve.wait_ge(decay_done.sem, decay_done.next())
            tt(dt_dec, dt_tok[:, 0:32], dec, ALU.mult).then_inc(step.sem, step.plus())
            units(3, conv_xbc, 9, evacuated=1, conv_base=1, conv_done=1, vec_step=5)
            one_unit(to_proj(0), 0)
            dve.wait_ge(turned.sem, turned.next())
            v.tensor_copy(flat(b_tok), ps[:, 0, :]).then_inc(bank_free.sem, bank_free.plus())
            dve.wait_ge(cb_done.sem, cb_done.next())
            for a in range(TH):
                ins = tt(cb[:, :, a, :], bank(1 + a, 4), rows(upper[:], 4), ALU.mult)
            ins.then_inc(cb_read.sem, cb_read.plus())
            dve.wait_ge(in_ready.sem, in_ready.next(12))

            def x_first(g, b=0):
                hs = slice(8 * g, 8 * g + 8)
                dve.wait_ge(turned.sem, turned.next())
                b0 = bank(b, 8)
                tt(x_dt[g % 2][0], b0, each(dt_tok[:, hs], 64), ALU.mult).then_inc(step.sem, step.plus())
                tt(x_dec[g % 2], b0, each(dt_dec[:, hs], 64), ALU.mult).then_inc(bank_free.sem, bank_free.plus())

            def x_second(g, b=0):
                dve.wait_ge(turned.sem, turned.next())
                tt(x_dt[g % 2][1], bank(b, 8),
                   each(dt_tok[:, 32 + 8 * g:40 + 8 * g], 64), ALU.mult).then_inc(x_dt_ready.sem, x_dt_ready.plus())

            def segments(p):
                dve.wait_ge(rows_done.sem, rows_done.next())
                if y_old.due():
                    dve.wait_ge(y_old.sem, y_old.value())
                for q in range(2):
                    for a in range(TH):
                        col, at = 32 * a + 2 * p + q, (2 * q + a) * P
                        ins = ts(seg[p % 3][:, q, a * P:(a + 1) * P], ps[:, 1 + p % 3, at:at + P],
                                 a_cs[:, col:col + 1], 0.0, ALU.subtract, ALU.min)
                ins.then_inc(seg_ready.sem, seg_ready.plus())

            def mask(p):
                g = p // 4
                dve.wait_ge(decay_ready.sem, decay_ready.next())
                m = seg[p % 3]
                tt(m, m, rows(flat(cb[:, g, :, :]), 2), ALU.mult).then_inc(step.sem, step.plus())
                dve.wait_ge(row_exp.sem, row_exp.next())
                tt(row_e[p % 3], row_e[p % 3], rows(proj[:, 36 + g, P:T], 2),
                   ALU.mult).then_inc(mask_ready.sem, mask_ready.plus())

            def take_y(p):
                dve.wait_ge(y_done.sem, y_done.next())
                t = proj[:, 16 + p, :]
                stt(t, t, heads[:, 3, p:p + 1], ps[:, 7, 0:T], ALU.mult, ALU.add).then_inc(y_read.sem, y_read.plus())

            def gate(p):
                if p % 2 == 0:
                    dve.wait_ge(z_ready.sem, z_ready.next())
                dve.wait_ge(y_read.sem, y_read.value())
                t = proj[:, 16 + p, :]
                tt(t, t, proj[:, p, :], ALU.mult).then_inc(gated.sem, gated.plus())

            x_first(0, 3)
            x_second(0, 7)
            one_unit(to_proj(0), 1)
            segments(0)
            gates = woven(Z_WOVEN, to_proj(0), 2)
            for p in range(SSD_PAIRS):
                if p + 1 < SSD_PAIRS:
                    segments(p + 1)
                if p:
                    take_y(p - 1)
                mask(p)
                if p:
                    gate(p - 1)
                if p // 4 + 1 < SSD_GROUPS:
                    if p % 4 == 1:
                        x_first(p // 4 + 1)
                    elif p % 4 == 2:
                        x_second(p // 4 + 1)
                gates(p)
            take_y(SSD_PAIRS - 1)
            gate(SSD_PAIRS - 1)
            dve.wait_ge(group_rstd.sem, group_rstd.next())

            def norm_group(j):
                if j % 2 == 0:
                    for t in range(2 * j, 2 * j + 4):
                        ins = stt(proj[:, 16 + t, :], proj[:, 16 + t, :], vcol("ssd_norm_g", t),
                                  group_rs[:, j // 2, :], ALU.mult, ALU.mult)
                    ins.then_inc(source_ready.sem, source_ready.plus())

            downs(8, proj[:, 16:32, :], prepare=norm_group)
            norm("norm_ffn_g", 0, residual())
            ffn(conv=0)

            norm("norm_mix_g", DK, residual())
            units(12, to_proj(0), evacuated=1)
            dve.wait_ge(evacuated.sem, evacuated.value())
            norm("mem_norm_2", 0, renew=None, src=mem_raw, sq=mem_squares, total=mem_partial)

            def to_memory(j, s):
                l, i = j // 4, j % 4
                evacuate(mem_k[:, l, 2 * i:2 * i + 2, :] if i < 2
                         else proj[:, 32 + 4 * l + 2 * i - 4:32 + 4 * l + 2 * i - 2, :], s)

            for j in range(4):
                one_unit(to_memory, j)
            kv_units = woven(KV_ROPE, to_memory, 4)
            for j in range(8):
                t = proj[:, 2 * j:2 * j + 2, :]
                if j % 4 == 0:
                    dve.wait_ge(qk_rstd.sem, qk_rstd.next())
                stt(t, t, vcol("attn_q_norm_g" if j < 4 else "attn_k_norm_g", 0), qk_rn[j // 4][:, 2 * (j % 4):2 * (j % 4) + 2, :],
                    ALU.mult, ALU.mult).then_inc(qk_normed.sem, qk_normed.plus())
                dve.wait_ge(qk_normed.sem, qk_normed.value())
                tt(qk_a, t, rows(cos[:], 2), ALU.mult).then_inc(step.sem, step.plus())
                dve.wait_ge(qk_swapped.sem, qk_swapped.next())
                tt(qk_b, bank(j % 4), rows(sin[:], 2), ALU.mult).then_inc(step.sem, step.plus())
                dve.wait_ge(step.sem, step.value())
                tt(t, qk_a, qk_b, ALU.add).then_inc(qk_rotated.sem, qk_rotated.plus())
                kv_units(j)
            copy_values([v_tok[:, a, 512 * b:512 * b + 512] for a in range(TH) for b in range(2)], 0)
            softmax_attention("diff", woven(KV_WOVEN, to_memory, 4 + KV_ROPE))
            copy_values([mem_v[:, l, a, :] for l in range(2) for a in range(TH)], 4)
            dve.wait_ge(o_rstd.sem, o_rstd.next())
            o = proj[:, 24:32, :]
            stt(o, o, subln_col, wide_b, ALU.mult, ALU.mult).then_inc(source_ready.sem, source_ready.plus())
            downs(4, proj[:, 24:32, :])
            norm("norm_ffn_g", DK, residual())
            ffn(conv=1)
            norm("ffn_norm_2", 0, residual())
            ffn()

            norm("mix_norm_2", 0, residual(0.5))
            units(2, to_proj(24), evacuated=1)
            one_unit(to_proj(8), 0)
            softmax_attention("mem0", woven(A_WOVEN, to_proj(8), 1))
            units(7 - A_WOVEN, to_proj(8), 1 + A_WOVEN, evacuated=1)
            dve.wait_ge(out_read.sem, out_read.next(ATT_HEADS + MEM_HEADS))
            for j in range(2):
                feed(proj[:, 36:40, :], j, (slot[0] + j) % RING)
            dve.wait_ge(evacuated.sem, evacuated.value())
            cu = proj[:, 8:16, :]
            tt(cu, cu, proj[:, 16:24, :], ALU.mult).then_inc(gated_input.sem, gated_input.plus())
            dve.wait_ge(su_done.sem, su_done.next())
            split_next()
            dve.wait_ge(conv_base.sem, conv_base.next())
            for d in (1, 2):
                for k in range(DK):
                    o = proj[:, 28 + k, d:T]
                    stt(o, proj[:, 8 + k, 0:T - d], vcol("a_conv_w_2", (2 - d) * DK + k), o,
                        ALU.mult, ALU.add).then_inc(step.sem, step.plus())
                if d == 1:
                    dve.wait_ge(su_done.sem, su_done.next())
                    split_next()
                dve.wait_ge(step.sem, step.value())
            units(4, to_proj(0), evacuated=1)
            dve.wait_ge(evacuated.sem, evacuated.value())

            def gate_convolved(j):
                o = proj[:, 28 + 2 * j:30 + 2 * j, :]
                tt(o, o, proj[:, 2 * j:2 * j + 2, :], ALU.mult).then_inc(source_ready.sem, source_ready.plus())

            downs(4, proj[:, 28:36, :], prepare=gate_convolved)
            norm("ffn_norm_2", DK, residual())
            ffn()

            norm("kv_norm_2", 0, residual(0.5))
            units(8, to_proj(0), evacuated=1)
            small_weights(FOX_HEADS)
            norm_small(FOX_HEADS)
            norm("ffn_norm_2", 2 * DK, stats=False, renew=None)
            softplus(True, gate_bias, FOX_HEADS)
            ts(log_f, sp[7][:, :, 0:FOX_HEADS], -1.0, None, ALU.mult).then_inc(log_f_ready.sem, log_f_ready.plus())
            ffn()
            dve.wait_ge(cum_f_done.sem, cum_f_done.next())
            v.tensor_copy(cum_f, ps[:, STAT, 0:16].rearrange("p (a h) -> p a h", a=TH)).then_inc(cum_f_read.sem, cum_f_read.plus())

            norm("mix_norm_2", DK, residual(0.5))
            units(2, to_proj(24), evacuated=1)
            one_unit(to_proj(16), 0)
            softmax_attention("mem1", woven(B_WOVEN, to_proj(16), 1))
            copy_values([v_tok[:, a, 512 * b:512 * b + 512] for a in range(TH) for b in range(2)], 0)
            softmax_attention("fox")
            dve.wait_ge(out_read.sem, out_read.next(MEM_HEADS + FOX_HEADS))
            downs(6, proj[:, 28:40, :], MIXED_ORDER)
            norm("ffn_norm_2", 3 * DK, residual())
            ffn()

            take = residual(0.5)
            for b in range(4):
                take(b)
            dve.wait_ge(squares_made.sem, squares_made.next(DK))
            v.tensor_reduce(partial, squares.rearrange("p k t -> p t k"), AX_X, ALU.add).then_inc(sums_ready.sem, sums_ready.plus())
            dve.wait_ge(turned.sem, turned.next(4))
            dve.wait_ge(rstd_ready.sem, rstd_ready.next())
            for a in range(TH):
                for b in range(2):
                    ts(out_tok[:, a, 512 * b:512 * b + 512], ps[:, 2 * a + b, :], cols[:, 8 + a:9 + a], None,
                       ALU.mult).then_inc(final_ready.sem, final_ready.plus())


def kernel(**inputs):
    import concourse.bacc as _bacc
    from concourse import mybir as _mybir
    from concourse.bass_utils import run_bass_kernel_spmd as _run

    nc = _bacc.Bacc("TRN2", target_bir_lowering=False, num_devices=1)
    arrays, args = {}, {}
    for name, value in inputs.items():
        a = np.ascontiguousarray(value)
        arrays[f"in_{name}_dram"] = a
        args[name] = nc.dram_tensor(f"in_{name}_dram", a.shape, _mybir.dt.from_np(a.dtype),
                                    kind="ExternalInput").ap()
    out = nc.dram_tensor("out_0_dram", (1, T, D), F32, kind="ExternalOutput").ap()
    build_program(nc, args, out)
    r = _run(nc, [arrays], core_ids=[0])
    return r.results[0]["out_0_dram"]
```

```python
import math
from contextlib import ExitStack, contextmanager

import numpy as np

import concourse.bass as bass
from concourse import mybir

F32 = mybir.dt.float32
F32R = mybir.dt.float32r
I32 = mybir.dt.int32
ACT = mybir.ActivationFunctionType
ALU = mybir.AluOpType
AX_X = mybir.AxisListType.X

P = 128
T = 256
TH = T // P
D = 1024
DK = D // P
EPS = 1e-6
RING = 3

Z_WOVEN = 4
KV_WOVEN = 3
A_WOVEN = 4
B_WOVEN = 3
MIXED_ORDER = (4, 5, 0, 1, 2, 3)

SSD_INNER, SSD_GROUPS, SSD_STATE, SSD_HEADS, SSD_HD, SSD_TAPS = 2048, 4, 128, 32, 64, 4
SSD_PAIRS = SSD_HEADS // 2
TURNED_BEFORE_DIFF = 4 + 2 + 1 + TH * SSD_GROUPS + 4
SSD_XBC = SSD_INNER + 2 * SSD_GROUPS * SSD_STATE
FF = 2816
FT = FF // P
FU = FT // 2
ATT_HEADS, ATT_HD = 8, 64
ROPE_HALF, THETA = 8, 500000.0
LAMBDA_INIT = 0.8 - 0.6 * math.exp(-0.3)
MEM_HEADS, FOX_HEADS = 4, 8
MASKED = -3.0e38
TWO_PI_HI = 6.28125
TWO_PI_LO = 2 * math.pi - 6.28125
ROUND = 1.5 * 2.0 ** 23


class Tally:

    def __init__(self, sem, start, step):
        self.sem, self.n, self.step, self.loop, self.per = sem, start, step, None, 0

    def value(self, ahead=0):
        v = (self.n + ahead) * self.step
        return v if self.loop is None else v + self.loop * (self.per * self.step)

    def plus(self):
        self.n += 1
        return self.step

    def next(self, n=1):
        self.n += n
        return self.value()

    def due(self, n=1):
        self.n += n
        return self.loop is not None or self.n > 0


class Counts:

    def __init__(self, eng, sem):
        self.eng, self.sem, self.all = eng, sem, {}

    def __call__(self, name, start=0, step=1):
        t = self.all.get((name, start))
        if t is None:
            t = self.all[(name, start)] = Tally(self.sem(name), start, step)
        return t

    @contextmanager
    def repeat(self, trips, counts):
        starts = {t: t.n for t in self.all.values()}
        with self.eng.Fori(0, trips) as i:
            for t, per in counts.items():
                t.loop, t.per = i, per
            yield i
        for t, n in starts.items():
            per = counts.get(t, 0)
            assert t.n - n == per, (str(t.sem), t.n - n, per)
            t.n = n + per * trips
            t.loop = None


VECTOR_ROWS = [
    ("norm_mix_g", 2 * DK), ("norm_ffn_g", 2 * DK), ("ffn_norm_2", 4 * DK), ("mix_norm_2", 2 * DK),
    ("mem_norm_2", DK), ("kv_norm_2", DK), ("final_norm_2", DK), ("ssd_norm_g", SSD_INNER // P),
    ("ssd_conv_w", SSD_TAPS * SSD_XBC // P), ("ssd_conv_b", SSD_XBC // P),
    ("ffn_conv_w", 2 * 3 * 2 * FT), ("ffn_conv_b", 2 * 2 * FT), ("a_conv_w_2", 3 * DK),
    ("attn_subln_g", 1), ("attn_q_norm_g", 1), ("attn_k_norm_g", 1),
]
VECTOR_ROWS.append(("pad", -sum(n for _, n in VECTOR_ROWS) % P))
COL = {}
_n = 0
for _name, _rows in VECTOR_ROWS:
    COL[_name] = _n
    _n += _rows
VECTORS = _n
VBLOCKS = -(-VECTORS // P)

STREAM = [
    ("up", "ssd_in_w", (0,), 8, 12), ("up", "ssd_in_w", (0,), 0, 8),
    ("down", "ssd_out_w", (0,), 0, 8),
    ("ffn", ("ffn_up_w", "ffn_down_w"), (0,), 0, 3 * FU),
    ("up", "attn_in_w", (0,), 0, 12),
    ("up", "mem_w_kv_2", (0,), 0, 4), ("up", "mem_w_kv_2", (1,), 0, 4),
    ("down", "attn_out_w", (0,), 0, 4),
    ("ffn", ("ffn_up_w", "ffn_down_w"), (1,), 0, 3 * FU),
    ("ffn", ("ffn_w_gate_up_2", "ffn_w_down_2"), (0, 0), 0, 3 * FU),
    ("up", "a_w_in_2", (0,), 12, 2), ("up", "a_w_in_2", (0,), 4, 8),
    ("down", "a_w_out_2", (0,), 4, 2),
    ("up", "a_w_in_2", (0,), 0, 4), ("down", "a_w_out_2", (0,), 0, 4),
    ("ffn", ("ffn_w_gate_up_2", "ffn_w_down_2"), (0, 1), 0, 3 * FU),
    ("up", "w_kvf_2", (), 0, 8),
    ("ffn", ("ffn_w_gate_up_2", "ffn_w_down_2"), (1, 0), 0, 3 * FU),
    ("up", "b_w_q_2", (0,), 4, 2), ("up", "b_w_q_2", (0,), 0, 4),
    ("down", "b_w_out_2", (0,), 4, 2), ("down", "b_w_out_2", (0,), 0, 4),
    ("ffn", ("ffn_w_gate_up_2", "ffn_w_down_2"), (1, 1), 0, 3 * FU),
]
UNITS = sum(s[4] for s in STREAM)

POOL_MADE = 9 + 2 + ROPE_HALF + 3 + 1 + 4
EARLY_EXTRAS, EXTRAS = 4, 9


def vector_loads():
    loads, row = [], 0
    for name, n in VECTOR_ROWS:
        at = 0
        while at < n:
            k = min(n - at, P - row % P)
            loads.append((name, at, k, row))
            at += k
            row += k
    return loads


LOADS = vector_loads()
HALVES = ("attn_q_norm_g", "attn_k_norm_g")
LOADED_FIRST = sum(row < P for _, _, _, row in LOADS)
LOADED_LATER = len(LOADS) - LOADED_FIRST + len(HALVES)


def build_program(nc, A, out):
    with ExitStack() as ctx:
        def sb(name, shape, dt=F32):
            return ctx.enter_context(nc.sbuf_tensor(name, shape, dt))

        sems = {}

        def sem(name):
            if name not in sems:
                sems[name] = ctx.enter_context(nc.semaphore(name))
            return sems[name]

        raw = sb("raw_weights", [P, RING, 2048])
        w_hi = sb("weights_hi", [P, RING, 2048], F32R)
        w_lo = sb("weights_lo", [P, RING, 2048], F32R)
        act_hi = sb("down_in_hi", [P, RING, 2, T], F32R)
        act_lo = sb("down_in_lo", [P, RING, 2, T], F32R)
        x = sb("residual", [P, DK, T])
        h_hi = sb("normed_hi", [P, DK, T], F32R)
        h_lo = sb("normed_lo", [P, DK, T], F32R)
        proj = sb("proj", [P, 40, T])
        mem_k = sb("mem_k", [P, 2, MEM_HEADS, T])
        mem_v = sb("mem_v", [P, 2, TH, MEM_HEADS * P])
        vec = sb("vectors", [P, VBLOCKS * P])
        rstd = sb("rstd", [P, T])
        small_raw = sb("small_w_raw", [P, DK, 32])
        small_hi = sb("small_w_hi", [P, DK, 32], F32R)
        small_lo = sb("small_w_lo", [P, DK, 32], F32R)
        ident = sb("ident", [P, P])
        ones = sb("ones", [P, P])
        upper = sb("upper", [P, P])
        half_ones = sb("half_ones", [P, P])
        swap = sb("rope_swap", [P, P])
        chunk_mask = sb("chunk_mask", [P, T])
        causal_mask = sb("causal_mask", [P, T])
        cos = sb("cos", [P, T])
        sin = sb("sin", [P, T])
        cols = sb("columns", [P, 64])
        eps_col, lam_col, subln_col, freq_col = (cols[:, i:i + 1] for i in range(4))
        log_f = cols[:, 16:32].rearrange("p (a h) -> p a h", a=TH)
        cum_f = cols[:, 32:48].rearrange("p (a h) -> p a h", a=TH)
        gate_bias = cols[:, 48:56]
        heads = sb("head_rows", [P, 4, 32])
        S = sb("scratch", [P, 7168])

        def scr(at, *shape):
            n = int(np.prod(shape))
            assert at + n <= 7168
            v = S[:, at:at + n]
            if len(shape) == 1:
                return v
            names = "abc"[:len(shape)]
            return v.rearrange("p (" + " ".join(names) + ") -> p " + " ".join(names),
                               **{names[i]: shape[i] for i in range(1, len(shape))})

        ps = ctx.enter_context(nc.psum_tensor("ps", [P, 8, 512], F32))
        STAT = 7

        mem_squares, mem_partial = proj[:, 24:32, :], proj[:, 32, :]

        squares = scr(0, DK, T)
        partial = scr(2048, T)
        f_in = scr(2304, 2, 2, T)
        f_out = scr(3328, 2, 2, T)
        hidden = scr(4352, 2, T)
        conv_in = [scr(2304 + 512 * s, 2, T) for s in range(RING)]
        conv_out = [scr(3840 + 512 * s, 2, T) for s in range(RING)]
        freq_row = scr(7040, P)[0:1, :]
        mem_flat = mem_v[:].rearrange("p l a n -> p (l a n)")
        mem_raw = mem_k[:].rearrange("p l h t -> p (l h) t")
        x_dt = [[scr(1024 * g + 512 * a, 8, 64) for a in range(TH)] for g in range(2)]
        state = [scr(2048 + 512 * g, 512) for g in range(2)]
        cb = scr(3072, 4, TH, P)
        b_tok = scr(4096, 4, P)
        x_dec = [scr(4608 + 512 * g, 8, 64) for g in range(2)]
        seg = [mem_flat[:, 512 * i:512 * i + 512].rearrange("p (q n) -> p q n", q=2) for i in range(3)]
        row_e = [scr(5632 + 256 * i, 2, P) for i in range(3)]
        group_rs = scr(0, SSD_GROUPS, T)
        dt_tok, dA, a_cs = scr(6784, 64), scr(6848, 64), scr(6912, 64)
        dt_dec, dec = scr(6976, 32), scr(7008, 32)
        small_sum = scr(6144, T)
        sp = [scr(5632 + 64 * i, TH, 32) for i in range(8)]
        v_tok = scr(0, TH, 1024)
        s_buf = [scr(2048 + 512 * i, 2, T) for i in range(2)]
        p_buf = [scr(3072 + 512 * i, 2, T) for i in range(2)]
        probs = [scr(4096 + 256 * i, T) for i in range(2)]
        probs_t = [scr(4608 + 256 * i, T) for i in range(2)]
        tiny = [scr(5120 + 16 * i, 8, 2) for i in range(2)]
        key_row = [scr(5248, P), scr(5376, T)]
        qk_sq = [scr(0, 8, T), scr(4096, 8, T)]
        qk_rn = [scr(2048, 8, T), scr(4096, 8, T)]
        qk_a, qk_b = scr(6144, 2, T), scr(6656, 2, T)
        o_rs = [proj[:, 4 * i:4 * i + 4, :] for i in range(2)]
        o_sq = [proj[:, 8 + 4 * i:12 + 4 * i, :] for i in range(2)]
        out_tok = scr(2304, TH, D)
        gained = proj[:, 0:DK, :]

        OUT = out.rearrange("b (a p) n -> p (b a) n", p=P)

        def rows(ap, n):
            return ap.unsqueeze(1).broadcast_to([P, n, ap.shape[-1]])

        def each(ap, n):
            return ap.unsqueeze(2).broadcast_to([P, ap.shape[-1], n])

        def flat(ap):
            return ap.rearrange("p k t -> p (k t)")

        def bank(b, n=2):
            return ps[:, b, :].rearrange("p (k t) -> p k t", k=n)

        def arr(name, idx):
            a = A[name]
            for i in idx:
                a = a[i]
            return a

        def vcol(name, i):
            return vec[:, bass.ds(COL[name] + i, 1)]

        def attention(kind):
            return {"diff": (ATT_HEADS, 0, 24, ATT_HD ** -0.5), "fox": (FOX_HEADS, 16, 28, P ** -0.5),
                    "mem0": (MEM_HEADS, 24, 36, P ** -0.5), "mem1": (MEM_HEADS, 24, 36, P ** -0.5)}[kind]

        def keys_of(kind, a):
            return T if kind.startswith("mem") else P * (a + 1)

        group_squares = [proj[:, 4 * g:4 * g + 4, :] for g in range(SSD_GROUPS)]

        block = ctx.enter_context(nc.Block())

        @block.sync
        def _(sp_eng):
            sp = sp_eng
            c = Counts(sp, sem)
            final_ready = c("final_ready")
            second_ready = c("second_ready")
            lo_split = c("lo_split", -RING)
            stored = c("stored", step=16)
            x_staged = c("x_staged", step=16)
            first_staged = c("first_staged", step=16)
            staged = c("staged", step=16)
            mem_staged = c("mem_staged", step=16)
            extras = c("extras_staged", step=16)
            pool_made = c("pool_made")
            y_done = c("y_done")
            landed = [c(f"landed{s}", step=16) for s in range(RING)]
            u = 0

            def load(dst, src, slot):
                if lo_split.due():
                    sp.wait_ge(lo_split.sem, lo_split.value())
                sp.dma_start(dst, src).then_inc(landed[slot].sem, landed[slot].plus())

            def up(w, col, slot):
                load(raw[:, slot, :].rearrange("p (k n) -> p k n", k=DK),
                     w.rearrange("(k p) n -> p k n", p=P)[:, :, bass.ds(col, 256)], slot)

            def down(w, j, slot):
                load(raw[:, slot, :].rearrange("p (j k n) -> p j k n", j=1, k=2),
                     w.rearrange("(j k p) n -> p j k n", k=2, p=P)[:, bass.ds(j, 1), :, :], slot)


            vrows = flat(proj[:, 24:27, :])
            sp.dma_start(flat(proj[:, 0:8, :]).rearrange("p (a n) -> p a n", a=TH),
                          A["x"][0].rearrange("(a p) n -> p a n", p=P)).then_inc(x_staged.sem, x_staged.plus())

            def load_vector(name, at, k, row):
                landing = first_staged if row < P else staged
                dst = vrows[row % P:row % P + k, row // P * P:row // P * P + P]
                if name in HALVES:
                    for half in range(2):
                        sp.dma_start(dst[:, 64 * half:64 * half + 64],
                                      A[name]).then_inc(landing.sem, landing.plus())
                    return
                src = A["ffn_conv_b" if name == "pad" else name]
                while len(src.shape) > 1:
                    dims = " ".join(f"d{i}" for i in range(len(src.shape)))
                    src = src.rearrange(f"{dims} -> ({dims})")
                src = src.rearrange("(r q) -> r q", q=P)
                sp.dma_start(dst, src[at:at + k, :]).then_inc(landing.sem, landing.plus())

            for vector in LOADS[:LOADED_FIRST]:
                load_vector(*vector)

            def load_rest():
                for vector in LOADS[LOADED_FIRST:]:
                    load_vector(*vector)
                assert (first_staged.n, staged.n) == (LOADED_FIRST, LOADED_LATER)
                for i, name in enumerate(("ssd_dt_bias", "ssd_a_log", "ssd_d")):
                    sp.dma_start(heads[:, i, :],
                                 A[name].broadcast_to([P, SSD_HEADS])).then_inc(extras.sem, extras.plus())
                sp.wait_ge(pool_made.sem, pool_made.next(POOL_MADE))
                sp.dma_start(gate_bias,
                             A["b_f_2"].unsqueeze(0).broadcast_to([P, FOX_HEADS])).then_inc(extras.sem, extras.plus())
                assert extras.n == EARLY_EXTRAS
                sp.dma_start(small_raw[:], A["ssd_in_w"][0].rearrange("(k p) n -> p k n", p=P)
                              [:, :, SSD_INNER + SSD_XBC:]).then_inc(sem("small_landed"), 16)

            def load_late():
                sp.wait_ge(y_done.sem, SSD_PAIRS)
                sp.dma_start(mem_flat.rearrange("p (a n) -> p a n", a=TH),
                              A["mem_2"][0].rearrange("(a p) n -> p a n",
                                                      p=P)).then_inc(mem_staged.sem, mem_staged.plus())
                sp.dma_start(scr(6400, T).bitcast(I32),
                             A["positions"].broadcast_to([P, T])).then_inc(extras.sem, extras.plus())
                for i, name in enumerate(("attn_lq1", "attn_lk1", "attn_lq2", "attn_lk2")):
                    sp.dma_start(scr(6656, 4, 64)[:, i, :],
                                 A[name].broadcast_to([P, ATT_HD])).then_inc(extras.sem, extras.plus())

            for kind, name, idx, first, n in STREAM:
                counts = {lo_split: RING, **{t: 1 for t in landed}}
                if kind == "ffn":
                    wu, wd = arr(name[0], idx), arr(name[1], idx)
                    up(wu, 0, u % RING)
                    up(wu, FF, (u + 1) % RING)
                    with c.repeat(FU - 1, counts) as i:
                        up(wu, i * 256 + 256, (u + 2) % RING)
                        up(wu, i * 256 + (256 + FF), u % RING)
                        down(wd, i, (u + 1) % RING)
                    down(wd, FU - 1, (u + 2) % RING)
                    u += 3 * FU
                    continue
                if name == "attn_in_w":
                    load_late()
                w = arr(name, idx)

                def load_unit(j, slot):
                    if kind == "up":
                        up(w, j * 256, slot)
                    else:
                        down(w, j, slot)

                peeled = max(RING - u, 0)
                trips = (n - peeled) // RING
                trips = trips if trips > 1 else 0
                for j in range(peeled):
                    load_unit(first + j, (u + j) % RING)
                if peeled:
                    load_rest()
                if trips:
                    with c.repeat(trips, counts) as i:
                        for j in range(RING):
                            load_unit(i * RING + (first + peeled + j), (u + peeled + j) % RING)
                for j in range(peeled + trips * RING, n):
                    load_unit(first + j, (u + j) % RING)
                u += n
            assert u == UNITS
            sp.wait_ge(final_ready.sem, final_ready.next(2))
            sp.dma_start(OUT[:, 0, :], out_tok[:, 0, :]).then_inc(stored.sem, stored.plus())
            sp.wait_ge(second_ready.sem, second_ready.next(2))
            sp.dma_start(OUT[:, 1, :], out_tok[:, 1, :]).then_inc(stored.sem, stored.plus())
            sp.wait_ge(stored.sem, stored.value())

        @block.gpsimd
        def _(pool):
            g = nc.gpsimd
            made = Counts(pool, sem)("pool_made")

            def fill(view, value):
                pool.wait_ge(made.sem, made.value())
                g.memset(view, value).then_inc(made.sem, made.plus())

            for m, v in ((ident, 0.0), (ones, 1.0), (upper, 1.0), (half_ones, 0.0), (swap, 0.0),
                         (chunk_mask, 0.0), (causal_mask, 0.0), (cols, EPS)):
                fill(m[:], v)
            fill(freq_row, 0.0)
            for a in range(2):
                fill(half_ones[64 * a:64 * a + 64, 64 * a:64 * a + 64], 1.0)
            row = freq_row.rearrange("p (a b c j) -> p a b c j", a=2, b=4, c=2)[:, :, 0, :, :]
            for j in range(ROPE_HALF):
                fill(row[:, :, :, j], float(np.float32(THETA) ** np.float32(-2.0 * j / (2 * ROPE_HALF))))

            def select(view, pattern, base, mult, value, op=ALU.not_equal):
                pool.wait_ge(made.sem, made.value())
                g.affine_select(out=view, in_=view, compare_op=op, fill=value, base=base, pattern=pattern,
                                channel_multiplier=mult).then_inc(made.sem, made.plus())

            select(ident[:], [[-1, P]], 0, 1, 1.0)
            select(upper[:], [[1, P]], 0, -1, 0.0, ALU.is_ge)
            select(causal_mask[:, P:T], [[-1, P]], 0, 1, MASKED, ALU.is_ge)
            fill(chunk_mask[0:64, P + 64:T], MASKED)
            for b in (0, 64):
                select(swap[:, b:b + 8], [[-1, 8]], -(b + 8), 1, -1.0)
                select(swap[:, b + 8:b + 16], [[-1, 8]], -b, 1, 1.0)
            assert made.n == POOL_MADE

        @block.tensor
        def _(pe):
            mm = nc.tensor.matmul
            c = Counts(pe, sem)
            bank_free = c("bank_free")
            bank_summed = c("bank_summed")
            cb_read = c("cb_read")
            first_staged = c("first_staged", step=16)
            mem_staged = c("mem_staged", step=16)
            cb_done = c("cb_done")
            cum_f_done = c("cum_f_done")
            cum_f_read = c("cum_f_read")
            cumsum_done = c("cumsum_done")
            dA_ready = c("dA_ready")
            decay_in = c("decay_in")
            first_scored = c("first_scored")
            evacuated = c("evacuated")
            freq_done = c("freq_done")
            group_sum = c("group_sum")
            h_ready = c("h_ready")
            hid_ready = c("hid_ready")
            in_ready = c("in_ready")
            lo_split = c("lo_split")
            log_f_ready = c("log_f_ready")
            mask_ready = c("mask_ready")
            o_squares = c("o_squares")
            o_summed = c("o_summed")
            out_done = c("out_done")
            out_read = c("out_read", -1)
            pool_made = c("pool_made")
            probs_copied = c("probs_copied")
            probs_ready = c("probs_ready")
            probs_turned = c("probs_turned")
            qk_normed = c("qk_normed")
            qk_logs = c("qk_logs")
            qk_rotated = c("qk_rotated", -4)
            qk_squares = c("qk_squares")
            qk_summed = c("qk_summed")
            qk_swapped = c("qk_swapped")
            rows_done = c("rows_done")
            scored = c("scored")
            setup_read = c("setup_read")
            small_done = c("small_done")
            small_normed = c("small_normed")
            small_turned = c("small_turned")
            final_x = c("final_x")
            small_ready = c("small_ready")
            staged = c("staged", step=16)
            stat_done = c("stat_done")
            state_done = c("state_done")
            state_ready = c("state_ready")
            su_done = c("su_done")
            sums_ready = c("sums_ready")
            turned = c("turned")
            values_copied = c("values_copied")
            x_dt_ready = c("x_dt_ready")
            x_staged = c("x_staged", step=16)
            y_done = c("y_done")
            y_read = c("y_read", -1)
            y_squares = c("y_squares")
            slot = [0]

            def up_unit(first=False, ks=range(DK)):
                s = slot[0]
                if ks[0] == 0:
                    pe.wait_ge(lo_split.sem, lo_split.next())
                    evacuated.n += 1
                wh = w_hi[:, s, :].rearrange("p (k n) -> p k n", k=DK)
                wl = w_lo[:, s, :].rearrange("p (k n) -> p k n", k=DK)
                for k in ks:
                    if first:
                        pe.wait_ge(h_ready.sem, h_ready.next())
                    for a in range(2):
                        o = ps[:, 4 + s, a * T:(a + 1) * T]
                        hi, lo = wh[:, k, a * P:(a + 1) * P], wl[:, k, a * P:(a + 1) * P]
                        mm(o, hi, h_hi[:, k, :], start=(k == 0 and a == 0), stop=False, skip_group_check=True)
                        mm(o, hi, h_lo[:, k, :], start=False, stop=False, skip_group_check=True)
                        last = mm(o, lo, h_hi[:, k, :], start=False, stop=(k == DK - 1), skip_group_check=True)
                if ks[-1] == DK - 1:
                    last.then_inc(su_done.sem, su_done.plus())
                    slot[0] = (s + 1) % RING

            def woven(n):
                def step(t):
                    if t < 2 * n:
                        up_unit(ks=range(t % 2 * DK // 2, (t % 2 + 1) * DK // 2))
                return step

            def down_unit(first=False, last=False):
                s = slot[0]
                pe.wait_ge(lo_split.sem, lo_split.next())
                pe.wait_ge(hid_ready.sem, hid_ready.next())
                wh = w_hi[:, s, :].rearrange("p (k n) -> p k n", k=2)
                wl = w_lo[:, s, :].rearrange("p (k n) -> p k n", k=2)
                for m in range(DK):
                    o = ps[:, m // 2, (m % 2) * T:(m % 2 + 1) * T]
                    for k in range(2):
                        hi, lo = wh[:, k, m * P:(m + 1) * P], wl[:, k, m * P:(m + 1) * P]
                        mm(o, hi, act_hi[:, s, k, :], start=(first and k == 0 and m % 2 == 0), stop=False,
                           skip_group_check=True)
                        mm(o, hi, act_lo[:, s, k, :], start=False, stop=False, skip_group_check=True)
                        ins = mm(o, lo, act_hi[:, s, k, :], start=False, stop=(k == 1), skip_group_check=True)
                    if last and m % 2:
                        ins.then_inc(bank_summed.sem, bank_summed.plus())
                if not last:
                    ins.then_inc(su_done.sem, su_done.plus())
                slot[0] = (s + 1) % RING

            def norm_sum(squares_sum=partial):
                pe.wait_ge(sums_ready.sem, sums_ready.next())
                mm(ps[:, STAT, 0:T], ones[:], squares_sum, start=True,
                   stop=True).then_inc(stat_done.sem, stat_done.plus())

            def more_ups(n):
                trips = n // RING if n >= 2 * RING else 0
                if trips:
                    with c.repeat(trips, {lo_split: RING, evacuated: RING, su_done: RING}):
                        for _ in range(RING):
                            up_unit()
                for _ in range(n - RING * trips):
                    up_unit()

            def second_up(squares_sum=partial):
                up_unit(ks=range(DK // 2))
                norm_sum(squares_sum)
                up_unit(ks=range(DK // 2, DK))

            def ups(n):
                up_unit(first=True)
                second_up()
                more_ups(n - 2)

            def downs(n):
                down_unit(first=True)
                trips = (n - 2) // RING if n >= 2 + 2 * RING else 0
                if trips:
                    with c.repeat(trips, {lo_split: RING, hid_ready: RING, su_done: RING}):
                        for _ in range(RING):
                            down_unit()
                for _ in range(n - 2 - RING * trips):
                    down_unit()
                down_unit(last=True)

            def ffn(stats=True):
                up_unit(first=True)
                if stats:
                    second_up()
                else:
                    turn_small(FOX_HEADS)
                    up_unit()
                up_unit()
                if stats:
                    pe.wait_ge(evacuated.sem, evacuated.value(-2))
                up_unit()
                down_unit(first=True)
                with c.repeat(FU - 2, {lo_split: 3, evacuated: 2, su_done: 3, hid_ready: 1}):
                    up_unit()
                    up_unit()
                    down_unit()
                down_unit(last=True)

            def turn_tiles(b, blocks):
                for j, t in enumerate(blocks):
                    last = nc.tensor.transpose(ps[:, b, j * P:(j + 1) * P], t, ident[:])
                last.then_inc(turned.sem, turned.plus())

            def turn_input(tok):
                for b in range(4):
                    turn_tiles(b, [tok[:, a, (2 * b + j) * P:(2 * b + j + 1) * P]
                                   for j in range(2) for a in range(TH)])

            def small_product(n):
                pe.wait_ge(small_ready.sem, small_ready.next())
                o = ps[0:n, STAT, 0:T]
                for k in range(DK):
                    mm(o, small_hi[:, k, 0:n], h_hi[:, k, :], start=(k == 0), stop=False)
                    mm(o, small_hi[:, k, 0:n], h_lo[:, k, :], start=False, stop=False)
                    last = mm(o, small_lo[:, k, 0:n], h_hi[:, k, :], start=False, stop=(k == DK - 1))
                last.then_inc(small_done.sem, small_done.plus())

            def turn_small(n):
                pe.wait_ge(small_normed.sem, small_normed.next())
                for a in range(TH):
                    last = nc.tensor.transpose(ps[:, STAT, T + 32 * a:T + 32 * a + n],
                                               small_sum[0:n, a * P:(a + 1) * P], ident[0:n, 0:n])
                last.then_inc(small_turned.sem, small_turned.plus())

            def ssd_core():
                pe.wait_ge(in_ready.sem, in_ready.next(12))
                turn_tiles(0, [proj[:, 32 + g, 0:P] for g in range(SSD_GROUPS)])
                for a in range(TH):
                    for g in range(SSD_GROUPS):
                        tok = slice(a * P, (a + 1) * P)
                        last = mm(ps[:, 1 + a, g * P:(g + 1) * P], proj[:, 32 + g, tok], proj[:, 36 + g, tok],
                                  start=True, stop=True)
                last.then_inc(cb_done.sem, cb_done.plus())

                def turn_x(g, a, b=0):
                    turn_tiles(b, [proj[:, 16 + 4 * g + j, a * P:(a + 1) * P] for j in range(4)])

                def new_state(g):
                    pe.wait_ge(x_dt_ready.sem, x_dt_ready.next())
                    mm(ps[:, 0, :], b_tok[:, g, :], flat(x_dec[g % 2]), start=True,
                       stop=True).then_inc(state_done.sem, state_done.plus())

                def head_rows(p):
                    for q in range(2):
                        for a in range(TH):
                            col = 32 * a + 2 * p + q
                            last = mm(ps[:, 1 + p % 3, (2 * q + a) * P:(2 * q + a + 1) * P],
                                      dA[:, col:col + 1].to_broadcast([P, P]), upper[:], start=True, stop=True)
                    last.then_inc(rows_done.sem, rows_done.plus())

                def heads_out(p):
                    g = p // 4
                    pe.wait_ge(mask_ready.sem, mask_ready.next())
                    if p % 4 == 0:
                        pe.wait_ge(state_ready.sem, state_ready.next())
                    if y_read.due():
                        pe.wait_ge(y_read.sem, y_read.value())
                    for q in range(2):
                        h, m = (2 * p + q) % 8, seg[p % 3][:, q, :]
                        o = ps[64 * q:64 * q + 64, 7, :]
                        mm(o[:, 0:P], x_dt[g % 2][0][:, h, :], m[:, 0:P], start=True, stop=True)
                        mm(o[:, P:T], x_dt[g % 2][1][:, h, :], m[:, P:T], start=True, stop=False)
                        last = mm(o[:, P:T], state[g % 2][:, 64 * h:64 * h + 64], row_e[p % 3][:, q, :],
                                  start=False, stop=True)
                    last.then_inc(y_done.sem, y_done.plus())

                def square_sum(g, b, half):
                    pe.wait_ge(y_squares.sem, y_squares.next())
                    for j in range(4):
                        last = mm(ps[:, b, half * T:(half + 1) * T], ones[:], group_squares[g][:, j, :],
                                  start=(j == 0), stop=(j == 3))
                    last.then_inc(group_sum.sem, group_sum.plus())

                turn_x(0, 0, 3)
                pe.wait_ge(decay_in.sem, decay_in.next())
                turn_x(0, 1, 7)
                pe.wait_ge(cb_read.sem, cb_read.next())
                head_rows(0)
                head_rows(1)
                pe.wait_ge(bank_free.sem, bank_free.next(2))
                new_state(0)
                up_unit()
                gates = woven(Z_WOVEN)
                for p in range(SSD_PAIRS):
                    if p + 2 < SSD_PAIRS:
                        head_rows(p + 2)
                    heads_out(p)
                    if p // 4 + 1 < SSD_GROUPS:
                        if p % 4 == 0:
                            turn_x(p // 4 + 1, 0)
                        elif p % 4 == 2:
                            pe.wait_ge(bank_free.sem, bank_free.next())
                            turn_x(p // 4 + 1, 1)
                        elif p % 4 == 3:
                            new_state(p // 4 + 1)
                    gates(p)
                    if p == SSD_PAIRS - 3:
                        pe.wait_ge(evacuated.sem, evacuated.value())
                    if p >= SSD_PAIRS - 3:
                        g = p - (SSD_PAIRS - 3)
                        square_sum(g, 4 + g // 2, g % 2)
                square_sum(3, 6, 0)

            def softmax_attention(kind, between=lambda n: None):
                n_heads, q0, _, _ = attention(kind)

                def scores(n):
                    h, a, b = n // 2, n % 2, n % 3
                    nk = keys_of(kind, a)
                    q = proj[:, q0 + h, a * P:(a + 1) * P]
                    if kind == "diff":
                        mm(ps[:, b, 0:nk], q[0:64, :], proj[0:64, 8 + h, 0:nk],
                           start=True, stop=True).then_inc(first_scored.sem, first_scored.plus())
                        return
                    elif kind == "fox":
                        if a == 0:
                            f0 = log_f[:, 0, h:h + 1].to_broadcast([P, P])
                            mm(ps[:, 4 + h % 2, 0:P], f0, upper[:], start=True, stop=True)
                            mm(ps[:, 4 + h % 2, P:T], f0, ones[:], start=True, stop=False)
                            mm(ps[:, 4 + h % 2, P:T], log_f[:, 1, h:h + 1].to_broadcast([P, P]), upper[:],
                               start=False, stop=True)
                        last = mm(ps[:, b, 0:nk], q, proj[:, h, 0:nk], start=True, stop=True)
                    else:
                        last = mm(ps[:, b, 0:nk], q, mem_k[:, int(kind[3]), h, :], start=True, stop=True)
                    last.then_inc(scored.sem, scored.plus())

                def scores_second(n):
                    if kind == "diff":
                        h, a, b = n // 2, n % 2, n % 3
                        nk = keys_of(kind, a)
                        pe.wait_ge(first_scored.sem, first_scored.value())
                        mm(ps[:, b, T:T + nk], proj[64:P, q0 + h, a * P:(a + 1) * P], proj[64:P, 8 + h, 0:nk],
                           start=True, stop=True).then_inc(scored.sem, scored.plus())

                def turn(n):
                    nk = keys_of(kind, n % 2)
                    pe.wait_ge(probs_ready.sem, probs_ready.next())
                    for kb in range(nk // P):
                        last = nc.tensor.transpose(ps[:, 3, kb * P:(kb + 1) * P],
                                                   probs[n % 2][:, kb * P:(kb + 1) * P], ident[:])
                    last.then_inc(probs_turned.sem, probs_turned.plus())

                def values(n):
                    h, a = n // 2, n % 2
                    nk = keys_of(kind, a)
                    if a == 0:
                        if out_read.due():
                            pe.wait_ge(out_read.sem, out_read.value())
                    pe.wait_ge(probs_copied.sem, probs_copied.next())
                    for kb in range(nk // P):
                        v = (mem_v[:, int(kind[3]), kb, h * P:(h + 1) * P] if kind.startswith("mem")
                             else v_tok[:, kb, h * P:(h + 1) * P])
                        last = mm(ps[:, 7, a * P:(a + 1) * P], v, probs_t[n % 2][:, kb * P:(kb + 1) * P],
                                  start=(kb == 0), stop=(kb == nk // P - 1))
                    if a == 1:
                        last.then_inc(out_done.sem, out_done.plus())

                n_units = 2 * n_heads
                for n in range(2):
                    scores(n)
                    scores_second(n)
                for n in range(n_units):
                    if n + 2 < n_units:
                        scores(n + 2)
                    if n >= 1:
                        values(n - 1)
                    if n + 2 < n_units:
                        scores_second(n + 2)
                    turn(n)
                    between(n)
                values(n_units - 1)

            def turn_values(v0):
                for a in range(TH):
                    for b in range(2):
                        turn_tiles(2 * a + b, [proj[:, v0 + 4 * b + h, a * P:(a + 1) * P] for h in range(4)])
                pe.wait_ge(values_copied.sem, values_copied.next(4))

            pe.wait_ge(pool_made.sem, pool_made.next(POOL_MADE))
            pe.wait_ge(x_staged.sem, x_staged.next())
            turn_input(flat(proj[:, 0:8, :]).rearrange("p (a n) -> p a n", a=TH))
            vrows = flat(proj[:, 24:27, :])
            pe.wait_ge(first_staged.sem, first_staged.next(LOADED_FIRST))
            turn_tiles(4, [vrows[:, 0:P]])
            pe.wait_ge(setup_read.sem, setup_read.next())

            up_unit(first=True)
            pe.wait_ge(staged.sem, staged.next(LOADED_LATER))
            turn_tiles(0, [vrows[:, b * P:(b + 1) * P] for b in range(1, VBLOCKS)])
            mm(ps[:, 1, 0:1], freq_row, ones[0:1, 0:1], start=True,
               stop=True).then_inc(freq_done.sem, freq_done.plus())
            second_up()
            more_ups(10)
            small_product(SSD_HEADS)
            pe.wait_ge(setup_read.sem, setup_read.next(2))
            up_unit()
            turn_small(SSD_HEADS)
            up_unit()
            pe.wait_ge(dA_ready.sem, dA_ready.next())
            mm(ps[:, STAT, 0:64], upper[:], dA, start=True, stop=True)
            mm(ps[:, STAT, 64:96], ones[:], dA[:, 0:32], start=True,
               stop=True).then_inc(cumsum_done.sem, cumsum_done.plus())
            up_unit()
            ssd_core()
            downs(8)
            ffn()

            up_unit(first=True)
            second_up()
            pe.wait_ge(mem_staged.sem, mem_staged.next())
            turn_input(mem_flat.rearrange("p (a n) -> p a n", a=TH))
            more_ups(10)
            pe.wait_ge(evacuated.sem, evacuated.value())

            def qk_sum(i):
                pe.wait_ge(qk_squares.sem, qk_squares.next())
                for j in range(4):
                    last = mm(ps[:, j, :], half_ones[:], flat(qk_sq[i][:, 2 * j:2 * j + 2, :]), start=True, stop=True)
                last.then_inc(qk_summed.sem, qk_summed.plus())

            up_unit(first=True)
            second_up(mem_partial)
            qk_sum(0)
            up_unit()
            pe.wait_ge(qk_logs.sem, qk_logs.next())
            qk_sum(1)
            up_unit()
            up_unit()
            pe.wait_ge(qk_logs.sem, qk_logs.next())
            kv_units = woven(KV_WOVEN)
            for j in range(8):
                pe.wait_ge(qk_normed.sem, qk_normed.next())
                if qk_rotated.due():
                    pe.wait_ge(qk_rotated.sem, qk_rotated.value())
                mm(ps[:, j % 4, :], swap[:], flat(proj[:, 2 * j:2 * j + 2, :]),
                   start=True, stop=True).then_inc(qk_swapped.sem, qk_swapped.plus())
                kv_units(j)
            if qk_rotated.due(4):
                pe.wait_ge(qk_rotated.sem, qk_rotated.value())
            turn_values(16)
            def turn_memory(b, l, a):
                turn_tiles(b, [proj[:, 32 + 4 * l + h, a * P:(a + 1) * P] for h in range(MEM_HEADS)])

            def o_sum(i):
                pe.wait_ge(o_squares.sem, o_squares.next())
                for j in range(2):
                    last = mm(ps[:, 5 + j, :], ones[:], flat(o_sq[i][:, 2 * j:2 * j + 2, :]), start=True, stop=True)
                last.then_inc(o_summed.sem, o_summed.plus())

            def diff_step(t):
                if t == 3:
                    pe.wait_ge(evacuated.sem, evacuated.value())
                    turn_memory(4, 0, 0)
                    turn_memory(5, 0, 1)
                    turn_memory(6, 1, 0)
                elif t == 5:
                    pe.wait_ge(bank_free.sem, bank_free.next(3))
                    turn_memory(4, 1, 1)
                elif t == 11:
                    o_sum(0)

            softmax_attention("diff", diff_step)
            o_sum(1)
            pe.wait_ge(bank_free.sem, bank_free.next())
            downs(4)
            ffn()
            ffn()

            ups(3)
            pe.wait_ge(evacuated.sem, evacuated.value(-1))
            softmax_attention("mem0", woven(A_WOVEN))
            more_ups(7 - A_WOVEN)
            down_unit(first=True)
            down_unit()
            more_ups(4)
            for j in range(4):
                down_unit(last=(j == 3))
            ffn()

            ups(8)
            small_product(FOX_HEADS)
            ffn(stats=False)
            pe.wait_ge(log_f_ready.sem, log_f_ready.next())
            mm(ps[:, STAT, 0:8], upper[:], log_f[:, 0, :], start=True, stop=True)
            mm(ps[:, STAT, 8:16], ones[:], log_f[:, 0, :], start=True, stop=False)
            mm(ps[:, STAT, 8:16], upper[:], log_f[:, 1, :], start=False,
               stop=True).then_inc(cum_f_done.sem, cum_f_done.plus())
            pe.wait_ge(cum_f_read.sem, cum_f_read.next())

            ups(3)
            pe.wait_ge(evacuated.sem, evacuated.value(-1))
            softmax_attention("mem1", woven(B_WOVEN))
            pe.wait_ge(evacuated.sem, evacuated.value())
            pe.wait_ge(out_read.sem, out_read.value(1))
            turn_values(8)
            softmax_attention("fox")
            downs(6)
            ffn()

            for b in range(2):
                pe.wait_ge(final_x.sem, final_x.next())
                for a in range(TH):
                    turn_tiles(2 * b + a, [gained[:, 4 * b + j, a * P:(a + 1) * P] for j in range(4)])
            pe.wait_ge(sums_ready.sem, sums_ready.next())
            for a in range(TH):
                last = mm(ps[:, STAT, a:a + 1], partial[:, a * P:(a + 1) * P], ones[:, 0:1], start=True, stop=True)
            last.then_inc(stat_done.sem, stat_done.plus())

        @block.scalar
        def _(act):
            f = nc.scalar.activation
            c = Counts(act, sem)
            act_hi_made = c("act_hi_made")
            biased = c("biased")
            conv_base = c("conv_base")
            conv_done = c("conv_done")
            decay_done = c("decay_done")
            decay_in = c("decay_in")
            decay_rate = c("decay_rate")
            decay_ready = c("decay_ready")
            evacuated = c("evacuated")
            exps_done = c("exps_done")
            second_ready = c("second_ready")
            gate_act = c("gate_act")
            gate_ready = c("gate_ready")
            gated = c("gated")
            gated_input = c("gated_input")
            group_rstd = c("group_rstd")
            group_sum = c("group_sum")
            h_hi_made = c("h_hi_made")
            half_sin = c("half_sin")
            hi_split = c("hi_split")
            hidden_ready = c("hidden_ready")
            in_ready = c("in_ready")
            small_done = c("small_done")
            lam_exp = c("lam_exp")
            lam_in = c("lam_in")
            o_rstd = c("o_rstd")
            o_squares = c("o_squares")
            o_summed = c("o_summed")
            out_done = c("out_done")
            out_read = c("out_read")
            probs_copied = c("probs_copied")
            probs_turned = c("probs_turned")
            qk_logs = c("qk_logs")
            qk_rstd = c("qk_rstd")
            qk_squares = c("qk_squares")
            qk_summed = c("qk_summed")
            row_exp = c("row_exp")
            rstd_ready = c("rstd_ready")
            scored = c("scored")
            seg_ready = c("seg_ready")
            setup_read = c("setup_read")
            z_ready = c("z_ready")
            shifted = c("shifted")
            small_free = c("small_free")
            small_hi_made = c("small_hi_made")
            small_landed = c("small_landed", step=16)
            source_ready = c("source_ready")
            sp_exp = c("sp_exp")
            sp_in = c("sp_in")
            sp_ln = c("sp_ln")
            sp_one = c("sp_one")
            squares_made = c("squares_made")
            stat_done = c("stat_done")
            state_done = c("state_done")
            state_ready = c("state_ready")
            step = c("act_step")
            su_done = c("su_done")
            trig_in = c("trig_in")
            turned = c("turned")
            values_copied = c("values_copied")
            x_ready = c("x_ready")
            y_squares = c("y_squares")
            landed = [c(f"landed{s}", step=16) for s in range(RING)]
            slot, unit = [0], [0]

            def split(s):
                act.wait_ge(landed[s].sem, landed[s].next())
                f(w_hi[:, s, :], raw[:, s, :], ACT.Copy).then_inc(hi_split.sem, hi_split.plus())

            def split_next(trips=1):
                if unit[0] + RING < UNITS:
                    split(slot[0])
                unit[0] += trips
                slot[0] = (slot[0] + 1) % RING

            def per_trip(**extra):
                return {hi_split: RING, su_done: RING, **{t: 1 for t in landed},
                        **{c(k): v for k, v in extra.items()}}

            def one_unit(work=lambda j, s: None, j=0, late=lambda j, s: None):
                act.wait_ge(su_done.sem, su_done.next())
                s = slot[0]
                work(j, s)
                split_next()
                late(j, s)

            def units(n, work=lambda j, s: None, j0=0, late=lambda j, s: None, **extra):
                trips = n // RING if n >= 2 * RING else 0
                if trips:
                    with c.repeat(trips, per_trip(**{k: RING * v for k, v in extra.items()})) as i:
                        for j in range(RING):
                            act.wait_ge(su_done.sem, su_done.next())
                            s = slot[0]
                            work(i * RING + (j0 + j), s)
                            split_next(trips)
                            late(i * RING + (j0 + j), s)
                for j in range(j0 + trips * RING, j0 + n):
                    one_unit(work, j, late)

            def woven(n, read=None, ahead=False):
                def step(t):
                    first = 0 if ahead else 2
                    if t % 2 == 0 and first <= t < 2 * n + 2:
                        act.wait_ge(su_done.sem, su_done.next())
                        split_next()
                    if t % 2 and first < t < 2 * n + 3:
                        act.wait_ge(evacuated.sem, evacuated.next())
                        if read:
                            read((t - 3) // 2)
                return step

            def columns():
                act.wait_ge(setup_read.sem, 3)

            def skip(j, s):
                act.wait_ge(evacuated.sem, evacuated.next())

            def inverse_root(dst, src, scale):
                f(dst, src, ACT.Ln, bias=eps_col, scale=scale).then_inc(step.sem, step.plus())
                act.wait_ge(step.sem, step.value())
                return f(dst, dst, ACT.Exp, scale=-0.5)

            def norm(gain, g0, again=False, h=True, stats=True, renew=True, src=x, sq=squares, ahead=False):
                for b in range(4):
                    if not again:
                        act.wait_ge(x_ready.sem, x_ready.next())
                    for k in (2 * b, 2 * b + 1):
                        if h:
                            f(h_hi[:, k, :], src[:, k, :], ACT.Copy,
                              scale=vcol(gain, g0 + k)).then_inc(h_hi_made.sem, h_hi_made.plus())
                if stats:
                    f(sq, src[:], ACT.Square).then_inc(squares_made.sem, squares_made.plus())
                if renew is True:
                    split_next()
                elif renew:
                    renew()
                if ahead:
                    act.wait_ge(su_done.sem, su_done.next())
                    split_next()
                if stats:
                    act.wait_ge(stat_done.sem, stat_done.next())
                    inverse_root(rstd[:], ps[:, STAT, 0:T], 1.0 / D).then_inc(rstd_ready.sem, rstd_ready.plus())

            def feed(src, j, s):
                f(act_hi[:, s, :, :], src[:, 2 * j:2 * j + 2, :],
                  ACT.Copy).then_inc(act_hi_made.sem, act_hi_made.plus())

            def downs(n, src, order=None, ready=lambda j: None, fed=0):
                s, order = slot[0], order or range(n)

                def give(j):
                    ready(j)
                    feed(src, order[j], (s + j) % RING)

                for j in range(fed, min(RING, n)):
                    give(j)
                for j in range(n - 1):
                    act.wait_ge(su_done.sem, su_done.next())
                    if j + RING < n:
                        give(j + RING)
                    split_next()

            def ffn(conv=None, ahead=True):
                def tap_and_bias(w, tile):
                    columns()
                    for a in range(2):
                        last = f(f_out[:, w, a, :], f_in[:, w, a, :], ACT.Identity,
                                 scale=vcol("ffn_conv_w", conv * 6 * FT + 4 * FT + a + tile),
                                 bias=vcol("ffn_conv_b", conv * 2 * FT + a + tile))
                    last.then_inc(conv_base.sem, conv_base.plus())

                def gate(j, renewed=False):
                    if not renewed:
                        act.wait_ge(su_done.sem, su_done.next())
                    act.wait_ge(evacuated.sem, evacuated.next())
                    if conv is None:
                        f(f_out[:, 0, :, :], f_in[:, 0, :, :], ACT.Silu).then_inc(gate_act.sem, gate_act.plus())
                    else:
                        tap_and_bias(0, j * 2)
                    if not renewed:
                        split_next()

                def up(j, renew=True):
                    act.wait_ge(su_done.sem, su_done.next())
                    act.wait_ge(evacuated.sem, evacuated.next())
                    if conv is not None:
                        tap_and_bias(1, j * 2 + FT)
                        act.wait_ge(gate_ready.sem, gate_ready.next())
                        f(f_out[:, 0, :, :], f_out[:, 0, :, :], ACT.Silu).then_inc(gate_act.sem, gate_act.plus())
                    if renew:
                        split_next()

                first = slot[0] - ahead
                down_slot, last_slot = (first + 4) % RING, (first + 2) % RING

                def give(s):
                    act.wait_ge(hidden_ready.sem, hidden_ready.next())
                    f(act_hi[:, s, :, :], hidden, ACT.Copy).then_inc(act_hi_made.sem, act_hi_made.plus())

                gate(0, renewed=ahead)
                up(0)
                give(down_slot)
                extra = dict(evacuated=2, gate_act=1, hidden_ready=1, act_hi_made=1)
                if conv is not None:
                    extra.update(conv_base=2, gate_ready=1)

                def trip(j, s, last=False):
                    gate(j + 1)
                    up(j + 1, renew=not last)
                    if last:
                        give(s)
                        split_next()
                    act.wait_ge(su_done.sem, su_done.next())
                    if not last:
                        give(s)
                    split_next()

                u0 = unit[0]
                with c.repeat(FU - 2, per_trip(**extra)) as i:
                    trip(i, down_slot)
                unit[0] = u0 + 3 * (FU - 2)
                trip(FU - 2, last_slot, last=True)

            def softmax_attention(kind, between=lambda n: None):
                n_heads, _, out0, scale = attention(kind)

                def query_bias(n):
                    h, a = n // 2, n % 2
                    nk = keys_of(kind, a)
                    act.wait_ge(scored.sem, scored.next())
                    if n >= 2:
                        act.wait_ge(exps_done.sem, exps_done.value())
                    f(s_buf[n % 2][:, 0, 0:nk], ps[:, n % 3, 0:nk], ACT.Identity,
                                       scale=scale, bias=cum_f[:, a, h:h + 1]).then_inc(biased.sem, biased.plus())

                def exps(n):
                    nk = keys_of(kind, n % 2)
                    t = tiny[n % 2]
                    act.wait_ge(shifted.sem, shifted.next())
                    if kind == "diff":
                        for j in range(2):
                            last = f(p_buf[n % 2][:, j, 0:nk], s_buf[n % 2][:, j, 0:nk], ACT.Exp,
                                     bias=t[:, 1, j:j + 1], accum_out=t[:, 2, j:j + 1])
                    elif kind == "fox":
                        last = f(p_buf[n % 2][:, 0, 0:nk], s_buf[n % 2][:, 0, 0:nk], ACT.Exp,
                                 bias=t[:, 1, 0:1], accum_out=t[:, 2, 0:1])
                    else:
                        last = f(p_buf[n % 2][:, 0, 0:nk], ps[:, n % 3, 0:nk], ACT.Exp, scale=scale,
                                 bias=t[:, 1, 0:1], accum_out=t[:, 2, 0:1])
                    last.then_inc(exps_done.sem, exps_done.plus())

                def copy_turned(n):
                    nk = keys_of(kind, n % 2)
                    act.wait_ge(probs_turned.sem, probs_turned.next())
                    f(probs_t[n % 2][:, 0:nk], ps[:, 3, 0:nk],
                      ACT.Copy).then_inc(probs_copied.sem, probs_copied.plus())

                def copy_out(h):
                    act.wait_ge(out_done.sem, out_done.next())
                    f(proj[:, out0 + h, :], ps[:, 7, 0:T], ACT.Copy).then_inc(out_read.sem, out_read.plus())

                n_units = 2 * n_heads
                if kind == "fox":
                    query_bias(0)
                else:
                    scored.n += n_units
                for n in range(n_units):
                    if kind == "fox" and n + 1 < n_units:
                        query_bias(n + 1)
                    exps(n)
                    if n % 2 == 1 and n >= 3:
                        copy_out((n - 3) // 2)
                    if n >= 1:
                        copy_turned(n - 1)
                    between(n)
                copy_turned(n_units - 1)
                copy_out(n_heads - 1)
                for n in range(n_units, n_units + 3):
                    between(n)
                act.wait_ge(out_read.sem, out_read.value())

            def copy_values(turned_before):
                turned.n = turned_before
                for i in range(4):
                    act.wait_ge(turned.sem, turned.next())
                    f(v_tok[:, i // 2, 512 * (i % 2):512 * (i % 2) + 512], ps[:, i, :],
                      ACT.Copy).then_inc(values_copied.sem, values_copied.plus())

            def softplus():
                act.wait_ge(sp_in.sem, sp_in.next())
                f(sp[1], sp[0], ACT.Abs).then_inc(step.sem, step.plus())
                act.wait_ge(step.sem, step.value())
                f(sp[2], sp[1], ACT.Exp, scale=-1.0).then_inc(sp_exp.sem, sp_exp.plus())
                act.wait_ge(sp_one.sem, sp_one.next())
                f(sp[4], sp[3], ACT.Ln).then_inc(sp_ln.sem, sp_ln.plus())

            def small_weights():
                act.wait_ge(small_landed.sem, small_landed.next())
                f(small_hi[:], small_raw[:], ACT.Copy).then_inc(small_hi_made.sem, small_hi_made.plus())

            split(0)

            def activate_z(j):
                z = proj[:, 2 * j:2 * j + 2, :]
                f(z, z, ACT.Silu).then_inc(z_ready.sem, z_ready.plus())

            def silu_z(j, s):
                act.wait_ge(evacuated.sem, evacuated.next())
                activate_z(j)

            def conv_xbc(j, s):
                act.wait_ge(evacuated.sem, evacuated.next())
                columns()
                for a in range(2):
                    last = f(conv_out[s][:, a, :], conv_in[s][:, a, :], ACT.Identity,
                             scale=vcol("ssd_conv_w", j * 2 + (3 * SSD_XBC // P + a)),
                             bias=vcol("ssd_conv_b", j * 2 + a))
                last.then_inc(conv_base.sem, conv_base.plus())

            def silu_xbc(j, s):
                act.wait_ge(conv_done.sem, conv_done.next())
                f(proj[:, bass.ds(j * 2 + 16, 2), :], conv_out[s], ACT.Silu).then_inc(in_ready.sem, in_ready.plus())

            act.wait_ge(setup_read.sem, 1)

            def fill_ring():
                split(1)
                split(2)

            norm("norm_mix_g", 0, renew=fill_ring)
            small_weights()
            units(12, conv_xbc, 0, late=silu_xbc, evacuated=1, in_ready=1, conv_base=1, conv_done=1)
            one_unit(j=0, late=silu_z)
            softplus()
            f(heads[:, 1, :], heads[:, 1, :], ACT.Exp).then_inc(decay_rate.sem, decay_rate.plus())
            act.wait_ge(decay_in.sem, decay_in.next())
            f(dec, dec, ACT.Exp).then_inc(decay_done.sem, decay_done.plus())
            one_unit(j=1, late=silu_z)
            one_unit(j=2, late=silu_z)

            def state_copy(g):
                act.wait_ge(state_done.sem, state_done.next())
                f(state[g % 2], ps[:, 0, :], ACT.Copy).then_inc(state_ready.sem, state_ready.plus())

            def group_square(g):
                act.wait_ge(gated.sem, gated.next(4))
                f(group_squares[g], proj[:, 16 + 4 * g:20 + 4 * g, :],
                  ACT.Square).then_inc(y_squares.sem, y_squares.plus())

            def group_roots(banks):
                for g0, g1, b in banks:
                    act.wait_ge(group_sum.sem, group_sum.next(g1 - g0))
                    f(flat(group_rs[:, g0:g1, :]), ps[:, b, 0:(g1 - g0) * T], ACT.Ln, bias=eps_col,
                      scale=1.0 / (SSD_INNER // SSD_GROUPS)).then_inc(step.sem, step.plus())
                act.wait_ge(step.sem, step.value())
                r = group_rs[:, banks[0][0]:banks[-1][1], :]
                f(r, r, ACT.Exp, scale=-0.5).then_inc(group_rstd.sem, group_rstd.plus())

            state_copy(0)

            def activate_gates(j):
                for k in {1: (3, 4, 5), 3: (6, 7)}.get(j, ()):
                    activate_z(k)

            gates = woven(Z_WOVEN, activate_gates, ahead=True)
            for p in range(SSD_PAIRS):
                act.wait_ge(seg_ready.sem, seg_ready.next())
                f(seg[p % 3], seg[p % 3], ACT.Exp).then_inc(decay_ready.sem, decay_ready.plus())
                rows_t = ps[:, 1 + p % 3, :].rearrange("p (q a t) -> p q a t", q=2, a=TH)[:, :, 1, :]
                f(row_e[p % 3], rows_t, ACT.Exp).then_inc(row_exp.sem, row_exp.plus())
                if p % 4 == 3 and p // 4 + 1 < SSD_GROUPS:
                    state_copy(p // 4 + 1)
                gates(p)
                if p >= SSD_PAIRS - 3:
                    group_square(p - (SSD_PAIRS - 3))
                if p == SSD_PAIRS - 1:
                    group_roots([(0, 2, 4)])
            group_square(3)
            def group_normed(j):
                if j == 2:
                    group_roots([(2, 3, 5), (3, 4, 6)])
                if j % 2 == 0:
                    act.wait_ge(source_ready.sem, source_ready.next())

            downs(8, proj[:, 16:32, :], ready=group_normed)
            norm("norm_ffn_g", 0, ahead=True)
            ffn(conv=0)

            norm("norm_mix_g", DK)
            units(6, late=skip, evacuated=1)
            act.wait_ge(trig_in.sem, trig_in.next())
            f(sin[:], scr(5632, T), ACT.Sin).then_inc(step.sem, step.plus())
            f(cos[:], scr(5632, T), ACT.Sin, scale=0.5).then_inc(half_sin.sem, half_sin.plus())
            act.wait_ge(lam_in.sem, lam_in.next(2))
            f(cols[:, 4:6], cols[:, 6:8], ACT.Exp).then_inc(lam_exp.sem, lam_exp.plus())
            units(5, late=skip, evacuated=1)
            act.wait_ge(su_done.sem, su_done.next())
            norm("mem_norm_2", 0, again=True, src=mem_raw, sq=mem_squares)
            act.wait_ge(evacuated.sem, evacuated.next())
            for i in range(2):
                f(qk_sq[i], proj[:, 8 * i:8 * i + 8, :], ACT.Square).then_inc(qk_squares.sem, qk_squares.plus())
            one_unit(late=skip)
            one_unit(late=skip)
            for i in range(2):
                act.wait_ge(qk_summed.sem, qk_summed.next())
                f(flat(qk_rn[i]), ps[:, 0:4, :].rearrange("p b t -> p (b t)"), ACT.Ln, bias=eps_col,
                  scale=1.0 / ATT_HD).then_inc(qk_logs.sem, qk_logs.plus())
                one_unit(late=skip)
            act.wait_ge(qk_logs.sem, qk_logs.value())
            for i in range(2):
                f(qk_rn[i], qk_rn[i], ACT.Exp, scale=-0.5).then_inc(qk_rstd.sem, qk_rstd.plus())
            kv_units = woven(KV_WOVEN, ahead=True)
            for j in range(8):
                kv_units(j)
            def o_square(i):
                act.wait_ge(out_read.sem, out_read.value())
                f(o_sq[i], proj[:, 24 + 4 * i:28 + 4 * i, :], ACT.Square).then_inc(o_squares.sem, o_squares.plus())

            def o_root(i):
                act.wait_ge(o_summed.sem, o_summed.next())
                inverse_root(flat(o_rs[i]), ps[:, 5:7, :].rearrange("p b t -> p (b t)"),
                             1.0 / P).then_inc(o_rstd.sem, o_rstd.plus())

            copy_values(TURNED_BEFORE_DIFF)

            def diff_step(t):
                if t == 10:
                    o_square(0)
                elif t == 12:
                    o_root(0)

            def heads_normed(j):
                if j == 2:
                    o_root(1)
                if j % 2 == 0:
                    act.wait_ge(source_ready.sem, source_ready.next())

            softmax_attention("diff", diff_step)
            o_square(1)
            downs(4, proj[:, 24:32, :], ready=heads_normed)
            norm("norm_ffn_g", DK, ahead=True)
            ffn(conv=1)
            norm("ffn_norm_2", 0, ahead=True)
            ffn()

            norm("mix_norm_2", 0)
            units(2, late=skip, evacuated=1)
            softmax_attention("mem0", woven(A_WOVEN, ahead=True))
            for j in range(2):
                feed(proj[:, 36:40, :], j, (slot[0] + 7 - A_WOVEN + j) % RING)
            units(7 - A_WOVEN, late=skip, evacuated=1)
            act.wait_ge(gated_input.sem, gated_input.next())
            for k in range(DK):
                last = f(proj[:, 28 + k, :], proj[:, 8 + k, :], ACT.Copy, scale=vcol("a_conv_w_2", 2 * DK + k))
            last.then_inc(conv_base.sem, conv_base.plus())
            for j in range(2):
                act.wait_ge(su_done.sem, su_done.next())
                split_next()
            units(4, late=skip, evacuated=1)

            def convolved(j):
                act.wait_ge(source_ready.sem, source_ready.next())

            downs(4, proj[:, 28:36, :], ready=convolved)
            norm("ffn_norm_2", DK, ahead=True)
            ffn()

            act.wait_ge(small_free.sem, small_free.next())
            w_small_f = A["w_kvf_2"].rearrange("(k p) n -> p k n", p=P)[:, :, 2 * D:]
            act.dma_start(small_raw[:, :, 0:FOX_HEADS], w_small_f).then_inc(sem("small_landed"), 16)
            norm("kv_norm_2", 0)
            act.wait_ge(small_landed.sem, small_landed.next())
            f(small_hi[:, :, 0:FOX_HEADS], small_raw[:, :, 0:FOX_HEADS],
              ACT.Copy).then_inc(small_hi_made.sem, small_hi_made.plus())
            units(8, late=skip, evacuated=1)
            act.wait_ge(small_done.sem, small_done.next(2))
            norm("ffn_norm_2", 2 * DK, again=True, stats=False, renew=None)
            softplus()
            ffn(ahead=False)

            norm("mix_norm_2", DK)
            units(2, late=skip, evacuated=1)
            softmax_attention("mem1", woven(B_WOVEN, ahead=True))
            for j in range(2):
                feed(proj[:, 36:40, :], j, (slot[0] + j) % RING)
            copy_values(TURNED_BEFORE_DIFF + 4 + 4)
            softmax_attention("fox")
            downs(6, proj[:, 28:40, :], MIXED_ORDER, fed=2)
            norm("ffn_norm_2", 3 * DK, ahead=True)
            ffn()
            for b in range(4):
                act.wait_ge(x_ready.sem, x_ready.next())
                for k in (2 * b, 2 * b + 1):
                    f(squares[:, k, :], x[:, k, :], ACT.Square).then_inc(squares_made.sem, squares_made.plus())
            act.wait_ge(stat_done.sem, stat_done.next())
            inverse_root(cols[:, 8:10], ps[:, STAT, 0:TH], 1.0 / D).then_inc(rstd_ready.sem, rstd_ready.plus())
            act.wait_ge(rstd_ready.sem, rstd_ready.value())
            for b in range(2):
                f(out_tok[:, 1, 512 * b:512 * b + 512], ps[:, 2 * b + 1, :], ACT.Copy,
                  scale=cols[:, 9:10]).then_inc(second_ready.sem, second_ready.plus())

        @block.vector
        def _(dve):
            v = nc.vector
            tt, stt, ts = v.tensor_tensor, v.scalar_tensor_tensor, v.tensor_scalar
            c = Counts(dve, sem)
            bank_summed = c("bank_summed")
            cb_read = c("cb_read")
            z_ready = c("z_ready")
            act_hi_made = c("act_hi_made")
            bank_free = c("bank_free")
            biased = c("biased")
            cb_done = c("cb_done")
            conv_base = c("conv_base")
            conv_done = c("conv_done")
            cum_f_done = c("cum_f_done")
            cum_f_read = c("cum_f_read")
            cumsum_done = c("cumsum_done")
            dA_ready = c("dA_ready")
            decay_done = c("decay_done")
            decay_in = c("decay_in")
            decay_rate = c("decay_rate")
            decay_ready = c("decay_ready")
            evacuated = c("evacuated")
            exps_done = c("exps_done")
            extras = c("extras_staged", step=16)
            final_ready = c("final_ready")
            final_x = c("final_x")
            freq_done = c("freq_done")
            gate_act = c("gate_act")
            gate_ready = c("gate_ready")
            gated = c("gated")
            gated_input = c("gated_input")
            group_rstd = c("group_rstd")
            h_hi_made = c("h_hi_made")
            h_ready = c("h_ready")
            half_sin = c("half_sin")
            hi_split = c("hi_split")
            hid_ready = c("hid_ready")
            hidden_ready = c("hidden_ready")
            in_ready = c("in_ready")
            lam_exp = c("lam_exp")
            lam_in = c("lam_in")
            lo_split = c("lo_split")
            log_f_ready = c("log_f_ready")
            mask_ready = c("mask_ready")
            o_rstd = c("o_rstd")
            out_read = c("out_read")
            pool_made = c("pool_made")
            probs_old = c("probs_turned", -2)
            probs_ready = c("probs_ready")
            qk_normed = c("qk_normed")
            qk_rotated = c("qk_rotated")
            qk_rstd = c("qk_rstd")
            qk_swapped = c("qk_swapped")
            row_exp = c("row_exp")
            rows_done = c("rows_done")
            rstd_ready = c("rstd_ready")
            scored = c("scored")
            seg_ready = c("seg_ready")
            setup_read = c("setup_read")
            shifted = c("shifted")
            small_done = c("small_done")
            small_normed = c("small_normed")
            small_turned = c("small_turned")
            small_free = c("small_free")
            small_hi_made = c("small_hi_made")
            small_ready = c("small_ready")
            source_ready = c("source_ready")
            sp_exp = c("sp_exp")
            sp_in = c("sp_in")
            sp_ln = c("sp_ln")
            sp_one = c("sp_one")
            squares_made = c("squares_made")
            step = c("vec_step")
            su_done = c("su_done")
            sums_ready = c("sums_ready")
            trig_in = c("trig_in")
            turned = c("turned")
            x_dt_ready = c("x_dt_ready")
            x_ready = c("x_ready")
            y_done = c("y_done")
            y_old = c("y_done", -3)
            y_read = c("y_read")
            slot, unit = [0], [0]

            def f32(ap):
                return ap.bitcast(F32)

            def split(s):
                dve.wait_ge(hi_split.sem, hi_split.next())
                tt(w_lo[:, s, :], raw[:, s, :], f32(w_hi[:, s, :]),
                   ALU.subtract).then_inc(lo_split.sem, lo_split.plus())

            def split_next(trips=1):
                if unit[0] + RING < UNITS:
                    split(slot[0])
                unit[0] += trips
                slot[0] = (slot[0] + 1) % RING

            def per_trip(**extra):
                return {hi_split: RING, lo_split: RING, su_done: RING, **{c(k): n for k, n in extra.items()}}

            def one_unit(work, j):
                dve.wait_ge(su_done.sem, su_done.next())
                work(j, slot[0])
                split_next()

            def units(n, work, j0=0, **extra):
                trips = n // RING if n >= 2 * RING else 0
                if trips:
                    with c.repeat(trips, per_trip(**{k: RING * m for k, m in extra.items()})) as i:
                        for j in range(RING):
                            dve.wait_ge(su_done.sem, su_done.next())
                            work(i * RING + (j0 + j), slot[0])
                            split_next(trips)
                for j in range(j0 + trips * RING, j0 + n):
                    one_unit(work, j)

            def woven(n, work, j0=0, ahead=False):
                def step(t):
                    first = 0 if ahead else 2
                    if t % 2 == 0 and first <= t < 2 * n + 2:
                        dve.wait_ge(su_done.sem, su_done.next())
                        work(j0 + (t - 2) // 2, slot[0])
                    if t % 2 and first < t < 2 * n + 3:
                        split_next()
                return step

            def evacuate(dst, s):
                tt(dst, bank(4 + s), rows(rstd[:], 2), ALU.mult).then_inc(evacuated.sem, evacuated.plus())

            def to_proj(first):
                def work(j, s):
                    evacuate(proj[:, bass.ds(j * 2 + first, 2), :], s)
                return work

            def residual(scale=1.0):
                def take(b):
                    dve.wait_ge(bank_summed.sem, bank_summed.next())
                    t = x[:, 2 * b:2 * b + 2, :]
                    stt(t, bank(b), scale, t, ALU.mult, ALU.add).then_inc(x_ready.sem, x_ready.plus())
                return take

            def norm(gain, g0, take=None, stats=True, renew=True, src=x, sq=squares, total=partial,
                     ahead=False):
                for b in range(5):
                    if take and b < 4:
                        take(b)
                    for k in (2 * b - 2, 2 * b - 1):
                        if gain and k >= 0:
                            dve.wait_ge(h_hi_made.sem, h_hi_made.next())
                            stt(h_lo[:, k, :], src[:, k, :], vcol(gain, g0 + k), f32(h_hi[:, k, :]),
                                ALU.mult, ALU.subtract).then_inc(h_ready.sem, h_ready.plus())
                if take and renew is True:
                    split_next()
                if stats:
                    dve.wait_ge(squares_made.sem, squares_made.next())
                    v.tensor_reduce(total, sq.rearrange("p k t -> p t k"), AX_X,
                                    ALU.add).then_inc(sums_ready.sem, sums_ready.plus())
                if renew is True:
                    split_next()
                elif renew:
                    renew()
                if ahead:
                    dve.wait_ge(su_done.sem, su_done.next())
                    split_next()
                if stats:
                    dve.wait_ge(rstd_ready.sem, rstd_ready.next())

            def feed(src, j, s):
                dve.wait_ge(act_hi_made.sem, act_hi_made.next())
                tt(act_lo[:, s, :, :], src[:, 2 * j:2 * j + 2, :], f32(act_hi[:, s, :, :]),
                   ALU.subtract).then_inc(hid_ready.sem, hid_ready.plus())

            def downs(n, src, order=None, prepare=lambda j: None, behind=False, fed=0):
                s, order = (slot[0] + behind) % RING, order or range(n)

                def give(j):
                    prepare(j)
                    feed(src, order[j], (s + j) % RING)

                for j in range(fed, min(RING, n)):
                    give(j)
                    if behind and j == 0:
                        split_next()
                for j in range(n - 1):
                    dve.wait_ge(su_done.sem, su_done.next())
                    if j + RING < n:
                        give(j + RING)
                    if j < n - 2:
                        split_next()

            def ffn(conv=None, ahead=True):
                first = slot[0] - ahead
                down_slot, last_slot = (first + 4) % RING, (first + 2) % RING

                def taps(w, tile):
                    dve.wait_ge(conv_base.sem, conv_base.next())
                    for d in (1, 2):
                        for a in range(2):
                            o = f_out[:, w, a, d:T]
                            if d > 1:
                                dve.wait_ge(step.sem, step.value(a - 1))
                            ins = stt(o, f_in[:, w, a, 0:T - d],
                                      vcol("ffn_conv_w", conv * 6 * FT + (2 - d) * 2 * FT + a + tile), o,
                                      ALU.mult, ALU.add)
                            if d == 1:
                                ins.then_inc(step.sem, step.plus())
                    return ins

                def gate(j, renewed=False):
                    if not renewed:
                        dve.wait_ge(su_done.sem, su_done.next())
                    evacuate(f_in[:, 0, :, :], (slot[0] - renewed) % RING)
                    if conv is not None:
                        taps(0, j * 2).then_inc(gate_ready.sem, gate_ready.plus())
                    if not renewed:
                        split_next()

                def up(j, renew=True):
                    dve.wait_ge(su_done.sem, su_done.next())
                    evacuate(f_in[:, 1, :, :], slot[0])
                    if conv is None:
                        dve.wait_ge(evacuated.sem, evacuated.value())
                    else:
                        taps(1, j * 2 + FT).then_inc(step.sem, step.plus())
                        dve.wait_ge(step.sem, step.value())
                    dve.wait_ge(gate_act.sem, gate_act.next())
                    u = f_in if conv is None else f_out
                    tt(hidden, f_out[:, 0, :, :], u[:, 1, :, :],
                       ALU.mult).then_inc(hidden_ready.sem, hidden_ready.plus())
                    if renew:
                        split_next()

                def give(s):
                    dve.wait_ge(act_hi_made.sem, act_hi_made.next())
                    tt(act_lo[:, s, :, :], hidden, f32(act_hi[:, s, :, :]),
                       ALU.subtract).then_inc(hid_ready.sem, hid_ready.plus())

                gate(0, renewed=ahead)
                up(0)
                give(down_slot)
                extra = dict(evacuated=2, gate_act=1, hidden_ready=1, act_hi_made=1, hid_ready=1)
                if conv is not None:
                    extra.update(conv_base=2, gate_ready=1, vec_step=5)

                def trip(j, s, last=False):
                    gate(j + 1)
                    up(j + 1, renew=not last)
                    if last:
                        give(s)
                        split_next()
                    dve.wait_ge(su_done.sem, su_done.next())
                    if not last:
                        give(s)
                        split_next()

                u0 = unit[0]
                with c.repeat(FU - 2, per_trip(**extra)) as i:
                    trip(i, down_slot)
                unit[0] = u0 + 3 * (FU - 2)
                trip(FU - 2, last_slot, last=True)

            def copy_values(dst, b0):
                for i, d in enumerate(dst):
                    dve.wait_ge(turned.sem, turned.next())
                    v.tensor_copy(d, ps[:, b0 + i, :]).then_inc(bank_free.sem, bank_free.plus())

            def norm_small(n):
                dve.wait_ge(small_done.sem, small_done.next())
                tt(small_sum[0:n, :], ps[0:n, STAT, 0:T], rstd[0:n, :],
                   ALU.mult).then_inc(small_normed.sem, small_normed.plus())

            def softplus(negate, bias, n):
                dve.wait_ge(small_turned.sem, small_turned.next())
                o = ps[:, STAT, T:T + 64].rearrange("p (a n) -> p a n", a=TH)[:, :, 0:n]
                tt(sp[0][:, :, 0:n], o, rows(bias, TH), ALU.add).then_inc(step.sem, step.plus())
                dve.wait_ge(step.sem, step.value())
                ts(sp[0][:, :, 0:n], sp[0][:, :, 0:n], -1.0 if negate else 1.0, None,
                   ALU.mult).then_inc(sp_in.sem, sp_in.plus())
                dve.wait_ge(sp_exp.sem, sp_exp.next())
                ts(sp[3], sp[2], 1.0, None, ALU.add).then_inc(sp_one.sem, sp_one.plus())
                dve.wait_ge(sp_one.sem, sp_one.value())
                ts(sp[5], sp[3], -1.0, None, ALU.add).then_inc(step.sem, step.plus())
                dve.wait_ge(step.sem, step.value())
                ts(sp[6], sp[5], 0.0, None, ALU.is_equal).then_inc(step.sem, step.plus())
                dve.wait_ge(step.sem, step.value())
                tt(sp[5], sp[5], sp[6], ALU.add).then_inc(step.sem, step.plus())
                dve.wait_ge(step.sem, step.value())
                v.reciprocal(sp[5], sp[5]).then_inc(step.sem, step.plus())
                dve.wait_ge(step.sem, step.value())
                dve.wait_ge(sp_ln.sem, sp_ln.next())
                tt(sp[6], sp[4], sp[6], ALU.add).then_inc(step.sem, step.plus())
                dve.wait_ge(step.sem, step.value())
                tt(sp[6], sp[6], sp[5], ALU.mult).then_inc(step.sem, step.plus())
                dve.wait_ge(step.sem, step.value())
                tt(sp[6], sp[6], sp[2], ALU.mult).then_inc(step.sem, step.plus())
                dve.wait_ge(step.sem, step.value())
                dve.wait_ge(sp_in.sem, sp_in.value())
                ts(sp[7], sp[0], 0.0, None, ALU.max).then_inc(step.sem, step.plus())
                dve.wait_ge(step.sem, step.value())
                tt(sp[7], sp[7], sp[6], ALU.add).then_inc(step.sem, step.plus())
                dve.wait_ge(step.sem, step.value())

            def small_weights(n):
                dve.wait_ge(small_hi_made.sem, small_hi_made.next())
                tt(small_lo[:, :, 0:n], small_raw[:, :, 0:n], f32(small_hi[:, :, 0:n]),
                                         ALU.subtract).then_inc(small_ready.sem, small_ready.plus())

            def softmax_attention(kind, between=lambda n: None):
                n_heads, _, _, scale = attention(kind)

                def shift(n):
                    h, a, i = n // 2, n % 2, n % 2
                    nk = keys_of(kind, a)
                    t, s = tiny[i], s_buf[i]
                    if kind == "diff":
                        dve.wait_ge(scored.sem, scored.next())
                        mask = chunk_mask[:, T - nk:T]
                        stt(s[:, :, 0:nk], bank(n % 3)[:, :, 0:nk], scale, rows(mask, 2),
                                  ALU.mult, ALU.add).then_inc(step.sem, step.plus())
                        dve.wait_ge(step.sem, step.value())
                        v.tensor_reduce(t[:, 0, :], s[:, :, 0:nk], AX_X, ALU.max).then_inc(step.sem, step.plus())
                        dve.wait_ge(step.sem, step.value())
                        ts(t[:, 1, :], t[:, 0, :], -1.0, None, ALU.mult).then_inc(shifted.sem, shifted.plus())
                        return
                    if kind == "fox":
                        if a == 0:
                            dve.wait_ge(scored.sem, scored.next())
                            tt(key_row[0], causal_mask[:, P:T], ps[:, 4 + h % 2, 0:P],
                               ALU.subtract).then_inc(step.sem, step.plus())
                            tt(key_row[1], causal_mask[:], ps[:, 4 + h % 2, 0:T],
                               ALU.subtract).then_inc(step.sem, step.plus())
                            dve.wait_ge(step.sem, step.value())
                        else:
                            scored.n += 1
                        dve.wait_ge(biased.sem, biased.next())
                        tt(s[:, 0, 0:nk], s[:, 0, 0:nk], key_row[a], ALU.add).then_inc(step.sem, step.plus())
                        dve.wait_ge(step.sem, step.value())
                        v.tensor_reduce(t[:, 0, 0:1], s[:, 0, 0:nk], AX_X, ALU.max).then_inc(step.sem, step.plus())
                        dve.wait_ge(step.sem, step.value())
                        ts(t[:, 1, 0:1], t[:, 0, 0:1], -1.0, None, ALU.mult).then_inc(shifted.sem, shifted.plus())
                        return
                    dve.wait_ge(scored.sem, scored.next())
                    v.tensor_reduce(t[:, 0, 0:1], ps[:, n % 3, 0:nk], AX_X, ALU.max).then_inc(step.sem, step.plus())
                    dve.wait_ge(step.sem, step.value())
                    ts(t[:, 1, 0:1], t[:, 0, 0:1], -scale, None, ALU.mult).then_inc(shifted.sem, shifted.plus())

                def normalise(n):
                    i = n % 2
                    nk = keys_of(kind, i)
                    t, p, o = tiny[i], p_buf[i], probs[i][:, 0:nk]
                    m = 2 if kind == "diff" else 1
                    dve.wait_ge(exps_done.sem, exps_done.next())
                    v.reciprocal(t[:, 3, 0:m], t[:, 2, 0:m]).then_inc(step.sem, step.plus())
                    dve.wait_ge(step.sem, step.value())
                    if probs_old.due():
                        dve.wait_ge(probs_old.sem, probs_old.value())
                    if kind != "diff":
                        ts(o, p[:, 0, 0:nk], t[:, 3, 0:1], None,
                           ALU.mult).then_inc(probs_ready.sem, probs_ready.plus())
                        return
                    tt(t[:, 4, 0:1], t[:, 3, 1:2], lam_col, ALU.mult).then_inc(step.sem, step.plus())
                    ts(o, p[:, 0, 0:nk], t[:, 3, 0:1], None, ALU.mult).then_inc(step.sem, step.plus())
                    dve.wait_ge(step.sem, step.value())
                    stt(o, p[:, 1, 0:nk], t[:, 4, 0:1], o, ALU.mult,
                        ALU.add).then_inc(probs_ready.sem, probs_ready.plus())

                shift(0)
                for n in range(2 * n_heads):
                    if n + 1 < 2 * n_heads:
                        shift(n + 1)
                    normalise(n)
                    between(n)
                for n in range(2 * n_heads, 2 * n_heads + 3):
                    between(n)

            def take_input(b):
                v.tensor_copy(x[:, 2 * b:2 * b + 2, :], bank(b)).then_inc(x_ready.sem, x_ready.plus())

            split(0)
            dve.wait_ge(turned.sem, turned.next(5))
            v.tensor_copy(vec[:, 0:P], ps[:, 4, 0:P]).then_inc(setup_read.sem, setup_read.plus())
            dve.wait_ge(setup_read.sem, setup_read.value())

            def fill_ring():
                split(1)
                split(2)

            norm("norm_mix_g", 0, take_input, renew=fill_ring)
            dve.wait_ge(turned.sem, turned.next())
            v.tensor_copy(vec[:, P:VBLOCKS * P],
                          ps[:, 0, 0:(VBLOCKS - 1) * P]).then_inc(setup_read.sem, setup_read.plus())
            dve.wait_ge(freq_done.sem, freq_done.next())
            dve.wait_ge(pool_made.sem, pool_made.next(POOL_MADE))
            v.tensor_copy(freq_col, ps[:, 1, 0:1]).then_inc(setup_read.sem, setup_read.plus())
            dve.wait_ge(setup_read.sem, setup_read.value())
            def conv_xbc(j, s, renew):
                dve.wait_ge(su_done.sem, su_done.next())
                evacuate(conv_in[s], s)
                renew()
                dve.wait_ge(conv_base.sem, conv_base.next())
                for d in (1, 2, 3):
                    for a in range(2):
                        o = conv_out[s][:, a, d:T]
                        if d > 1:
                            dve.wait_ge(step.sem, step.value(-1))
                        ins = stt(o, conv_in[s][:, a, 0:T - d],
                                  vcol("ssd_conv_w", j * 2 + ((3 - d) * SSD_XBC // P + a)), o, ALU.mult, ALU.add)
                        if d < 3 or a == 0:
                            ins.then_inc(step.sem, step.plus())
                ins.then_inc(conv_done.sem, conv_done.plus())

            small_weights(SSD_HEADS)
            conv_xbc(0, slot[0], lambda: None)
            with c.repeat(3, per_trip(evacuated=3, conv_base=3, conv_done=3, vec_step=15)) as i:
                for j in range(RING):
                    conv_xbc(i * RING + (1 + j), (slot[0] + 1) % RING, lambda: split_next(3))
            for j in (10, 11):
                conv_xbc(j, (slot[0] + 1) % RING, split_next)
            split_next()
            norm_small(SSD_HEADS)
            one_unit(to_proj(0), 0)
            dve.wait_ge(extras.sem, extras.next(EARLY_EXTRAS))
            d_skip = heads[:, 2, :].rearrange("p (t q) -> p t q", q=2)
            for q in range(2):
                rng = slice(64 * q, 64 * q + 64)
                v.tensor_copy(heads[rng, 3, 0:16], d_skip[rng, :, q]).then_inc(step.sem, step.plus())

            softplus(False, heads[:, 0, :], SSD_HEADS)
            v.tensor_copy(dt_tok.rearrange("p (a n) -> p a n", a=TH),
                          sp[7]).then_inc(small_free.sem, small_free.plus())
            dve.wait_ge(small_free.sem, small_free.value())
            dve.wait_ge(decay_rate.sem, decay_rate.next())
            stt(dA.rearrange("p (a n) -> p a n", a=TH), sp[7], -1.0, rows(heads[:, 1, :], TH),
                                   ALU.mult, ALU.mult).then_inc(dA_ready.sem, dA_ready.plus())
            dve.wait_ge(cumsum_done.sem, cumsum_done.next())
            v.tensor_copy(a_cs, ps[:, STAT, 0:64]).then_inc(step.sem, step.plus())
            dve.wait_ge(step.sem, step.value())
            tt(dec, ps[:, STAT, 64:96], a_cs[:, 0:32], ALU.subtract).then_inc(decay_in.sem, decay_in.plus())
            dve.wait_ge(decay_done.sem, decay_done.next())
            tt(dt_dec, dt_tok[:, 0:32], dec, ALU.mult).then_inc(step.sem, step.plus())
            one_unit(to_proj(0), 1)
            one_unit(to_proj(0), 2)
            dve.wait_ge(turned.sem, turned.next())
            v.tensor_copy(flat(b_tok), ps[:, 0, :]).then_inc(bank_free.sem, bank_free.plus())
            dve.wait_ge(cb_done.sem, cb_done.next())
            for a in range(TH):
                ins = tt(cb[:, :, a, :], bank(1 + a, 4), rows(upper[:], 4), ALU.mult)
            ins.then_inc(cb_read.sem, cb_read.plus())
            dve.wait_ge(step.sem, step.value())
            dve.wait_ge(in_ready.sem, in_ready.next(12))

            def x_first(g, b=0):
                hs = slice(8 * g, 8 * g + 8)
                dve.wait_ge(turned.sem, turned.next())
                b0 = bank(b, 8)
                tt(x_dt[g % 2][0], b0, each(dt_tok[:, hs], 64), ALU.mult).then_inc(step.sem, step.plus())
                tt(x_dec[g % 2], b0, each(dt_dec[:, hs], 64), ALU.mult).then_inc(bank_free.sem, bank_free.plus())

            def x_second(g, b=0):
                dve.wait_ge(turned.sem, turned.next())
                tt(x_dt[g % 2][1], bank(b, 8),
                   each(dt_tok[:, 32 + 8 * g:40 + 8 * g], 64), ALU.mult).then_inc(x_dt_ready.sem, x_dt_ready.plus())

            def segments(p):
                dve.wait_ge(rows_done.sem, rows_done.next())
                if y_old.due():
                    dve.wait_ge(y_old.sem, y_old.value())
                for q in range(2):
                    for a in range(TH):
                        col, at = 32 * a + 2 * p + q, (2 * q + a) * P
                        ins = ts(seg[p % 3][:, q, a * P:(a + 1) * P], ps[:, 1 + p % 3, at:at + P],
                                 a_cs[:, col:col + 1], 0.0, ALU.subtract, ALU.min)
                ins.then_inc(seg_ready.sem, seg_ready.plus())

            def mask(p):
                g = p // 4
                dve.wait_ge(decay_ready.sem, decay_ready.next())
                m = seg[p % 3]
                tt(m, m, rows(flat(cb[:, g, :, :]), 2), ALU.mult).then_inc(step.sem, step.plus())
                dve.wait_ge(row_exp.sem, row_exp.next())
                tt(row_e[p % 3], row_e[p % 3], rows(proj[:, 36 + g, P:T], 2),
                   ALU.mult).then_inc(mask_ready.sem, mask_ready.plus())

            def take_y(p):
                dve.wait_ge(y_done.sem, y_done.next())
                t = proj[:, 16 + p, :]
                stt(t, t, heads[:, 3, p:p + 1], ps[:, 7, 0:T], ALU.mult, ALU.add).then_inc(y_read.sem, y_read.plus())

            def gate(p):
                if p % 2 == 0:
                    dve.wait_ge(z_ready.sem, z_ready.next())
                dve.wait_ge(y_read.sem, y_read.value())
                t = proj[:, 16 + p, :]
                tt(t, t, proj[:, p, :], ALU.mult).then_inc(gated.sem, gated.plus())

            x_first(0, 3)
            x_second(0, 7)
            segments(0)
            gates = woven(Z_WOVEN, to_proj(0), 4, ahead=True)
            for p in range(SSD_PAIRS):
                if p + 1 < SSD_PAIRS:
                    segments(p + 1)
                if p:
                    take_y(p - 1)
                mask(p)
                if p:
                    gate(p - 1)
                if p // 4 + 1 < SSD_GROUPS:
                    if p % 4 == 0:
                        x_first(p // 4 + 1)
                    elif p % 4 == 2:
                        x_second(p // 4 + 1)
                gates(p)
            take_y(SSD_PAIRS - 1)
            gate(SSD_PAIRS - 1)

            def norm_group(j):
                if j in (0, 4):
                    dve.wait_ge(group_rstd.sem, group_rstd.next())
                if j % 2 == 0:
                    for t in range(2 * j, 2 * j + 4):
                        ins = stt(proj[:, 16 + t, :], proj[:, 16 + t, :], vcol("ssd_norm_g", t),
                                  group_rs[:, j // 2, :], ALU.mult, ALU.mult)
                    ins.then_inc(source_ready.sem, source_ready.plus())

            downs(8, proj[:, 16:32, :], prepare=norm_group)
            norm("norm_ffn_g", 0, residual(), ahead=True)
            ffn(conv=0)

            norm("norm_mix_g", DK, residual())
            for b in range(4):
                dve.wait_ge(turned.sem, turned.next())
                v.tensor_copy(mem_raw[:, 2 * b:2 * b + 2, :], bank(b)).then_inc(step.sem, step.plus())
            units(6, to_proj(0), evacuated=1)
            dve.wait_ge(extras.sem, extras.next(EXTRAS - EARLY_EXTRAS))
            ang, turns = scr(5632, T), scr(5888, T)
            v.tensor_copy(ang, scr(6400, T).bitcast(I32)).then_inc(step.sem, step.plus())
            dve.wait_ge(step.sem, step.value())
            ts(ang, ang, freq_col, None, ALU.mult).then_inc(step.sem, step.plus())
            dve.wait_ge(step.sem, step.value())
            ts(turns, ang, 1.0 / (2 * math.pi), ROUND, ALU.mult, ALU.add).then_inc(step.sem, step.plus())
            dve.wait_ge(step.sem, step.value())
            ts(turns, turns, -ROUND, None, ALU.add).then_inc(step.sem, step.plus())
            dve.wait_ge(step.sem, step.value())
            stt(ang, turns, -TWO_PI_HI, ang, ALU.mult, ALU.add).then_inc(step.sem, step.plus())
            dve.wait_ge(step.sem, step.value())
            stt(ang, turns, -TWO_PI_LO, ang, ALU.mult, ALU.add).then_inc(step.sem, step.plus())
            dve.wait_ge(step.sem, step.value())
            ts(ang, ang, 3.1415925, -3.1415925, ALU.min, ALU.max).then_inc(trig_in.sem, trig_in.plus())
            lam = scr(6656, 4, 64)
            for i in range(2):
                tt(lam[:, 2 * i, :], lam[:, 2 * i, :], lam[:, 2 * i + 1, :], ALU.mult).then_inc(step.sem, step.plus())
                dve.wait_ge(step.sem, step.value())
                v.tensor_reduce(cols[:, 6 + i:7 + i], lam[:, 2 * i, :], AX_X,
                                ALU.add).then_inc(lam_in.sem, lam_in.plus())
            dve.wait_ge(half_sin.sem, half_sin.next())
            tt(cos[:], cos[:], cos[:], ALU.mult).then_inc(step.sem, step.plus())
            dve.wait_ge(step.sem, step.value())
            ts(cos[:], cos[:], -2.0, 1.0, ALU.mult, ALU.add).then_inc(step.sem, step.plus())
            dve.wait_ge(lam_exp.sem, lam_exp.next())
            tt(lam_col, cols[:, 5:6], cols[:, 4:5], ALU.subtract).then_inc(step.sem, step.plus())
            dve.wait_ge(step.sem, step.value())
            ts(lam_col, lam_col, -LAMBDA_INIT, None, ALU.add).then_inc(step.sem, step.plus())
            ts(subln_col, vcol("attn_subln_g", 0), 1.0 - LAMBDA_INIT, None, ALU.mult).then_inc(step.sem, step.plus())
            units(5, to_proj(0), 6, evacuated=1)
            dve.wait_ge(su_done.sem, su_done.next())
            to_proj(0)(11, slot[0])
            norm("mem_norm_2", 0, src=mem_raw, sq=mem_squares, total=mem_partial)
            dve.wait_ge(evacuated.sem, evacuated.value())

            def to_memory(j, s):
                l, i = j // 4, j % 4
                evacuate(mem_k[:, l, 2 * i:2 * i + 2, :] if i < 2
                         else proj[:, 32 + 4 * l + 2 * i - 4:32 + 4 * l + 2 * i - 2, :], s)

            for j in range(4):
                one_unit(to_memory, j)
            kv_units = woven(KV_WOVEN, to_memory, 5, ahead=True)

            def norm_pair(j):
                if j % 4 == 0:
                    dve.wait_ge(qk_rstd.sem, qk_rstd.next())
                t = proj[:, 2 * j:2 * j + 2, :]
                stt(t, t, vcol("attn_q_norm_g" if j < 4 else "attn_k_norm_g", 0),
                    qk_rn[j // 4][:, 2 * (j % 4):2 * (j % 4) + 2, :],
                    ALU.mult, ALU.mult).then_inc(qk_normed.sem, qk_normed.plus())

            norm_pair(0)
            for j in range(8):
                t = proj[:, 2 * j:2 * j + 2, :]
                if j < 7:
                    norm_pair(j + 1)
                dve.wait_ge(qk_normed.sem, j + 1)
                if j:
                    dve.wait_ge(qk_rotated.sem, qk_rotated.value())
                tt(qk_a, t, rows(cos[:], 2), ALU.mult).then_inc(step.sem, step.plus())
                dve.wait_ge(qk_swapped.sem, qk_swapped.next())
                tt(qk_b, bank(j % 4), rows(sin[:], 2), ALU.mult).then_inc(step.sem, step.plus())
                dve.wait_ge(step.sem, step.value())
                tt(t, qk_a, qk_b, ALU.add).then_inc(qk_rotated.sem, qk_rotated.plus())
                kv_units(j)
            turned.n += 4
            def norm_heads(i):
                dve.wait_ge(o_rstd.sem, o_rstd.next())
                o = proj[:, 24 + 4 * i:28 + 4 * i, :]
                stt(o, o, subln_col, o_rs[i], ALU.mult, ALU.mult).then_inc(source_ready.sem, source_ready.plus())

            def diff_step(t):
                if t == 4:
                    copy_values([mem_v[:, l, a, :] for l, a in ((0, 0), (0, 1), (1, 0))], 4)
                elif t == 6:
                    copy_values([mem_v[:, 1, 1, :]], 4)
                elif t == 13:
                    norm_heads(0)

            softmax_attention("diff", diff_step)
            downs(4, proj[:, 24:32, :], prepare=lambda j: norm_heads(1) if j == 2 else None)
            norm("norm_ffn_g", DK, residual(), ahead=True)
            ffn(conv=1)
            norm("ffn_norm_2", 0, residual(), ahead=True)
            ffn()

            norm("mix_norm_2", 0, residual(0.5))
            units(2, to_proj(24), evacuated=1)
            softmax_attention("mem0", woven(A_WOVEN, to_proj(8), 1, ahead=True))
            dve.wait_ge(out_read.sem, out_read.next(ATT_HEADS + MEM_HEADS))
            for j in range(2):
                feed(proj[:, 36:40, :], j, (slot[0] + 7 - A_WOVEN + j) % RING)
            units(7 - A_WOVEN, to_proj(8), 1 + A_WOVEN, evacuated=1)
            dve.wait_ge(evacuated.sem, evacuated.value())
            cu = proj[:, 8:16, :]
            tt(cu, cu, proj[:, 16:24, :], ALU.mult).then_inc(gated_input.sem, gated_input.plus())
            dve.wait_ge(su_done.sem, su_done.next())
            split_next()
            dve.wait_ge(conv_base.sem, conv_base.next())
            for d in (1, 2):
                for k in range(DK):
                    o = proj[:, 28 + k, d:T]
                    stt(o, proj[:, 8 + k, 0:T - d], vcol("a_conv_w_2", (2 - d) * DK + k), o,
                        ALU.mult, ALU.add).then_inc(step.sem, step.plus())
                if d == 1:
                    dve.wait_ge(su_done.sem, su_done.next())
                    split_next()
                dve.wait_ge(step.sem, step.value())
            units(3, to_proj(0), evacuated=1)
            dve.wait_ge(su_done.sem, su_done.next())
            to_proj(0)(3, slot[0])
            dve.wait_ge(evacuated.sem, evacuated.value())

            def gate_convolved(j):
                o = proj[:, 28 + 2 * j:30 + 2 * j, :]
                tt(o, o, proj[:, 2 * j:2 * j + 2, :], ALU.mult).then_inc(source_ready.sem, source_ready.plus())

            downs(4, proj[:, 28:36, :], prepare=gate_convolved, behind=True)
            norm("ffn_norm_2", DK, residual(), ahead=True)
            ffn()

            norm("kv_norm_2", 0, residual(0.5))
            small_weights(FOX_HEADS)
            units(8, to_proj(0), evacuated=1)
            norm_small(FOX_HEADS)
            norm("ffn_norm_2", 2 * DK, stats=False, renew=None)
            softplus(True, gate_bias, FOX_HEADS)
            ts(log_f, sp[7][:, :, 0:FOX_HEADS], -1.0, None, ALU.mult).then_inc(log_f_ready.sem, log_f_ready.plus())
            ffn(ahead=False)
            dve.wait_ge(cum_f_done.sem, cum_f_done.next())
            v.tensor_copy(cum_f,
                          ps[:, STAT, 0:16].rearrange("p (a h) -> p a h",
                                                      a=TH)).then_inc(cum_f_read.sem, cum_f_read.plus())

            norm("mix_norm_2", DK, residual(0.5))
            units(2, to_proj(24), evacuated=1)
            softmax_attention("mem1", woven(B_WOVEN, to_proj(16), 1, ahead=True))
            turned.n += 4
            dve.wait_ge(out_read.sem, out_read.next(MEM_HEADS))
            for j in range(2):
                feed(proj[:, 36:40, :], j, (slot[0] + j) % RING)
            softmax_attention("fox")
            dve.wait_ge(out_read.sem, out_read.next(FOX_HEADS))
            downs(6, proj[:, 28:40, :], MIXED_ORDER, fed=2)
            norm("ffn_norm_2", 3 * DK, residual(), ahead=True)
            ffn()

            take = residual(0.5)
            for b in range(4):
                take(b)
                dve.wait_ge(x_ready.sem, x_ready.value())
                for k in (2 * b, 2 * b + 1):
                    ins = ts(gained[:, k, :], x[:, k, :], vcol("final_norm_2", k), None, ALU.mult)
                if b % 2:
                    ins.then_inc(final_x.sem, final_x.plus())
            dve.wait_ge(squares_made.sem, squares_made.next(DK))
            v.tensor_reduce(partial, squares.rearrange("p k t -> p t k"), AX_X,
                            ALU.add).then_inc(sums_ready.sem, sums_ready.plus())
            dve.wait_ge(turned.sem, turned.next(4))
            dve.wait_ge(rstd_ready.sem, rstd_ready.next())
            for b in range(2):
                ts(out_tok[:, 0, 512 * b:512 * b + 512], ps[:, 2 * b, :], cols[:, 8:9], None,
                   ALU.mult).then_inc(final_ready.sem, final_ready.plus())


def kernel(**inputs):
    import concourse.bacc as _bacc
    from concourse import mybir as _mybir
    from concourse.bass_utils import run_bass_kernel_spmd as _run

    nc = _bacc.Bacc("TRN2", target_bir_lowering=False, num_devices=1)
    arrays, args = {}, {}
    for name, value in inputs.items():
        a = np.ascontiguousarray(value)
        arrays[f"in_{name}_dram"] = a
        args[name] = nc.dram_tensor(f"in_{name}_dram", a.shape, _mybir.dt.from_np(a.dtype),
                                    kind="ExternalInput").ap()
    out = nc.dram_tensor("out_0_dram", (1, T, D), F32, kind="ExternalOutput").ap()
    build_program(nc, args, out)
    r = _run(nc, [arrays], core_ids=[0])
    return r.results[0]["out_0_dram"]
```
